# Optimizing a Trainium2 kernel written in Bass

```python
import math
import jax, jax.numpy as jnp
from jax import lax
import numpy as np

D_MODEL = 2048
BATCH = 1
SEQ = 256
DEPTH = 1

CHUNK = 64
LN_EPS = 1e-5
D_LRU = 1024
N_LRU_BLOCKS = 8
LRU_BLOCK = D_LRU // N_LRU_BLOCKS
CONV_W = 4
LRU_C = 8.0
N_HEADS = 8
HEAD_DIM = 128
D_ATT = N_HEADS * HEAD_DIM
N_IDX_HEADS = 16
IDX_DIM = 64
TOPK_MAX = 256
Q_BLOCK = 128
ROPE_THETA = 500000.0
ROT_ATT = HEAD_DIM // 4
ROT_IDX = IDX_DIM // 4
D_MIX = D_LRU + D_ATT
IN_SPLITS = (D_LRU, D_LRU, D_ATT, D_ATT, D_ATT, N_IDX_HEADS * IDX_DIM, IDX_DIM, N_IDX_HEADS)
D_IN = sum(IN_SPLITS)
PEER_HEADS = 8
N_KEYS = 128
N_EXPERTS = N_KEYS * N_KEYS
PEER_KEY_DIM = 256
PEER_TOPK = 16
TOK_BLOCK = 128
DEEPNORM_ALPHA = (2.0 * DEPTH) ** 0.25
DEEPNORM_BETA = (8.0 * DEPTH) ** -0.25

kernel_name = "hybrid_rglru_dsa_peer_deepnorm_adaln"

def layer_norm(x):
    xf = x.astype(jnp.float32)
    mu = jnp.mean(xf, -1, keepdims=True)
    var = jnp.mean(jnp.square(xf - mu), -1, keepdims=True)
    return ((xf - mu) * lax.rsqrt(var + LN_EPS)).astype(x.dtype)

def partial_rope(x, pos, rot_dim):
    half = rot_dim // 2
    inv_freq = ROPE_THETA ** (-jnp.arange(half, dtype=jnp.float32) / half)
    ang = pos.astype(jnp.float32)[:, :, None] * inv_freq
    cos = jnp.cos(ang)[:, :, None, :].astype(x.dtype)
    sin = jnp.sin(ang)[:, :, None, :].astype(x.dtype)
    x1, x2, xp = x[..., :half], x[..., half:rot_dim], x[..., rot_dim:]
    return jnp.concatenate([x1 * cos - x2 * sin, x2 * cos + x1 * sin, xp], -1)

def rglru_group(xb, gb, conv_w, conv_b, w_rg_a, b_rg_a, w_rg_x, b_rg_x, lam):
    B, S, _ = xb.shape
    xpad = jnp.pad(xb, ((0, 0), (CONV_W - 1, 0), (0, 0)))
    xc = sum(xpad[:, j:j + S] * conv_w[j] for j in range(CONV_W)) + conv_b
    xblk = xc.reshape(B, S, N_LRU_BLOCKS, LRU_BLOCK)
    r = jax.nn.sigmoid(jnp.einsum('bsnd,nde->bsne', xblk, w_rg_a).reshape(B, S, D_LRU) + b_rg_a)
    i = jax.nn.sigmoid(jnp.einsum('bsnd,nde->bsne', xblk, w_rg_x).reshape(B, S, D_LRU) + b_rg_x)
    log_a = -LRU_C * r.astype(jnp.float32) * jax.nn.softplus(-lam.astype(jnp.float32))
    a = jnp.exp(log_a)
    b = jnp.sqrt(-jnp.expm1(2.0 * log_a)) * (i * xc).astype(jnp.float32)

    def combine(e1, e2):
        a1, b1 = e1
        a2, b2 = e2
        return a1 * a2, a2 * b1 + b2

    _, h = lax.associative_scan(combine, (a, b), axis=1)
    return h.astype(xb.dtype) * jax.nn.gelu(gb)

def dsa_group(q, k, v, q_idx, k_idx, w_idx, k_idx_g, pos):
    B, S, _ = q.shape
    topk = min(TOPK_MAX, S // 4)
    q = partial_rope(q.reshape(B, S, N_HEADS, HEAD_DIM), pos, ROT_ATT)
    k = partial_rope(k.reshape(B, S, N_HEADS, HEAD_DIM), pos, ROT_ATT)
    v = v.reshape(B, S, N_HEADS, HEAD_DIM)
    q_idx = partial_rope(q_idx.reshape(B, S, N_IDX_HEADS, IDX_DIM), pos, ROT_IDX)
    k_idx = partial_rope((layer_norm(k_idx) * k_idx_g)[:, :, None, :], pos, ROT_IDX)[:, :, 0]
    w_idx = w_idx * (N_IDX_HEADS ** -0.5)
    key_chunk = jnp.arange(S) // CHUNK
    idx_scale = IDX_DIM ** -0.5
    att_scale = HEAD_DIM ** -0.5

    def block(bi):
        start = bi * Q_BLOCK
        qib = lax.dynamic_slice_in_dim(q_idx, start, Q_BLOCK, axis=1)
        wib = lax.dynamic_slice_in_dim(w_idx, start, Q_BLOCK, axis=1)
        logits = jnp.einsum('bthd,bsd->bths', qib, k_idx).astype(jnp.float32)
        score = jnp.einsum('bth,bths->bts', wib.astype(jnp.float32), jax.nn.relu(logits) * idx_scale)
        q_chunk = (start + jnp.arange(Q_BLOCK)) // CHUNK
        adm = key_chunk[None, :] <= q_chunk[:, None]
        score = jnp.where(adm[None], score, -jnp.inf)
        _, sel = lax.top_k(score, topk)
        valid = key_chunk[sel] <= q_chunk[None, :, None]
        k_sel = jax.vmap(lambda kk, ii: kk[ii])(k, sel)
        v_sel = jax.vmap(lambda vv, ii: vv[ii])(v, sel)
        qb = lax.dynamic_slice_in_dim(q, start, Q_BLOCK, axis=1)
        s = jnp.einsum('bthd,btkhd->bhtk', qb, k_sel).astype(jnp.float32) * att_scale
        s = jnp.where(valid[:, None], s, -jnp.inf)
        p = jax.nn.softmax(s, axis=-1).astype(v.dtype)
        return jnp.einsum('bhtk,btkhd->bthd', p, v_sel)

    out = lax.map(block, jnp.arange(S // Q_BLOCK))
    return out.transpose(1, 0, 2, 3, 4).reshape(B, S, D_ATT)

def peer(u, w_pq, sub_keys, u_tab, v_tab):
    B, S, D = u.shape
    q = (u @ w_pq).reshape(B, S, PEER_HEADS, 2, PEER_KEY_DIM // 2)
    s = jnp.einsum('bshpd,hpnd->bshpn', q, sub_keys).astype(jnp.float32)
    s1, i1 = lax.top_k(s[..., 0, :], PEER_TOPK)
    s2, i2 = lax.top_k(s[..., 1, :], PEER_TOPK)
    cand_s = (s1[..., :, None] + s2[..., None, :]).reshape(B, S, PEER_HEADS, PEER_TOPK * PEER_TOPK)
    cand_i = (i1[..., :, None] * N_KEYS + i2[..., None, :]).reshape(B, S, PEER_HEADS, PEER_TOPK * PEER_TOPK)
    top_s, pick = lax.top_k(cand_s, PEER_TOPK)
    eidx = jnp.take_along_axis(cand_i, pick, axis=-1)
    g = jax.nn.softmax(top_s, axis=-1)
    nb = (B * S) // TOK_BLOCK
    uf = u.reshape(nb, TOK_BLOCK, D)
    ef = eidx.reshape(nb, TOK_BLOCK, PEER_HEADS, PEER_TOPK)
    gf = g.reshape(nb, TOK_BLOCK, PEER_HEADS, PEER_TOPK)

    def apply(args):
        xb, eb, gb = args
        act = jax.nn.gelu(jnp.einsum('thkd,td->thk', u_tab[eb], xb).astype(jnp.float32))
        hk = (gb * act).astype(xb.dtype)
        return jnp.einsum('thk,thkd->td', hk, v_tab[eb])

    return lax.map(apply, (uf, ef, gf)).reshape(B, S, D)

def setup_inputs(seed: int = 0) -> dict:
    key = jax.random.key(seed)
    ks = jax.random.split(key, 24)
    f32 = jnp.float32
    L = DEPTH

    def nrm(k, shape, scale):
        return jax.random.normal(k, shape, f32) * scale

    x = nrm(ks[0], (BATCH, SEQ, D_MODEL), 1.0)
    c = nrm(ks[1], (BATCH, D_MODEL), 1.0)
    offs = jax.random.randint(ks[2], (BATCH, 1), 0, 1024, dtype=jnp.int32)
    positions = (offs + jnp.arange(SEQ, dtype=jnp.int32)[None, :]).astype(jnp.int32)
    w_ada = nrm(ks[3], (L, D_MODEL, 6 * D_MODEL), 0.2 * D_MODEL ** -0.5)
    b_ada = nrm(ks[4], (L, 6 * D_MODEL), 0.02)
    w_in = nrm(ks[5], (L, D_MODEL, D_IN), D_MODEL ** -0.5)
    conv_w = nrm(ks[6], (L, CONV_W, D_LRU), CONV_W ** -0.5)
    conv_b = nrm(ks[7], (L, D_LRU), 0.02)
    w_rg_a = nrm(ks[8], (L, N_LRU_BLOCKS, LRU_BLOCK, LRU_BLOCK), LRU_BLOCK ** -0.5)
    b_rg_a = nrm(ks[9], (L, D_LRU), 0.02)
    w_rg_x = nrm(ks[10], (L, N_LRU_BLOCKS, LRU_BLOCK, LRU_BLOCK), LRU_BLOCK ** -0.5)
    b_rg_x = nrm(ks[11], (L, D_LRU), 0.02)
    a_c = jax.random.uniform(ks[12], (L, D_LRU), f32, 0.9, 0.999)
    sg = a_c ** (1.0 / LRU_C)
    lru_lambda = jnp.log(sg) - jnp.log1p(-sg)
    k_idx_g = 1.0 + nrm(ks[13], (L, IDX_DIM), 0.02)
    w_out = nrm(ks[14], (L, D_MIX, D_MODEL), DEEPNORM_BETA * D_MIX ** -0.5)
    ln1_g = 1.0 + nrm(ks[15], (L, D_MODEL), 0.02)
    ln1_b = nrm(ks[16], (L, D_MODEL), 0.02)
    w_pq = nrm(ks[17], (L, D_MODEL, PEER_HEADS * PEER_KEY_DIM), D_MODEL ** -0.5)
    peer_sub_keys = nrm(ks[18], (L, PEER_HEADS, 2, N_KEYS, PEER_KEY_DIM // 2), (PEER_KEY_DIM // 2) ** -0.5)
    peer_u = nrm(ks[19], (L, N_EXPERTS, D_MODEL), D_MODEL ** -0.5)
    peer_v = nrm(ks[20], (L, N_EXPERTS, D_MODEL), DEEPNORM_BETA * PEER_HEADS ** -0.5)
    ln2_g = 1.0 + nrm(ks[21], (L, D_MODEL), 0.02)
    ln2_b = nrm(ks[22], (L, D_MODEL), 0.02)
    return {"x": x, "c": c, "positions": positions, "w_ada": w_ada, "b_ada": b_ada,
            "w_in": w_in, "conv_w": conv_w, "conv_b": conv_b, "w_rg_a": w_rg_a,
            "b_rg_a": b_rg_a, "w_rg_x": w_rg_x, "b_rg_x": b_rg_x, "lru_lambda": lru_lambda,
            "k_idx_g": k_idx_g, "w_out": w_out, "ln1_g": ln1_g, "ln1_b": ln1_b,
            "w_pq": w_pq, "peer_sub_keys": peer_sub_keys, "peer_u": peer_u, "peer_v": peer_v,
            "ln2_g": ln2_g, "ln2_b": ln2_b}

def reference(x, c, positions, w_ada, b_ada, w_in, conv_w, conv_b, w_rg_a, b_rg_a, w_rg_x,
              b_rg_x, lru_lambda, k_idx_g, w_out, ln1_g, ln1_b, w_pq, peer_sub_keys, peer_u,
              peer_v, ln2_g, ln2_b):
    split_at = np.cumsum(IN_SPLITS)[:-1].tolist()
    for l in range(DEPTH):
        mod = jax.nn.silu(c) @ w_ada[l] + b_ada[l]
        sh1, sc1, gt1, sh2, sc2, gt2 = [m[:, None, :] for m in jnp.split(mod, 6, axis=-1)]
        u1 = layer_norm(x) * (1.0 + sc1) + sh1
        xl, gl, q, k, v, qi, ki, wi = jnp.split(u1 @ w_in[l], split_at, axis=-1)
        y_lru = rglru_group(xl, gl, conv_w[l], conv_b[l], w_rg_a[l], b_rg_a[l], w_rg_x[l],
                            b_rg_x[l], lru_lambda[l])
        y_att = dsa_group(q, k, v, qi, ki, wi, k_idx_g[l], positions)
        mix = jnp.concatenate([y_lru, y_att], axis=-1) @ w_out[l]
        x = layer_norm(DEEPNORM_ALPHA * x + (1.0 + gt1) * mix) * ln1_g[l] + ln1_b[l]
        u2 = layer_norm(x) * (1.0 + sc2) + sh2
        y_ffn = peer(u2, w_pq[l], peer_sub_keys[l], peer_u[l], peer_v[l])
        x = layer_norm(DEEPNORM_ALPHA * x + (1.0 + gt2) * y_ffn) * ln2_g[l] + ln2_b[l]
    return x


_drawn_inputs = setup_inputs


def setup_inputs(seed=0):
    import zlib

    import numpy as np

    out = dict(_drawn_inputs(seed))
    spreads = {}
    factors = {'b_rg_a': 54.245, 'b_rg_x': 32.029, 'k_idx_g': 29.159, 'ln2_g': 7.629, 'ln2_b': 7.809}
    for name, (base, spread) in spreads.items():
        noise = np.random.default_rng([zlib.crc32(name.encode()), seed]).standard_normal(out[name].shape)
        drawn = base * np.exp(spread * noise) if base else spread * noise
        out[name] = __import__('jax').numpy.asarray(drawn.astype(out[name].dtype))
    for name, factor in factors.items():
        out[name] = (out[name] * factor).astype(out[name].dtype)
    return out
```

```python
from contextlib import ExitStack

import numpy as np
import concourse.bass as bass
from concourse import mybir

ALU = mybir.AluOpType
ACT = mybir.ActivationFunctionType
AX = mybir.AxisListType
F32 = mybir.dt.float32
I32 = mybir.dt.int32
U32 = mybir.dt.uint32

P = 128
SEQ = 256
TB = SEQ // P
D = 2048
KT = D // P
D_LRU = 1024
NLT = D_LRU // P
CONV_W = 4
NH, HD = 8, 128
NI, ID = 16, 64
CHUNK = 64
TOPK = 64
D_IN = 2 * D_LRU + 3 * NH * HD + NI * ID + ID + NI
COL_Q, COL_QI, COL_KI = 2 * D_LRU, 2 * D_LRU + 3 * NH * HD, 2 * D_LRU + 3 * NH * HD + NI * ID
NT = D_IN - COL_Q
T_Q, T_K, T_V, T_QI, T_KI, T_WI = 0, 1024, 2048, 3072, 4096, 4160
PH, NK, PK = 8, 128, 16
EPS = 1e-5
ALPHA = 2.0 ** 0.25
ROPE_THETA = 500000.0
RA, RI = 16, 8
NF = RA + RI
NEG = -1.0e30
TAKEN = -3.0e38

PIECE_K = 4
NPIECE = KT // PIECE_K
CW = 512
RING = 6
NGR = 8
NPAIR = 4
LO, HI = 0, 1

SH1, SC1, GT1, SH2, SC2, GT2 = range(6)

CHUNKS = [("ada", g, c) for g in (SH1, SC1) for c in range(4)]
CHUNKS += [("qi", 0, c) for c in range(2)] + [("q", 0, c) for c in range(2)] + [("k", 0, c) for c in range(2)]
CHUNKS += [("v", 0, c) for c in range(2)] + [("xl", 0, c) for c in range(2)] + [("gl", 0, c) for c in range(2)]
CHUNKS += [("ada", GT1, c) for c in range(4)] + [("ada", SC2, c) for c in range(4)] + [("ada", SH2, c) for c in range(4)]
CHUNKS += [("wo", 0, c) for c in range(4)] + [("ada", GT2, c) for c in range(4)] + [("pq", 0, c) for c in range(4)]
CHUNK_AT = {c: n for n, c in enumerate(CHUNKS)}

JOBS = [("par", 0, "dve"), ("par", 1, "dve")]
JOBS += [("zt", i, "act") for i in range(4)]
JOBS += [("ada", (g, c), "dve") for g in (SH1, SC1) for c in range(4)]
JOBS += [("kiwi", 0, "act"), ("qi", 0, "act"), ("qi", 1, "act"), ("q", 0, "act")]
JOBS += [("kit", 0, "dve"), ("qit", 0, "act"), ("qit", 1, "act"), ("q", 1, "act")]
JOBS += [("lg", i, "act") for i in range(6)]
JOBS += [("k", 0, "act"), ("k", 1, "act"), ("v", 0, "act"), ("v", 1, "act")]
JOBS += [("qt", 0, "act"), ("qt", 1, "act"), ("kt", 0, "act"), ("kt", 1, "act")]
JOBS += [("xl", 0, "act"), ("at", 0, "dve"), ("xl", 1, "act"), ("at", 1, "dve")]
JOBS += [("pt", 0, "act"), ("pv", 0, "act"), ("gl", 0, "act"), ("at", 2, "dve"), ("pt", 1, "act"), ("pv", 1, "act"),
         ("gl", 1, "act"), ("pt", 2, "act"), ("pv", 2, "act")]
JOBS += [("gate", i, "act") for i in range(4)]
JOBS += [("ada", (g, c), "dve") for g in (GT1, SC2, SH2) for c in range(4)]
JOBS += [("bc", (GT1, i), "act") for i in range(2)]
JOBS += [("wo", c, "dve") for c in range(4)]
JOBS += [("bc", (SC2, i), "act") for i in range(2)] + [("bc", (SH2, i), "act") for i in range(2)]
JOBS += [("skt", 0, "act"), ("skt", 1, "act")]
JOBS += [("ada", (GT2, c), "dve") for c in range(4)]
JOBS += [("ut", i, "act") for i in range(4)]
JOBS += [("pq", c, "act") for c in range(4)]
JOBS += [("sc", i, "act") for i in range(4)]
JOBS += [("bc", (GT2, i), "act") for i in range(2)]
JOB_AT = {(kind, i): n for n, (kind, i, _) in enumerate(JOBS)}
JOB_ENG = [e for _, _, e in JOBS]
JOB_OF = {c: ("ada", (c[1], c[2])) if c[0] == "ada" else (c[0], c[2]) for c in CHUNKS}
BC_SEEN = [i for k, i, _ in JOBS if k == "bc"]

PAR_C, PAR_BADA = 0, KT
PAR_CW, PAR_CB, PAR_BA, PAR_BX, PAR_LAM = 112, 144, 152, 160, 168
NPAR = 176
UNITS = [(0, 0, 8, P), (1, 0, 4, SEQ), (1, 4, 4, SEQ)]
LG_UNITS = [(0, 0, 8, P), (0, 8, 8, P)] + [(1, 4 * i, 4, SEQ) for i in range(4)]


class Steps:

    def __init__(self, eng, sem):
        self.eng, self.sem, self.n = eng, sem, 0

    def mark(self, ins):
        ins.then_inc(self.sem, 1)
        self.n += 1

    def settle(self):
        self.eng.wait_ge(self.sem, self.n)

    def restart(self):
        self.settle()
        self.eng.sem_clear(self.sem)
        self.n = 0

    def seq(self, ins):
        self.mark(ins)
        self.settle()


def lg_col(j, n, keys):
    return ((j % 2) * (n // 2) + j // 2) * keys


def take(eng, sem):
    eng.wait_ge(sem, 1)
    eng.sem_clear(sem)


def build_layer(nc, x, c, positions, w_ada, b_ada, w_in, conv_w, conv_b, w_rg_a, b_rg_a, w_rg_x, b_rg_x,
                lru_lambda, k_idx_g, w_out, ln1_g, ln1_b, w_pq, peer_sub_keys, peer_u, peer_v, ln2_g, ln2_b, out):
    ctx = ExitStack()
    with ctx:
        def sb(name, shape, dt=F32):
            return ctx.enter_context(nc.sbuf_tensor(name, shape, dt))

        def sem(name):
            return ctx.enter_context(nc.semaphore(name))

        arena = sb("arena", [P, 64 * 256])
        ring = arena[:, 0:RING * PIECE_K * CW].rearrange("p (s k n) -> p s k n", s=RING, k=PIECE_K)
        QK0 = RING * PIECE_K * CW
        qT = arena[:, QK0:QK0 + NH * SEQ].rearrange("p (h t) -> p h t", h=NH)
        kT = arena[:, QK0 + NH * SEQ:QK0 + 2 * NH * SEQ].rearrange("p (h t) -> p h t", h=NH)
        qpT = arena[:, QK0:QK0 + 2 * NH * SEQ].rearrange("p (h t) -> p h t", h=2 * PH)
        gathered = arena[:, :].rearrange("p (s d) -> p s d", s=NGR)
        xres = sb("xres", [P, TB, D])
        uT = sb("uT", [P, KT, SEQ])
        tokbuf = sb("tokbuf", [P, (17 * 256) + TB * D])
        tok = tokbuf[:, 0:TB * NT].rearrange("p (b n) -> p b n", b=TB)
        z = tokbuf[:, 0:TB * D].rearrange("p (b d) -> p b d", b=TB)
        u2 = z
        keyscore = tokbuf[:, TB * D:TB * D + 17 * 256]
        lru = sb("lru", [P, 5 * D + 32])
        work = [lru[:, 32 + i * D:32 + (i + 1) * D] for i in range(5)]
        xlp = lru[:, 0:NLT * (SEQ + 3)].rearrange("p (n t) -> p n t", n=NLT)
        xc, rg, ig, th = (w.rearrange("p (n t) -> p n t", n=NLT) for w in work[1:5])
        w_tail = work[3][:, 0:KT * 80].rearrange("p (k n) -> p k n", k=KT)
        PT = work[2].rearrange("p (u n) -> p u n", u=2)
        gate_w = work[4].rearrange("p (w n e) -> p w n e", w=2, n=NLT)
        bc = work
        BC_GT1, BC_G, BC_B, BC_SC2, BC_SH2 = range(5)
        BC_GT2 = BC_SC2
        concatT = sb("concatT", [P, KT, SEQ])
        qiT = concatT[:, NLT:KT, :]
        subkT = concatT[:, 0:NLT, :].rearrange("p n (a t) -> p (n a) t", a=2)
        sm = sb("sm", [P, 2, 1024])
        small = sb("small", [P, 1024])
        score = small[:, 0:TB * SEQ].rearrange("p (b s) -> p b s", b=TB)
        kdT = small[:, 512:768]
        kd = small[:, 768:1024].rearrange("p (b n) -> p b n", b=TB)
        cand = small[:, 0:256].rearrange("p (a c) -> p a c", a=PK)
        onehot = small[:, 256:512].rearrange("p (a c) -> p a c", a=PK)
        stage = small[:, 512:768].rearrange("p (a n) -> p a n", a=2)
        ident = sb("ident", [P, P])
        ones = sb("ones", [P, P])
        diag = sm[:, :, 512:1024].rearrange("p u (k n) -> p u k n", k=4)
        zeros = sm[:, 0, 0:512]
        paramA, paramB = sm[:, 0, 0:P], sm[:, 1, 0:P]
        parT = sb("parT", [P, NPAR])
        sT = sb("sT", [P, KT])
        mod = sb("mod", [P, 6 * KT])
        pos_i = sb("pos_i", [P, TB], I32)
        posf = sb("posf", [P, TB])
        freq = sb("freq", [P, NF])
        ang = sb("ang", [P, TB, NF])
        ang2 = sb("ang2", [P, TB, NF])
        sin = sb("sin", [P, TB, NF])
        cos = sb("cos", [P, TB, NF])
        kig = sb("kig", [P, ID])
        st = sb("st", [P, 4, 6])
        mv = sb("mv", [P, TB, 2])
        rstd = sb("rstd", [P, TB])
        m8 = sb("m8", [P, 8])
        amax = sb("amax", [P, 8])
        asum = sb("asum", [P, 8])
        sp = sb("sp", [P, 6, NLT])
        nsp8 = sb("nsp8", [P, NLT])
        psp8 = sb("psp8", [P, NLT])
        iota_i = sb("iota_i", [P, PK], I32)
        iota = sb("iota", [P, PK])
        topv = sb("topv", [P, 2, PK])
        topi = sb("topi", [P, 2, PK], U32)
        topf = sb("topf", [P, 2, PK])
        tops = sb("tops", [P, 2, PK])
        pick = sb("pick", [P, PK], U32)
        pick2 = sb("pick2", [P, 2, PK], U32)
        pickf = sb("pickf", [P, 2, PK])
        esel = sb("esel", [P, 2, PK])
        eidx = sb("eidx", [P, 2, PK], U32)
        ntop = sb("ntop", [P, 2])
        gexp = sb("gexp", [P, 2, PK])
        gsum = sb("gsum", [P, 2])
        dots = sb("dots", [P, 2, PK])
        gel = sb("gel", [P, 2, PK])
        hk = sb("hk", [P, 2, PK])
        ropet = sm[:, :, :].rearrange("p u n -> p (u n)")
        ps = ctx.enter_context(nc.psum_tensor("ps", [P, NPAIR, 1024], F32))

        piece_landed = [sem(f"piece_landed{i}") for i in range(RING)]
        pieces_used = sem("pieces_used")
        psum_full = sem("psum_full")
        psum_freed = {"act": sem("psum_freed_by_act"), "dve": sem("psum_freed_by_dve")}
        x_landed = [sem(f"x_landed{i}") for i in range(TB)]
        params_landed = sem("params_landed")
        small_landed = sem("small_landed")
        tail_landed = sem("tail_landed")
        gates_landed = sem("gates_landed")
        subkeys_landed = sem("subkeys_landed")
        ln1_landed = sem("ln1_landed")
        ln2_landed = sem("ln2_landed")
        out_landed = sem("out_landed")
        consts_ready = sem("consts_ready")
        pool_step = sem("pool_step")
        dve_step = sem("dve_step")
        act_step = sem("act_step")
        var_ready = sem("var_ready")
        std_ready = sem("std_ready")
        z_ready = sem("z_ready")
        zt_scaled = sem("zt_scaled")
        sT_ready = sem("sT_ready")
        lam_exp = sem("lam_exp")
        ang_ready = sem("ang_ready")
        sincos_ready = sem("sincos_ready")
        qi_roped = sem("qi_roped")
        kd_ready = sem("kd_ready")
        relu_used = sem("relu_used")
        qk_roped = sem("qk_roped")
        scored_ready = sem("scored_ready")
        exp_ready = sem("exp_ready")
        prob_ready = sem("prob_ready")
        xc_ready = sem("xc_ready")
        decay_ready = sem("decay_ready")
        pow_ready = sem("pow_ready")
        sqrt_ready = sem("sqrt_ready")
        lru_done = sem("lru_done")
        diag_built = sem("diag_built")
        u2_ready = sem("u2_ready")
        peer_zeros = sem("peer_zeros")
        stage_ready = sem("stage_ready")
        idx_ready = sem("idx_ready")
        top_ready = sem("top_ready")
        gexp_ready = sem("gexp_ready")
        dots_done = sem("dots_done")
        gel_ready = sem("gel_ready")
        hk_ready = sem("hk_ready")
        diag_ready = sem("diag_ready")
        row_landed = [sem(f"row_landed{i}") for i in range(NGR)]
        slot_free = [sem(f"slot_free{i}") for i in range(NGR)]
        v_started = sem("v_started")
        y_ready = sem("y_ready")
        out_ready = sem("out_ready")

        SRC = {"qi": (w_in, COL_QI), "q": (w_in, COL_Q), "k": (w_in, COL_Q + 1024), "v": (w_in, COL_Q + 2048),
               "xl": (w_in, 0), "gl": (w_in, D_LRU), "wo": (w_out, 0), "pq": (w_pq, 0)}
        u_rows = peer_u[0]
        v_rows = peer_v[0]

        def bank(name):
            return ps[:, JOB_AT[name] % NPAIR, :]

        def await_job(eng, name):
            eng.wait_ge(psum_full, JOB_AT[name] + 1)

        def await_taken(eng, name):
            n = JOB_AT[name]
            eng.wait_ge(psum_freed[JOB_ENG[n]], JOB_ENG[0:n + 1].count(JOB_ENG[n]))

        block = ctx.enter_context(nc.Block())

        @block.sync
        def _(sp_):
            for b in range(TB):
                sp_.dma_start(xres[:, b, :], x[0, b * P:(b + 1) * P, :]).then_inc(x_landed[b], 16)
            n = 0
            for kind, g, col in CHUNKS:
                w, c0 = (w_ada, g * D) if kind == "ada" else SRC[kind]
                for q in range(NPIECE):
                    old = n - RING
                    if old >= 0 and old % NPIECE == NPIECE - 1:
                        await_job(sp_, JOB_OF[CHUNKS[old // NPIECE]])
                    elif old >= 0:
                        sp_.wait_ge(pieces_used, old - old // NPIECE + 1)
                    src = w[0, q * PIECE_K * P:(q + 1) * PIECE_K * P, c0 + col * CW:c0 + (col + 1) * CW]
                    sp_.dma_start(ring[:, n % RING], src.rearrange("(k p) n -> p k n", p=P)).then_inc(
                        piece_landed[n % RING], 16)
                    n += 1
            for b in range(TB):
                sp_.wait_ge(out_ready, b + 1)
                sp_.dma_start(out[0, b * P:(b + 1) * P, :], xres[:, b, :]).then_inc(out_landed, 16)
            sp_.wait_ge(out_landed, 16 * TB)

        @block.gpsimd
        def _(pool):
            g = nc.gpsimd
            steps = Steps(pool, pool_step)
            steps.mark(g.memset(ident[:, :], 0.0))
            g.memset(ones[:, :], 1.0).then_inc(consts_ready, 1)
            for j in range(RA):
                f = float(np.float32(ROPE_THETA) ** (-np.float32(j) / np.float32(RA)))
                g.memset(freq[:, j:j + 1], f).then_inc(consts_ready, 1)
            for j in range(RI):
                f = float(np.float32(ROPE_THETA) ** (-np.float32(j) / np.float32(RI)))
                g.memset(freq[:, RA + j:RA + j + 1], f).then_inc(consts_ready, 1)
            steps.settle()
            g.affine_select(out=ident[:, :], in_=ident[:, :], compare_op=ALU.not_equal, fill=1.0, base=0,
                            pattern=[[-1, P]], channel_multiplier=1).then_inc(consts_ready, 1)
            g.iota(iota_i[:, :], pattern=[[1, PK]], base=0, channel_multiplier=0).then_inc(consts_ready, 1)

            await_taken(pool, ("bc", (GT2, 1)))
            for slot in slot_free:
                pool.sem_inc(slot, 1)
            for b in range(TB):
                with pool.Fori(0, PH // 2) as r:
                    for par in range(2):
                        take(pool, idx_ready)
                        for use in range(4):
                            for s in range(NGR):
                                k = (use % 2) * NGR + s
                                take(pool, slot_free[s])
                                rows = u_rows if use < 2 else v_rows
                                g.indirect_dma_start(
                                    out=gathered[:, s, :], out_offset=None, in_=rows,
                                    in_offset=bass.IndirectOffsetOnAxis(ap=eidx[:, par, k:k + 1], axis=0),
                                ).then_inc(row_landed[s], 16)

        @block.scalar
        def _(act):
            s = nc.scalar
            steps = Steps(act, act_step)

            def free(ins):
                ins.then_inc(psum_freed["act"], 1)

            def row(v, n):
                return v.rearrange("l (r p) -> (l r) p", p=P)[0:n]

            act.dma_start(paramA[PAR_C:PAR_C + KT, :], c.rearrange("l (r p) -> (l r) p", p=P)).then_inc(params_landed, 16)
            act.dma_start(paramA[PAR_BADA:PAR_BADA + 96, :], row(b_ada, 96)).then_inc(params_landed, 16)
            act.dma_start(paramB[0:32, :], conv_w[0].rearrange("j (n p) -> (j n) p", p=P)).then_inc(params_landed, 16)
            for i, v in enumerate((conv_b, b_rg_a, b_rg_x, lru_lambda)):
                act.dma_start(paramB[32 + 8 * i:40 + 8 * i, :], row(v, 8)).then_inc(params_landed, 16)
            for b in range(TB):
                act.dma_start(pos_i[:, b:b + 1], positions[0, b * P:(b + 1) * P].unsqueeze(1)).then_inc(small_landed, 16)
            act.dma_start(kig[:, :], k_idx_g[0].partition_broadcast(P)).then_inc(small_landed, 16)
            act.dma_start(w_tail, w_in[0, :, COL_KI:D_IN].rearrange("(k p) n -> p k n", p=P)).then_inc(tail_landed, 16)
            act.dma_start(gate_w[:, 0], w_rg_a[0].rearrange("n d e -> d n e")).then_inc(gates_landed, 16)
            act.dma_start(gate_w[:, 1], w_rg_x[0].rearrange("n d e -> d n e")).then_inc(gates_landed, 16)

            await_taken(act, ("par", 0))
            s.activation(sT[:, :], parT[:, PAR_C:PAR_C + KT], ACT.Silu).then_inc(sT_ready, 1)
            for b in range(TB):
                act.wait_ge(var_ready, b + 1)
                s.activation(rstd[:, b:b + 1], rstd[:, b:b + 1], ACT.Sqrt).then_inc(std_ready, 1)
            for i in range(4):
                b, half = i // 2, i % 2
                await_job(act, ("zt", i))
                free(s.copy(uT[:, 8 * half:8 * half + 8, b * P:(b + 1) * P],
                            bank(("zt", i)).rearrange("p (k t) -> p k t", k=8)))
            act.wait_ge(ang_ready, 1)
            s.activation(sin[:, :, :], ang[:, :, :], ACT.Sin).then_inc(sincos_ready, 1)
            s.activation(cos[:, :, :], ang2[:, :, :], ACT.Sin).then_inc(sincos_ready, 1)
            act.wait_ge(lam_exp, 1)
            s.activation(sp[:, 1, :], sp[:, 0, :], ACT.Exp).then_inc(lam_exp, 1)

            await_job(act, ("kiwi", 0))
            free(s.copy(tok[:, :, T_KI:NT],
                        bank(("kiwi", 0)).rearrange("p (b n) -> p b n", b=TB)[:, :, 0:80]))

            def keep(kind, cc, at):
                await_job(act, (kind, cc))
                free(s.copy(tok[:, :, at + cc * CW:at + (cc + 1) * CW],
                            bank((kind, cc)).rearrange("p (b n) -> p b n", b=TB)))

            keep("qi", 0, T_QI)
            keep("qi", 1, T_QI)
            for b in range(TB):
                act.wait_ge(var_ready, TB + b + 1)
                s.activation(rstd[:, b:b + 1], rstd[:, b:b + 1], ACT.Sqrt).then_inc(std_ready, 1)
            keep("q", 0, T_Q)
            for i in range(2):
                await_job(act, ("qit", i))
                free(s.copy(qiT[:, 4 * i:4 * i + 4, :], bank(("qit", i)).rearrange("p (h t) -> p h t", h=4)))
            keep("q", 1, T_Q)
            for i, (b, h0, n, keys) in enumerate(LG_UNITS):
                await_job(act, ("lg", i))
                if i >= 2:
                    act.wait_ge(relu_used, i - 1)
                free(s.activation(sm[:, i % 2, :], bank(("lg", i)), ACT.Relu, scale=ID ** -0.5))
            keep("k", 0, T_K)
            keep("k", 1, T_K)
            keep("v", 0, T_V)
            keep("v", 1, T_V)
            for i in range(2):
                await_job(act, ("qt", i))
                free(s.copy(qT[:, 4 * i:4 * i + 4, :], bank(("qt", i)).rearrange("p (h t) -> p h t", h=4)))
            for i in range(2):
                await_job(act, ("kt", i))
                free(s.copy(kT[:, 4 * i:4 * i + 4, :], bank(("kt", i)).rearrange("p (h t) -> p h t", h=4)))

            def keep_xl(i):
                await_job(act, ("xl", i))
                free(s.copy(xlp[:, 4 * i:4 * i + 4, 3:3 + SEQ], bank(("xl", i)).rearrange("p (n t) -> p n t", n=4)))

            def keep_gl(i):
                await_job(act, ("gl", i))
                free(s.activation(concatT[:, 4 * i:4 * i + 4, :], bank(("gl", i)).rearrange("p (n t) -> p n t", n=4),
                                  ACT.Gelu_apprx_tanh))

            def exps(u):
                b, h0, n, keys = UNITS[u]
                act.wait_ge(scored_ready, u + 1)
                for h in range(n):
                    sl = sm[:, u % 2, h * keys:(h + 1) * keys]
                    s.activation(sl, sl, ACT.Exp, bias=amax[:, h:h + 1],
                                 accum_out=asum[:, h:h + 1]).then_inc(exp_ready, 1)

            def probs_out(u):
                b, h0, n, keys = UNITS[u]
                await_job(act, ("pt", u))
                free(s.copy(PT[:, u % 2, :], bank(("pt", u))))
                await_job(act, ("pv", u))
                free(s.copy(concatT[:, NLT + h0:NLT + h0 + n, b * P:(b + 1) * P],
                            bank(("pv", u))[:, 0:n * P].rearrange("p (h t) -> p h t", h=n)))

            keep_xl(0)
            exps(0)
            keep_xl(1)
            exps(1)
            probs_out(0)
            keep_gl(0)
            exps(2)
            probs_out(1)
            keep_gl(1)
            probs_out(2)
            for i in range(4):
                await_job(act, ("gate", i))
                pb = bank(("gate", i)).rearrange("p (n g t) -> p n g t", n=2, g=2)
                for j in range(2):
                    n = 2 * i + j
                    steps.mark(s.activation(rg[:, n], pb[:, j, 0], ACT.Sigmoid, bias=parT[:, PAR_BA + n:PAR_BA + n + 1]))
                    ins = s.activation(ig[:, n], pb[:, j, 1], ACT.Sigmoid, bias=parT[:, PAR_BX + n:PAR_BX + n + 1])
                free(ins)
            steps.settle()
            for n in range(NLT):
                steps.mark(s.activation(th[:, n], rg[:, n], ACT.Tanh, scale=psp8[:, n:n + 1]))
            for n in range(NLT):
                s.activation(rg[:, n], rg[:, n], ACT.Exp, scale=nsp8[:, n:n + 1]).then_inc(decay_ready, 1)
            act.wait_ge(pow_ready, 1)
            s.activation(th[:, :, :], th[:, :, :], ACT.Sqrt).then_inc(sqrt_ready, 1)

            def broadcast_out(vec, slot):
                for i in range(2):
                    await_job(act, ("bc", (vec, i)))
                    free(s.copy(bc[slot][:, 1024 * i:1024 * (i + 1)], bank(("bc", (vec, i)))))

            act.wait_ge(lru_done, 1)
            await_job(act, ("gate", 3))
            act.dma_start(bc[BC_G], ln1_g[0].partition_broadcast(P)).then_inc(ln1_landed, 16)
            act.dma_start(bc[BC_B], ln1_b[0].partition_broadcast(P)).then_inc(ln1_landed, 16)
            act.dma_start(keyscore[:, 0:2 * PH * P].rearrange("p (h d) -> p h d", h=2 * PH),
                          peer_sub_keys[0].rearrange("h a n d -> n (h a) d")).then_inc(subkeys_landed, 16)
            broadcast_out(GT1, BC_GT1)
            broadcast_out(SC2, BC_SC2)
            broadcast_out(SH2, BC_SH2)
            for i in range(2):
                await_job(act, ("skt", i))
                free(s.copy(subkT[:, 8 * i:8 * i + 8, :], bank(("skt", i)).rearrange("p (n t) -> p n t", n=8)))
            for b in range(TB):
                for i in range(2):
                    act.wait_ge(var_ready, 2 * TB + 2 * b + i + 1)
                    s.activation(rstd[:, b:b + 1], rstd[:, b:b + 1], ACT.Sqrt).then_inc(std_ready, 1)
            for i in range(4):
                b, half = i // 2, i % 2
                await_job(act, ("ut", i))
                free(s.copy(uT[:, 8 * half:8 * half + 8, b * P:(b + 1) * P],
                            bank(("ut", i)).rearrange("p (k t) -> p k t", k=8)))
            for i in range(4):
                await_job(act, ("pq", i))
                free(s.copy(qpT[:, 4 * i:4 * i + 4, :], bank(("pq", i)).rearrange("p (h t) -> p h t", h=4)))
            for i in range(4):
                await_job(act, ("sc", i))
                free(s.copy(keyscore[:, 1024 * i:1024 * (i + 1)], bank(("sc", i))))
            act.wait_ge(u2_ready, TB)
            act.dma_start(bc[BC_G], ln2_g[0].partition_broadcast(P)).then_inc(ln2_landed, 16)
            act.dma_start(bc[BC_B], ln2_b[0].partition_broadcast(P)).then_inc(ln2_landed, 16)
            broadcast_out(GT2, BC_GT2)

            await_taken(act, ("sc", 3))
            s.copy(stage[:, :, :].rearrange("p a n -> p (a n)"), keyscore[:, 0:256]).then_inc(stage_ready, 1)
            for b in range(TB):
                with act.Fori(0, PH // 2) as r:
                    for par in range(2):
                        it = r * 2 + (PH * b + par)
                        act.wait_ge(top_ready, it + 1)
                        s.activation(gexp[:, par, :], tops[:, par, :], ACT.Exp, bias=ntop[:, par:par + 1],
                                     accum_out=gsum[:, par:par + 1]).then_inc(gexp_ready, 1)
                        s.copy(stage[:, :, :].rearrange("p a n -> p (a n)"),
                               keyscore[:, bass.ds(it * 256 + 256, 256)]).then_inc(stage_ready, 1)
                        act.wait_ge(dots_done, it + 1)
                        s.activation(gel[:, par, :], dots[:, par, :], ACT.Gelu_apprx_tanh).then_inc(gel_ready, 1)
                        act.wait_ge(hk_ready, it + 1)
                        for k in range(PK):
                            act.wait_ge(v_started, it * PK + (k + PK - 8 + 2))
                            s.mul(diag[:, k // 4 % 2, k % 4, :], ident[:, :], hk[:, par, k:k + 1]).then_inc(diag_ready, 1)
            for b in range(TB):
                act.wait_ge(var_ready, 4 * TB + b + 1)
                s.activation(rstd[:, b:b + 1], rstd[:, b:b + 1], ACT.Sqrt).then_inc(std_ready, 1)

        @block.vector
        def _(dve):
            v = nc.vector
            steps = Steps(dve, dve_step)
            norms = [0]

            def free(ins):
                ins.then_inc(psum_freed["dve"], 1)

            def normalise(b, dst, src):
                w = src.shape[-1]
                parts = max(1, w // 512)
                for i in range(parts):
                    steps.mark(v.bn_stats(st[:, i, :], src[:, i * (w // parts):(i + 1) * (w // parts)]))
                steps.settle()
                steps.seq(v.bn_aggr(mv[:, b, :], st[:, 0:parts, :]))
                v.tensor_scalar(rstd[:, b:b + 1], mv[:, b, 1:2], EPS, None, ALU.add).then_inc(var_ready, 1)
                norms[0] += 1
                dve.wait_ge(std_ready, norms[0])
                steps.seq(v.reciprocal(rstd[:, b:b + 1], rstd[:, b:b + 1]))
                return v.tensor_scalar(dst, src, mv[:, b, 0:1], rstd[:, b:b + 1], ALU.subtract, ALU.mult)

            for i, (c0, n) in enumerate(((0, 112), (112, 64))):
                await_job(dve, ("par", i))
                free(v.tensor_copy(parT[:, c0:c0 + n], bank(("par", i))[:, 0:n]))
            for b in range(TB):
                dve.wait_ge(x_landed[b], 16)
                normalise(b, z[:, b, :], xres[:, b, :]).then_inc(z_ready, 1)

            await_taken(dve, ("par", 1))
            TWO_PI = 2.0 * np.pi
            C1 = 6.28125
            C2 = 0.00193500518798828125
            C3 = float(TWO_PI - C1 - C2)
            ROUND = 1.5 * 2.0 ** 23
            dve.wait_ge(small_landed, 48)
            dve.wait_ge(consts_ready, 1 + NF + 2)
            steps.seq(v.tensor_copy(posf[:, :], pos_i[:, :]))
            for b in range(TB):
                steps.mark(v.tensor_scalar(ang[:, b, :], freq[:, :], posf[:, b:b + 1], None, ALU.mult))
            steps.settle()
            steps.seq(v.tensor_scalar(ang2[:, :, :], ang[:, :, :], 1.0 / TWO_PI, ROUND, ALU.mult, ALU.add))
            steps.seq(v.tensor_scalar(ang2[:, :, :], ang2[:, :, :], -ROUND, None, ALU.add))
            for part in (C1, C2, C3):
                steps.seq(v.scalar_tensor_tensor(out=ang[:, :, :], in0=ang2[:, :, :], scalar=-part, in1=ang[:, :, :],
                                                 op0=ALU.mult, op1=ALU.add))
            PI32 = float(np.nextafter(np.float32(np.pi), np.float32(0)))
            steps.seq(v.tensor_scalar(ang[:, :, :], ang[:, :, :], PI32, -PI32, ALU.min, ALU.max))
            steps.seq(v.tensor_scalar(ang2[:, :, :], ang[:, :, :], -1.0, None, ALU.mult))
            steps.seq(v.tensor_tensor(ang2[:, :, :], ang[:, :, :], ang2[:, :, :], ALU.max))
            v.tensor_scalar(ang2[:, :, :], ang2[:, :, :], -1.0, float(np.pi / 2), ALU.mult, ALU.add).then_inc(ang_ready, 1)

            steps.mark(v.tensor_copy(iota[:, :], iota_i[:, :]))
            lam = parT[:, PAR_LAM:PAR_LAM + NLT]
            steps.seq(v.tensor_scalar(sp[:, 2, :], lam, -1.0, None, ALU.mult))
            steps.seq(v.tensor_tensor(sp[:, 0, :], lam, sp[:, 2, :], ALU.min))
            v.tensor_scalar(sp[:, 2, :], sp[:, 2, :], 0.0, None, ALU.max).then_inc(lam_exp, 1)
            dve.wait_ge(lam_exp, 2)
            steps.seq(v.tensor_scalar(sp[:, 3, :], sp[:, 1, :], 2.0, None, ALU.add))
            steps.seq(v.reciprocal(sp[:, 3, :], sp[:, 3, :]))
            steps.seq(v.tensor_tensor(sp[:, 3, :], sp[:, 3, :], sp[:, 1, :], ALU.mult))
            steps.seq(v.tensor_tensor(sp[:, 4, :], sp[:, 3, :], sp[:, 3, :], ALU.mult))
            NTERM = 9
            steps.seq(v.tensor_scalar(sp[:, 5, :], sp[:, 4, :], 1.0 / (2 * NTERM + 1), 1.0 / (2 * NTERM - 1), ALU.mult, ALU.add))
            for j in range(NTERM - 1, 0, -1):
                steps.seq(v.tensor_tensor(sp[:, 5, :], sp[:, 5, :], sp[:, 4, :], ALU.mult))
                steps.seq(v.tensor_scalar(sp[:, 5, :], sp[:, 5, :], 1.0 / (2 * j - 1), None, ALU.add))
            steps.seq(v.tensor_tensor(sp[:, 5, :], sp[:, 5, :], sp[:, 3, :], ALU.mult))
            steps.seq(v.scalar_tensor_tensor(out=sp[:, 5, :], in0=sp[:, 5, :], scalar=2.0, in1=sp[:, 2, :],
                                             op0=ALU.mult, op1=ALU.add))
            steps.mark(v.tensor_scalar(nsp8[:, :], sp[:, 5, :], -8.0, None, ALU.mult))
            steps.mark(v.tensor_scalar(psp8[:, :], sp[:, 5, :], 8.0, None, ALU.mult))
            steps.mark(v.memset(xlp[:, :, 0:3], 0.0))
            steps.settle()

            def modulation(group):
                for cc in range(4):
                    j = group * KT + 4 * cc
                    await_job(dve, ("ada", (group, cc)))
                    free(v.scalar_tensor_tensor(out=mod[:, j:j + 4], in0=bank(("ada", (group, cc)))[:, 0:4],
                                                scalar=0.0 if group in (SH1, SH2) else 1.0,
                                                in1=parT[:, PAR_BADA + j:PAR_BADA + j + 4], op0=ALU.add, op1=ALU.add))
                await_taken(dve, ("ada", (group, 3)))

            modulation(SH1)
            modulation(SC1)
            await_taken(dve, ("zt", 3))
            for k in range(KT):
                v.tensor_scalar(uT[:, k, :], uT[:, k, :], mod[:, SC1 * KT + k:SC1 * KT + k + 1],
                                mod[:, SH1 * KT + k:SH1 * KT + k + 1], ALU.mult, ALU.add).then_inc(zt_scaled, 1)

            def rope(col, heads, width, half, f0):
                xs = tok[:, :, col:col + heads * width].rearrange("p b (h w) -> p b h w", h=heads)
                x1, x2 = xs[:, :, :, 0:half], xs[:, :, :, half:2 * half]
                cs = cos[:, :, f0:f0 + half].unsqueeze(2).to_broadcast([P, TB, heads, half])
                sn = sin[:, :, f0:f0 + half].unsqueeze(2).to_broadcast([P, TB, heads, half])
                n = TB * heads * half
                t = [ropet[:, i * 512:i * 512 + n].rearrange("p (b h f) -> p b h f", b=TB, h=heads) for i in range(4)]
                steps.mark(v.tensor_tensor(t[0], x1, cs, ALU.mult))
                steps.mark(v.tensor_tensor(t[1], x2, sn, ALU.mult))
                steps.mark(v.tensor_tensor(t[2], x2, cs, ALU.mult))
                steps.mark(v.tensor_tensor(t[3], x1, sn, ALU.mult))
                steps.settle()
                steps.mark(v.tensor_tensor(x1, t[0], t[1], ALU.subtract))
                return v.tensor_tensor(x2, t[2], t[3], ALU.add)

            dve.wait_ge(sincos_ready, 2)
            await_taken(dve, ("kiwi", 0))
            for b in range(TB):
                ki = tok[:, b, T_KI:T_KI + ID]
                steps.seq(normalise(b, ki, ki))
                steps.seq(v.tensor_tensor(ki, ki, kig[:, :], ALU.mult))
            steps.seq(rope(T_KI, 1, ID, RI, RA))
            for i in range(2):
                v.tensor_copy(kd[:, :, ID * i:ID * (i + 1)], tok[:, :, T_KI:T_KI + ID]).then_inc(kd_ready, 1)
            steps.seq(v.tensor_scalar(tok[:, :, T_WI:T_WI + NI], tok[:, :, T_WI:T_WI + NI], NI ** -0.5, None, ALU.mult))
            await_taken(dve, ("qi", 1))
            rope(T_QI, NI, ID, RI, RA).then_inc(qi_roped, 1)
            await_job(dve, ("kit", 0))
            free(v.tensor_copy(kdT, bank(("kit", 0))[:, 0:SEQ]))

            seen = 0
            for i, (b, h0, n, keys) in enumerate(LG_UNITS):
                await_taken(dve, ("lg", i))
                for j in range(n):
                    h = h0 + j
                    wcol = tok[:, b, T_WI + h:T_WI + h + 1]
                    o = lg_col(j, n, keys)
                    rl = sm[:, i % 2, o:o + keys]
                    if h == 0:
                        ins = v.tensor_scalar(score[:, b, 0:keys], rl, wcol, None, ALU.mult)
                    else:
                        ins = v.scalar_tensor_tensor(out=score[:, b, 0:keys], in0=rl, scalar=wcol,
                                                     in1=score[:, b, 0:keys], op0=ALU.mult, op1=ALU.add)
                    if j == n - 1:
                        ins.then_inc(relu_used, 1)
                        dve.wait_ge(relu_used, i + 1)
                    else:
                        steps.seq(ins)
            for b in range(TB):
                steps.mark(v.memset(score[0:CHUNK, b, (2 * b + 1) * CHUNK:(2 * b + 2) * CHUNK], NEG))
            steps.settle()
            for rnd in range(TOPK // 8):
                for b in range(TB):
                    keys = (b + 1) * P
                    steps.seq(v.max(m8[:, :], score[:, b, 0:keys]))
                    steps.seq(v.match_replace(score[:, b, 0:keys], m8[:, :], score[:, b, 0:keys], TAKEN))
            for b in range(TB):
                keys = (b + 1) * P
                steps.seq(v.tensor_scalar(score[:, b, 0:keys], score[:, b, 0:keys], TAKEN / 2, NEG, ALU.is_gt, ALU.mult))

            await_taken(dve, ("k", 1))
            rope(T_Q, 2 * NH, HD, RA, 0).then_inc(qk_roped, 1)
            dve.wait_ge(qk_roped, 1)

            def attention_scores(u):
                b, h0, n, keys = UNITS[u]
                await_job(dve, ("at", u))
                if u == 2:
                    dve.wait_ge(psum_full, JOB_AT[("pt", 0)] + 1)
                sc = sm[:, u % 2, :].rearrange("p (h k) -> p h k", h=n)
                free(v.scalar_tensor_tensor(out=sc, in0=bank(("at", u)).rearrange("p (h k) -> p h k", h=n),
                                            scalar=HD ** -0.5,
                                            in1=score[:, b, 0:keys].unsqueeze(1).to_broadcast([P, n, keys]),
                                            op0=ALU.mult, op1=ALU.add))
                await_taken(dve, ("at", u))
                steps.seq(v.tensor_reduce(amax[:, 0:n], sc, AX.X, ALU.max))
                v.tensor_scalar(amax[:, 0:n], amax[:, 0:n], -1.0, None, ALU.mult).then_inc(scored_ready, 1)

            def probabilities(u):
                b, h0, n, keys = UNITS[u]
                dve.wait_ge(exp_ready, sum(w[2] for w in UNITS[0:u + 1]))
                steps.seq(v.reciprocal(asum[:, 0:n], asum[:, 0:n]))
                sc = sm[:, u % 2, :].rearrange("p (h k) -> p h k", h=n)
                v.tensor_tensor(sc, sc, asum[:, 0:n].unsqueeze(2).to_broadcast([P, n, keys]),
                                ALU.mult).then_inc(prob_ready, 1)
                dve.wait_ge(prob_ready, u + 1)

            def conv(i):
                await_taken(dve, ("xl", i))
                for j in range(CONV_W):
                    for n in range(4 * i, 4 * i + 4):
                        wj = parT[:, PAR_CW + j * NLT + n:PAR_CW + j * NLT + n + 1]
                        if j == 0:
                            ins = v.tensor_scalar(xc[:, n], xlp[:, n, 0:SEQ], wj, parT[:, PAR_CB + n:PAR_CB + n + 1],
                                                  ALU.mult, ALU.add)
                        else:
                            ins = v.scalar_tensor_tensor(out=xc[:, n], in0=xlp[:, n, j:j + SEQ], scalar=wj,
                                                         in1=xc[:, n], op0=ALU.mult, op1=ALU.add)
                        if j < CONV_W - 1:
                            steps.mark(ins)
                        else:
                            ins.then_inc(xc_ready, 1)
                    if j < CONV_W - 1:
                        steps.settle()

            attention_scores(0)
            probabilities(0)
            conv(0)
            attention_scores(1)
            probabilities(1)
            attention_scores(2)
            probabilities(2)
            conv(1)

            dve.wait_ge(xc_ready, NLT)
            await_taken(dve, ("gate", 3))
            steps.seq(v.tensor_tensor(xc[:, :, :], xc[:, :, :], ig[:, :, :], ALU.mult))
            dve.wait_ge(decay_ready, NLT)
            steps.seq(v.tensor_tensor(ig[:, :, :], rg[:, :, :], rg[:, :, :], ALU.mult))
            v.scalar_tensor_tensor(out=th[:, :, :], in0=ig[:, :, :], scalar=1.0, in1=th[:, :, :], op0=ALU.add,
                                   op1=ALU.mult).then_inc(pow_ready, 1)
            dve.wait_ge(sqrt_ready, 1)
            steps.seq(v.tensor_tensor(xc[:, :, :], xc[:, :, :], th[:, :, :], ALU.mult))
            for n in range(NLT):
                steps.mark(v.tensor_tensor_scan(ig[:, n], rg[:, n], xc[:, n], 0.0, ALU.mult, ALU.add))
            steps.settle()
            v.tensor_tensor(concatT[:, 0:NLT, :], ig[:, :, :], concatT[:, 0:NLT, :], ALU.mult).then_inc(lru_done, 1)
            for group in (GT1, SC2, SH2):
                modulation(group)

            def diagonals(vec):
                for i in range(2):
                    n = BC_SEEN.index((vec, i))
                    if n:
                        await_job(dve, ("bc", BC_SEEN[n - 1]))
                    j = vec * KT + 8 * i
                    cols = mod[:, j:j + 8].rearrange("p (u k) -> p u k", u=2).unsqueeze(3)
                    eye = ident[:, :].unsqueeze(1).unsqueeze(1)
                    v.tensor_tensor(diag, eye.to_broadcast([P, 2, 4, P]), cols.to_broadcast([P, 2, 4, P]),
                                    ALU.mult).then_inc(diag_built, 1)

            diagonals(GT1)

            await_taken(dve, ("bc", (GT1, 1)))
            for cc in range(4):
                await_job(dve, ("wo", cc))
                sl = slice(cc * CW, (cc + 1) * CW)
                pb = bank(("wo", cc)).rearrange("p (b n) -> p b n", b=TB)
                tmp = sm[:, :, 0:CW]
                free(v.tensor_tensor(tmp, pb, bc[BC_GT1][:, sl].unsqueeze(1).to_broadcast([P, TB, CW]), ALU.mult))
                await_taken(dve, ("wo", cc))
                steps.seq(v.scalar_tensor_tensor(out=xres[:, :, sl], in0=xres[:, :, sl], scalar=ALPHA, in1=tmp,
                                                 op0=ALU.mult, op1=ALU.add))
            diagonals(SC2)
            diagonals(SH2)
            dve.wait_ge(ln1_landed, 32)
            for b in range(TB):
                steps.seq(normalise(b, xres[:, b, :], xres[:, b, :]))
                steps.seq(v.tensor_tensor(xres[:, b, :], xres[:, b, :], bc[BC_G], ALU.mult))
                steps.seq(v.tensor_tensor(xres[:, b, :], xres[:, b, :], bc[BC_B], ALU.add))
                steps.seq(normalise(b, u2[:, b, :], xres[:, b, :]))
                if b == 0:
                    await_taken(dve, ("bc", (SH2, 1)))
                steps.seq(v.tensor_tensor(u2[:, b, :], u2[:, b, :], bc[BC_SC2], ALU.mult))
                v.tensor_tensor(u2[:, b, :], u2[:, b, :], bc[BC_SH2], ALU.add).then_inc(u2_ready, 1)
            modulation(GT2)
            diagonals(GT2)
            await_job(dve, ("skt", 1))
            v.memset(keyscore[:, 16 * 256:17 * 256], 0.0).then_inc(peer_zeros, 1)
            v.memset(zeros, 0.0).then_inc(peer_zeros, 1)
            dve.wait_ge(u2_ready, TB)

            def route(it, par):
                take(dve, stage_ready)
                for i in range(2):
                    steps.mark(v.max(topv[:, i, 0:8], stage[:, i, :]))
                steps.settle()
                for i in range(2):
                    steps.mark(v.max_index(topi[:, i, 0:8], topv[:, i, 0:8], stage[:, i, :]))
                    steps.mark(v.match_replace(stage[:, i, :], topv[:, i, 0:8], stage[:, i, :], TAKEN))
                steps.settle()
                for i in range(2):
                    steps.mark(v.max(topv[:, i, 8:16], stage[:, i, :]))
                steps.settle()
                for i in range(2):
                    steps.mark(v.max_index(topi[:, i, 8:16], topv[:, i, 8:16], stage[:, i, :]))
                steps.mark(v.tensor_tensor(cand[:, :, :], topv[:, 0, :].unsqueeze(2).to_broadcast([P, PK, PK]),
                                           topv[:, 1, :].unsqueeze(1).to_broadcast([P, PK, PK]), ALU.add))
                steps.settle()
                cf = cand[:, :, :].rearrange("p a c -> p (a c)")
                steps.mark(v.tensor_copy(topf[:, :, :], topi[:, :, :]))
                steps.seq(v.max(tops[:, par, 0:8], cf))
                steps.mark(v.max_index(pick[:, 0:8], tops[:, par, 0:8], cf))
                steps.seq(v.match_replace(cf, tops[:, par, 0:8], cf, TAKEN))
                steps.seq(v.max(tops[:, par, 8:16], cf))
                steps.mark(v.tensor_scalar(ntop[:, par:par + 1], tops[:, par, 0:1], -1.0, None, ALU.mult))
                v.max_index(pick[:, 8:16], tops[:, par, 8:16], cf).then_inc(top_ready, 1)
                steps.settle()
                dve.wait_ge(top_ready, it + 1)
                steps.mark(v.tensor_scalar(pick2[:, 0, :], pick[:, :], 4, None, ALU.logical_shift_right))
                steps.mark(v.tensor_scalar(pick2[:, 1, :], pick[:, :], PK - 1, None, ALU.bitwise_and))
                steps.settle()
                steps.seq(v.tensor_copy(pickf[:, :, :], pick2[:, :, :]))
                for i in range(2):
                    steps.seq(v.tensor_tensor(onehot[:, :, :], pickf[:, i, :].unsqueeze(2).to_broadcast([P, PK, PK]),
                                              iota[:, :].unsqueeze(1).to_broadcast([P, PK, PK]), ALU.is_equal))
                    steps.seq(v.tensor_tensor(onehot[:, :, :], onehot[:, :, :],
                                              topf[:, i, :].unsqueeze(1).to_broadcast([P, PK, PK]), ALU.mult))
                    steps.seq(v.tensor_reduce(esel[:, i, :], onehot[:, :, :], AX.X, ALU.add))
                v.scalar_tensor_tensor(out=eidx[:, par, :], in0=esel[:, 0, :], scalar=float(NK), in1=esel[:, 1, :],
                                       op0=ALU.mult, op1=ALU.add).then_inc(idx_ready, 1)

            for b in range(TB):
                steps.restart()
                with dve.Fori(0, PH // 2) as r:
                    for par in range(2):
                        it = r * 2 + (PH * b + par)
                        route(it, par)
                        for k in range(PK):
                            dve.wait_ge(row_landed[k % NGR], it * 64 + 16 * (k // NGR + 1))
                            v.scalar_tensor_tensor(out=gathered[:, k % NGR, :], in0=gathered[:, k % NGR, :], scalar=1.0,
                                                   in1=u2[:, b, :], op0=ALU.mult, op1=ALU.mult,
                                                   accum_out=dots[:, par, k:k + 1]).then_inc(slot_free[k % NGR], 1)
                        dve.wait_ge(gexp_ready, it + 1)
                        v.reciprocal(gsum[:, par:par + 1], gsum[:, par:par + 1]).then_inc(dots_done, 1)
                        dve.wait_ge(dots_done, it + 1)
                        dve.wait_ge(gel_ready, it + 1)
                        v.scalar_tensor_tensor(out=hk[:, par, :], in0=gexp[:, par, :], scalar=gsum[:, par:par + 1],
                                               in1=gel[:, par, :], op0=ALU.mult, op1=ALU.mult).then_inc(hk_ready, 1)
                    steps.restart()

            await_taken(dve, ("bc", (GT2, 1)))
            dve.wait_ge(ln2_landed, 32)
            for b in range(TB):
                dve.wait_ge(y_ready, b + 1)
                y = ps[:, 2 * b:2 * b + 2, :].rearrange("p a n -> p (a n)")
                steps.seq(v.tensor_tensor(u2[:, b, :], y, bc[BC_GT2], ALU.mult))
                steps.seq(v.scalar_tensor_tensor(out=xres[:, b, :], in0=xres[:, b, :], scalar=ALPHA, in1=u2[:, b, :],
                                                 op0=ALU.mult, op1=ALU.add))
                steps.seq(normalise(b, xres[:, b, :], xres[:, b, :]))
                steps.seq(v.tensor_tensor(xres[:, b, :], xres[:, b, :], bc[BC_G], ALU.mult))
                v.tensor_tensor(xres[:, b, :], xres[:, b, :], bc[BC_B], ALU.add).then_inc(out_ready, 1)

        @block.tensor
        def _(pe):
            t = nc.tensor
            piece = [0]

            def start_job(name):
                n = JOB_AT[name]
                if n >= NPAIR:
                    await_taken(pe, (JOBS[n - NPAIR][0], JOBS[n - NPAIR][1]))
                return bank(name)

            def stream(name, step):
                out_ = start_job(name)
                for q in range(NPIECE):
                    n = piece[0]
                    pe.wait_ge(piece_landed[n % RING], 16 * (n // RING + 1))
                    for kk in range(PIECE_K):
                        last = step(out_, q * PIECE_K + kk, ring[:, n % RING, kk, :])
                    last.then_inc(psum_full if q == NPIECE - 1 else pieces_used, 1)
                    piece[0] += 1

            def vector_step(out_, k, w):
                for j in range(4):
                    last = t.matmul(out_[:, j:j + 1], w[:, j * P:(j + 1) * P], sT[:, k:k + 1],
                                    start=(k == 0 and j == 0), stop=(k == KT - 1), skip_group_check=True)
                return last

            def token_step(act_T):
                def step(out_, k, w):
                    for b in range(TB):
                        last = t.matmul(out_[:, b * CW:(b + 1) * CW], act_T[:, k, b * P:(b + 1) * P], w,
                                        start=(k == 0), stop=(k == KT - 1))
                    return last
                return step

            def channel_step(out_, k, w):
                for j in range(4):
                    last = t.matmul(out_[:, j * SEQ:(j + 1) * SEQ], w[:, j * P:(j + 1) * P], uT[:, k, :],
                                    start=(k == 0 and j % 2 == 0), stop=(k == KT - 1), skip_group_check=True)
                return last

            def transposes(name, tiles, rows=P):
                out_ = start_job(name)
                for j, tile_ in enumerate(tiles):
                    n = tile_.shape[0]
                    last = t.transpose(out_[:, j * P:j * P + n], tile_, ident[0:n, 0:n])
                last.then_inc(psum_full, 1)

            def token_transposes(name, col, i):
                transposes(name, [tok[:, b, col + (4 * i + j) * P:col + (4 * i + j + 1) * P]
                                  for j in range(4) for b in range(TB)])

            pe.wait_ge(consts_ready, 1 + NF + 1)
            pe.wait_ge(params_landed, 16 * 7)
            transposes(("par", 0), [paramA[0:112, :]])
            transposes(("par", 1), [paramB[0:64, :]])
            for i in range(4):
                b, half = i // 2, i % 2
                pe.wait_ge(z_ready, b + 1)
                transposes(("zt", i), [z[:, b, (8 * half + k) * P:(8 * half + k + 1) * P] for k in range(8)])
            pe.wait_ge(sT_ready, 1)
            for g in (SH1, SC1):
                for cc in range(4):
                    stream(("ada", (g, cc)), vector_step)

            pe.wait_ge(zt_scaled, KT)
            pe.wait_ge(tail_landed, 16)
            out_ = start_job(("kiwi", 0))
            for b in range(TB):
                for k in range(KT):
                    last = t.matmul(out_[:, b * CW:b * CW + 80], uT[:, k, b * P:(b + 1) * P], w_tail[:, k, :],
                                    start=(k == 0), stop=(k == KT - 1))
            last.then_inc(psum_full, 1)
            stream(("qi", 0), token_step(uT))
            stream(("qi", 1), token_step(uT))
            stream(("q", 0), token_step(uT))
            pe.wait_ge(kd_ready, 2)
            transposes(("kit", 0), [kd[:, b, :] for b in range(TB)])
            pe.wait_ge(qi_roped, 1)
            token_transposes(("qit", 0), T_QI, 0)
            token_transposes(("qit", 1), T_QI, 1)
            stream(("q", 1), token_step(uT))
            await_taken(pe, ("kit", 0))
            await_taken(pe, ("qit", 1))
            for i, (b, h0, n, keys) in enumerate(LG_UNITS):
                out_ = start_job(("lg", i))
                for j in range(n):
                    h = h0 + j
                    p0 = ID * (h % 2)
                    o = lg_col(j, n, keys)
                    last = t.matmul(out_[:, o:o + keys], qiT[p0:p0 + ID, h // 2, b * P:(b + 1) * P],
                                    kdT[p0:p0 + ID, 0:keys], start=True, stop=True)
                last.then_inc(psum_full, 1)
            for kind in ("k", "v"):
                for cc in range(2):
                    stream((kind, cc), token_step(uT))
            pe.wait_ge(qk_roped, 1)
            for kind, col in (("qt", T_Q), ("kt", T_K)):
                for i in range(2):
                    token_transposes((kind, i), col, i)

            def attention_logits(u):
                b, h0, n, keys = UNITS[u]
                out_ = start_job(("at", u))
                await_taken(pe, ("kt", 1))
                for j in range(n):
                    last = t.matmul(out_[:, j * keys:(j + 1) * keys], qT[:, h0 + j, b * P:(b + 1) * P],
                                    kT[:, h0 + j, 0:keys], start=True, stop=True)
                last.then_inc(psum_full, 1)

            def attend(u):
                b, h0, n, keys = UNITS[u]
                pe.wait_ge(prob_ready, u + 1)
                transposes(("pt", u), [sm[:, u % 2, j * P:(j + 1) * P] for j in range(8)])
                out_ = start_job(("pv", u))
                await_taken(pe, ("pt", u))
                for j in range(n):
                    for i in range(keys // P):
                        last = t.matmul(out_[:, j * P:(j + 1) * P],
                                        tok[:, i, T_V + (h0 + j) * HD:T_V + (h0 + j + 1) * HD],
                                        PT[:, u % 2, j * keys + i * P:j * keys + (i + 1) * P],
                                        start=(i == 0), stop=(i == keys // P - 1))
                last.then_inc(psum_full, 1)

            stream(("xl", 0), channel_step)
            attention_logits(0)
            stream(("xl", 1), channel_step)
            attention_logits(1)
            attend(0)
            stream(("gl", 0), channel_step)
            attention_logits(2)
            attend(1)
            stream(("gl", 1), channel_step)
            attend(2)
            pe.wait_ge(gates_landed, 32)
            for i in range(4):
                out_ = start_job(("gate", i))
                pe.wait_ge(xc_ready, 2 * i + 2)
                for j in range(2):
                    for w in range(2):
                        o = (2 * j + w) * SEQ
                        last = t.matmul(out_[:, o:o + SEQ], gate_w[:, w, 2 * i + j, :], xc[:, 2 * i + j, :],
                                        start=True, stop=True)
                last.then_inc(psum_full, 1)
            for g in (GT1, SC2, SH2):
                for cc in range(4):
                    stream(("ada", (g, cc)), vector_step)

            def broadcast(vec):
                for i in range(2):
                    out_ = start_job(("bc", (vec, i)))
                    pe.wait_ge(diag_built, BC_SEEN.index((vec, i)) + 1)
                    for u in range(2):
                        last = t.matmul(out_[:, u * 512:(u + 1) * 512], ones[:, :],
                                        diag[:, u].rearrange("p k n -> p (k n)"), start=True, stop=True)
                    last.then_inc(psum_full, 1)

            broadcast(GT1)
            pe.wait_ge(lru_done, 1)
            await_taken(pe, ("pv", 2))
            for cc in range(4):
                stream(("wo", cc), token_step(concatT))
            broadcast(SC2)
            broadcast(SH2)
            pe.wait_ge(subkeys_landed, 16)
            for i in range(2):
                transposes(("skt", i), [keyscore[:, (8 * i + j) * P:(8 * i + j + 1) * P] for j in range(8)])
            for cc in range(4):
                stream(("ada", (GT2, cc)), vector_step)
            for i in range(4):
                b, half = i // 2, i % 2
                pe.wait_ge(u2_ready, b + 1)
                transposes(("ut", i), [u2[:, b, (8 * half + k) * P:(8 * half + k + 1) * P] for k in range(8)])
            await_taken(pe, ("ut", 3))
            for cc in range(4):
                stream(("pq", cc), channel_step)
            await_taken(pe, ("pq", 3))
            for i in range(4):
                out_ = start_job(("sc", i))
                b, half = i // 2, i % 2
                for j in range(8):
                    last = t.matmul(out_[:, j * P:(j + 1) * P], qpT[:, 8 * half + j, b * P:(b + 1) * P],
                                    subkT[:, 8 * half + j, :], start=True, stop=True)
                last.then_inc(psum_full, 1)
            broadcast(GT2)

            await_taken(pe, ("bc", (GT2, 1)))
            await_taken(pe, ("ada", (GT2, 3)))
            pe.wait_ge(peer_zeros, 2)
            for b in range(TB):
                y = ps[:, 2 * b:2 * b + 2, :].rearrange("p a n -> p (a n)")
                for j in range(4):
                    last = t.matmul(y[:, j * 512:(j + 1) * 512], ones[:, :], zeros, start=True, stop=False,
                                    skip_group_check=True)
                if b == 0:
                    last.then_inc(v_started, PK)
                with pe.Fori(0, PH // 2) as r:
                    for par in range(2):
                        it = r * 2 + (PH * b + par)
                        for k in range(PK):
                            pe.wait_ge(diag_ready, it * PK + (k + 1))
                            pe.wait_ge(row_landed[k % NGR], it * 64 + (32 + 16 * (k // NGR + 1)))
                            for j in range(4):
                                last = t.matmul(y[:, j * 512:(j + 1) * 512], diag[:, k // 4 % 2, k % 4, :],
                                                gathered[:, k % NGR, j * 512:(j + 1) * 512], start=False,
                                                stop=False, skip_group_check=True)
                                if j == 0:
                                    last.then_inc(v_started, 1)
                            last.then_inc(slot_free[k % NGR], 1)
                t.matmul(y[:, 0:512], ones[:, :], zeros, start=False, stop=True,
                         skip_group_check=True).then_inc(y_ready, 1)


_INS = ["x", "c", "positions", "w_ada", "b_ada", "w_in", "conv_w", "conv_b", "w_rg_a", "b_rg_a", "w_rg_x", "b_rg_x",
        "lru_lambda", "k_idx_g", "w_out", "ln1_g", "ln1_b", "w_pq", "peer_sub_keys", "peer_u", "peer_v", "ln2_g",
        "ln2_b"]


def kernel(**inputs):
    import concourse.bacc as _bacc
    from concourse.bass_utils import run_bass_kernel_spmd as _run

    nc = _bacc.Bacc("TRN2", target_bir_lowering=False, num_devices=1)
    arrays, args = {}, []
    for name in _INS:
        a = np.ascontiguousarray(inputs[name])
        arrays[f"in_{name}_dram"] = a
        args.append(nc.dram_tensor(f"in_{name}_dram", a.shape, mybir.dt.from_np(a.dtype), kind="ExternalInput").ap())
    args.append(nc.dram_tensor("out_dram", (1, SEQ, D), F32, kind="ExternalOutput").ap())
    build_layer(nc, *args)
    r = _run(nc, [arrays], core_ids=[0])
    return r.results[0]["out_dram"]
```

```python
from contextlib import ExitStack

import numpy as np
import concourse.bass as bass
from concourse import mybir

ALU = mybir.AluOpType
ACT = mybir.ActivationFunctionType
AX = mybir.AxisListType
F32 = mybir.dt.float32
I32 = mybir.dt.int32
U32 = mybir.dt.uint32

P = 128
SEQ = 256
TB = SEQ // P
D = 2048
KT = D // P
D_LRU = 1024
NLT = D_LRU // P
CONV_W = 4
NH, HD = 8, 128
NI, ID = 16, 64
CHUNK = 64
TOPK = 64
D_IN = 2 * D_LRU + 3 * NH * HD + NI * ID + ID + NI
COL_Q, COL_QI, COL_KI = 2 * D_LRU, 2 * D_LRU + 3 * NH * HD, 2 * D_LRU + 3 * NH * HD + NI * ID
NT = D_IN - COL_Q
T_Q, T_K, T_V, T_QI, T_KI, T_WI = 0, 1024, 2048, 3072, 4096, 4160
PH, NK, PK = 8, 128, 16
EPS = 1e-5
ALPHA = 2.0 ** 0.25
ROPE_THETA = 500000.0
RA, RI = 16, 8
NF = RA + RI
NEG = -1.0e30
TAKEN = -3.0e38

PIECE_K = 4
NPIECE = KT // PIECE_K
CW = 512
RING = 3
ARING = 4
NGR = 8
NPAIR = 4
LO, HI = 0, 1

SH1, SC1, GT1, SH2, SC2, GT2 = range(6)

CHUNKS = [(w, c) for w, n in (("qi", 2), ("xl", 2), ("gl", 2), ("q", 2), ("k", 2), ("v", 2), ("wo", 4), ("pq", 4))
          for c in range(n)]
ADA = [(g, half) for g in (SH1, SC1, GT1, SC2, SH2, GT2) for half in range(2)]

JOBS = [("par", 0, "dve"), ("par", 1, "dve")]
JOBS += [("zt", i, "act") for i in range(4)]
JOBS += [("ada", i, "dve") for i in range(4)]
JOBS += [("kiwi", 0, "act"), ("qi", 0, "act"), ("qi", 1, "act"), ("xl", 0, "act")]
JOBS += [("kit", 0, "dve"), ("qit", 0, "act"), ("qit", 1, "act"), ("xl", 1, "act")]
JOBS += [("lg", i, "act") for i in range(6)]
JOBS += [("gl", 0, "act"), ("gl", 1, "act")] + [("gate", i, "act") for i in range(4)]
JOBS += [("q", 0, "act"), ("ada", 4, "dve"), ("ada", 5, "dve"), ("q", 1, "act"), ("k", 0, "act")]
JOBS += [("ada", 6, "dve"), ("ada", 7, "dve"), ("k", 1, "act"), ("v", 0, "act"), ("ada", 8, "dve")]
JOBS += [("qt", 0, "act"), ("qt", 1, "act"), ("kt", 0, "act"), ("kt", 1, "act")]
JOBS += [("at", 0, "dve"), ("at", 1, "dve"), ("at", 2, "dve"), ("v", 1, "act"), ("ada", 9, "dve")]
JOBS += [("pt", 0, "act"), ("pt", 1, "act"), ("pv", 0, "act"), ("pt", 2, "act"), ("pv", 1, "act"), ("pv", 2, "act")]
JOBS += [("bc", (GT1, i), "act") for i in range(2)]
JOBS += [("wo", 0, "dve"), ("ada", 10, "dve"), ("bc", (SC2, 0), "act"), ("bc", (SC2, 1), "act")]
JOBS += [("wo", 1, "dve"), ("ada", 11, "dve"), ("bc", (SH2, 0), "act"), ("bc", (SH2, 1), "act")]
JOBS += [("wo", 2, "dve"), ("wo", 3, "dve"), ("bc", (GT2, 0), "act"), ("bc", (GT2, 1), "act")]
JOBS += [("skt", 0, "act"), ("skt", 1, "act")]
JOBS += [("ut", i, "act") for i in range(4)]
JOBS += [("pq", 0, "act"), ("sc", 0, "act")]
for _c in range(1, 4):
    JOBS += [("pq", _c, "act"), ("sc", _c, "act")]
JOB_AT = {(kind, i): n for n, (kind, i, _) in enumerate(JOBS)}
JOB_ENG = [e for _, _, e in JOBS]
BC_SEEN = [i for k, i, _ in JOBS if k == "bc"]

PAR_C, PAR_BADA = 0, KT
PAR_CW, PAR_CB, PAR_BA, PAR_BX, PAR_LAM = 112, 144, 152, 160, 168
NPAR = 176
UNITS = [(0, 0, 8, P), (1, 0, 4, SEQ), (1, 4, 4, SEQ)]
LG_UNITS = [(0, 0, 8, P), (0, 8, 8, P)] + [(1, 4 * i, 4, SEQ) for i in range(4)]


class Steps:

    def __init__(self, eng, sem):
        self.eng, self.sem, self.n = eng, sem, 0

    def mark(self, ins):
        ins.then_inc(self.sem, 1)
        self.n += 1

    def settle(self):
        self.eng.wait_ge(self.sem, self.n)

    def restart(self):
        self.settle()
        self.eng.sem_clear(self.sem)
        self.n = 0

    def seq(self, ins):
        self.mark(ins)
        self.settle()


def lg_col(j, n, keys):
    return ((j % 2) * (n // 2) + j // 2) * keys


def take(eng, sem):
    eng.wait_ge(sem, 1)
    eng.sem_clear(sem)


def build_layer(nc, x, c, positions, w_ada, b_ada, w_in, conv_w, conv_b, w_rg_a, b_rg_a, w_rg_x, b_rg_x,
                lru_lambda, k_idx_g, w_out, ln1_g, ln1_b, w_pq, peer_sub_keys, peer_u, peer_v, ln2_g, ln2_b, out):
    ctx = ExitStack()
    with ctx:
        def sb(name, shape, dt=F32):
            return ctx.enter_context(nc.sbuf_tensor(name, shape, dt))

        def sem(name):
            return ctx.enter_context(nc.semaphore(name))

        arena = sb("arena", [P, 64 * 256])
        ring = arena[:, 0:RING * PIECE_K * CW].rearrange("p (s k n) -> p s k n", s=RING, k=PIECE_K)
        A0 = RING * PIECE_K * CW
        A1 = A0 + ARING * PIECE_K * CW
        aring = arena[:, A0:A1].rearrange("p (s k n) -> p s k n", s=ARING, k=PIECE_K)
        partial = arena[:, A1:A1 + 4 * CW].rearrange("p (a c n) -> p a c n", a=2, c=2)
        gathered = arena[:, :].rearrange("p (s d) -> p s d", s=NGR)
        xres = sb("xres", [P, TB, D])
        uT = sb("uT", [P, KT, SEQ])
        tokbuf = sb("tokbuf", [P, TB * NT])
        tok = tokbuf[:, 0:TB * NT].rearrange("p (b n) -> p b n", b=TB)
        z = tokbuf[:, 0:TB * D].rearrange("p (b d) -> p b d", b=TB)
        keyscore = tokbuf[:, 0:TB * D]
        u2 = tokbuf[:, TB * D:2 * TB * D].rearrange("p (b d) -> p b d", b=TB)
        lru = sb("lru", [P, 5 * D + 32])
        work = [lru[:, 32 + i * D:32 + (i + 1) * D] for i in range(5)]
        xlp = lru[:, 0:NLT * (SEQ + 3)].rearrange("p (n t) -> p n t", n=NLT)
        xc, rg, ig, th = (w.rearrange("p (n t) -> p n t", n=NLT) for w in work[1:5])
        w_tail = work[3][:, 0:KT * 80].rearrange("p (k n) -> p k n", k=KT)
        PT = work[2].rearrange("p (u n) -> p u n", u=2)
        qT, kT = (w.rearrange("p (h t) -> p h t", h=NH) for w in work[3:5])
        qpT = lru[:, 32:32 + 2 * D].rearrange("p (h t) -> p h t", h=2 * PH)
        gate_w = work[4].rearrange("p (w n e) -> p w n e", w=2, n=NLT)
        BC_GT1, BC_G, BC_B, BC_SC2, BC_SH2 = range(5)
        BC_GT2 = 5
        concatT = sb("concatT", [P, KT, SEQ])
        qiT = concatT[:, NLT:KT, :]
        bc = work + [concatT[:, NLT:KT, :].rearrange("p n t -> p (n t)")]
        subkT = concatT[:, 0:NLT, :].rearrange("p n (a t) -> p (n a) t", a=2)
        sm = sb("sm", [P, 2, 1024])
        small = sb("small", [P, 1024])
        score = small[:, 0:TB * SEQ].rearrange("p (b s) -> p b s", b=TB)
        kdT = small[:, 512:768]
        kd = small[:, 768:1024].rearrange("p (b n) -> p b n", b=TB)
        cand = small[:, 0:256].rearrange("p (a c) -> p a c", a=PK)
        onehot = small[:, 256:512].rearrange("p (a c) -> p a c", a=PK)
        stage = small[:, 512:768].rearrange("p (a n) -> p a n", a=2)
        ident = sb("ident", [P, P])
        ones = sb("ones", [P, P])
        diag = sm[:, :, 512:1024].rearrange("p u (k n) -> p u k n", k=4)
        zeros = sm[:, 0, 0:512]
        paramA, paramB = sm[:, 0, 0:P], sm[:, 1, 0:P]
        parT = sb("parT", [P, NPAR])
        sT = sb("sT", [P, KT])
        mod = sb("mod", [P, 6 * KT])
        pos_i = sb("pos_i", [P, TB], I32)
        posf = sb("posf", [P, TB])
        freq = sb("freq", [P, NF])
        ang = sb("ang", [P, TB, NF])
        ang2 = sb("ang2", [P, TB, NF])
        sin = sb("sin", [P, TB, NF])
        cos = sb("cos", [P, TB, NF])
        kig = sb("kig", [P, ID])
        st = sb("st", [P, 4, 6])
        st2 = sb("st2", [P, TB, 4, 6])
        mv = sb("mv", [P, TB, 2])
        rstd = sb("rstd", [P, TB])
        m8 = sb("m8", [P, 8])
        amax = sb("amax", [P, 24])
        asum = sb("asum", [P, 24])
        sp = sb("sp", [P, 6, NLT])
        nsp8 = sb("nsp8", [P, NLT])
        psp8 = sb("psp8", [P, NLT])
        iota_i = sb("iota_i", [P, PK], I32)
        iota = sb("iota", [P, PK])
        topv = sb("topv", [P, 2, PK])
        topi = sb("topi", [P, 2, PK], U32)
        topf = sb("topf", [P, 2, PK])
        tops = sb("tops", [P, 2, PK])
        pick = sb("pick", [P, PK], U32)
        pick2 = sb("pick2", [P, 2, PK], U32)
        pickf = sb("pickf", [P, 2, PK])
        esel = sb("esel", [P, 2, PK])
        eidx = sb("eidx", [P, 2, PK], U32)
        ntop = sb("ntop", [P, 2])
        gexp = sb("gexp", [P, 2, PK])
        gsum = sb("gsum", [P, 2])
        dots = sb("dots", [P, 2, PK])
        gel = sb("gel", [P, 2, PK])
        hk = sb("hk", [P, 2, PK])
        ropet = sm[:, :, :].rearrange("p u n -> p (u n)")
        ps = ctx.enter_context(nc.psum_tensor("ps", [P, NPAIR, 1024], F32))

        def scores_of(u):
            return sm[:, u, :] if u < 2 else work[1][:, 0:1024]

        piece_landed = [sem(f"piece_landed{i}") for i in range(RING)]
        pieces_used = sem("pieces_used")
        ada_landed = [sem(f"ada_landed{i}") for i in range(ARING)]
        ada_summed = sem("ada_summed")
        c_landed = sem("c_landed")
        psum_full = sem("psum_full")
        psum_freed = {"act": sem("psum_freed_by_act"), "dve": sem("psum_freed_by_dve")}
        x_landed = [sem(f"x_landed{i}") for i in range(TB)]
        params_landed = sem("params_landed")
        small_landed = sem("small_landed")
        tail_landed = sem("tail_landed")
        gates_landed = sem("gates_landed")
        subkeys_landed = sem("subkeys_landed")
        ln1_landed = sem("ln1_landed")
        ln2_landed = sem("ln2_landed")
        out_landed = sem("out_landed")
        consts_ready = sem("consts_ready")
        pool_step = sem("pool_step")
        dve_step = sem("dve_step")
        act_step = sem("act_step")
        var_ready = sem("var_ready")
        std_ready = sem("std_ready")
        z_ready = sem("z_ready")
        zt_scaled = sem("zt_scaled")
        sT_ready = sem("sT_ready")
        lam_exp = sem("lam_exp")
        ang_ready = sem("ang_ready")
        sincos_ready = sem("sincos_ready")
        qi_roped = sem("qi_roped")
        kd_ready = sem("kd_ready")
        relu_used = sem("relu_used")
        qk_roped = sem("qk_roped")
        scored_ready = sem("scored_ready")
        exp_ready = sem("exp_ready")
        prob_ready = sem("prob_ready")
        xc_ready = sem("xc_ready")
        decay_ready = sem("decay_ready")
        pow_ready = sem("pow_ready")
        sqrt_ready = sem("sqrt_ready")
        lru_done = sem("lru_done")
        diag_built = sem("diag_built")
        z2_ready = sem("z2_ready")
        u2_ready = sem("u2_ready")
        peer_zeros = sem("peer_zeros")
        stage_ready = sem("stage_ready")
        idx_ready = sem("idx_ready")
        top_ready = sem("top_ready")
        gexp_ready = sem("gexp_ready")
        dots_done = sem("dots_done")
        gel_ready = sem("gel_ready")
        hk_ready = sem("hk_ready")
        diag_ready = sem("diag_ready")
        row_landed = [sem(f"row_landed{i}") for i in range(NGR)]
        slot_free = [sem(f"slot_free{i}") for i in range(NGR)]
        v_started = sem("v_started")
        y_ready = sem("y_ready")
        out_ready = sem("out_ready")

        SRC = {"qi": (w_in, COL_QI), "q": (w_in, COL_Q), "k": (w_in, COL_Q + 1024), "v": (w_in, COL_Q + 2048),
               "xl": (w_in, 0), "gl": (w_in, D_LRU), "wo": (w_out, 0), "pq": (w_pq, 0)}
        u_rows = peer_u[0]
        v_rows = peer_v[0]

        def bank(name):
            return ps[:, JOB_AT[name] % NPAIR, :]

        def await_job(eng, name):
            eng.wait_ge(psum_full, JOB_AT[name] + 1)

        def await_taken(eng, name):
            n = JOB_AT[name]
            eng.wait_ge(psum_freed[JOB_ENG[n]], JOB_ENG[0:n + 1].count(JOB_ENG[n]))

        block = ctx.enter_context(nc.Block())

        @block.sync
        def _(sp_):
            for b in range(TB):
                sp_.dma_start(xres[:, b, :], x[0, b * P:(b + 1) * P, :]).then_inc(x_landed[b], 16)
            n = 0
            for kind, col in CHUNKS:
                w, c0 = SRC[kind]
                for q in range(NPIECE):
                    old = n - RING
                    if old >= 0 and old % NPIECE == NPIECE - 1:
                        await_job(sp_, CHUNKS[old // NPIECE])
                    elif old >= 0:
                        sp_.wait_ge(pieces_used, old - old // NPIECE + 1)
                    src = w[0, q * PIECE_K * P:(q + 1) * PIECE_K * P, c0 + col * CW:c0 + (col + 1) * CW]
                    sp_.dma_start(ring[:, n % RING], src.rearrange("(k p) n -> p k n", p=P)).then_inc(
                        piece_landed[n % RING], 16)
                    n += 1
            for b in range(TB):
                sp_.wait_ge(out_ready, b + 1)
                sp_.dma_start(out[0, b * P:(b + 1) * P, :], xres[:, b, :]).then_inc(out_landed, 16)
            sp_.wait_ge(out_landed, 16 * TB)

        @block.gpsimd
        def _(pool):
            g = nc.gpsimd

            def load_ada(n):
                if n >= ARING:
                    pool.wait_ge(ada_summed, n - ARING + 1)
                (grp, half), cc, q = ADA[n // 8], n // 4 % 2, n % 4
                c0 = grp * D + (2 * half + cc) * CW
                src = w_ada[0, q * PIECE_K * P:(q + 1) * PIECE_K * P, c0:c0 + CW]
                g.dma_start(aring[:, n % ARING], src.rearrange("(k p) n -> p k n", p=P)).then_inc(
                    ada_landed[n % ARING], 16)

            for n in range(ARING):
                load_ada(n)
            steps = Steps(pool, pool_step)
            steps.mark(g.memset(ident[:, :], 0.0))
            g.memset(ones[:, :], 1.0).then_inc(consts_ready, 1)
            for j in range(RA):
                f = float(np.float32(ROPE_THETA) ** (-np.float32(j) / np.float32(RA)))
                g.memset(freq[:, j:j + 1], f).then_inc(consts_ready, 1)
            for j in range(RI):
                f = float(np.float32(ROPE_THETA) ** (-np.float32(j) / np.float32(RI)))
                g.memset(freq[:, RA + j:RA + j + 1], f).then_inc(consts_ready, 1)
            steps.settle()
            g.affine_select(out=ident[:, :], in_=ident[:, :], compare_op=ALU.not_equal, fill=1.0, base=0,
                            pattern=[[-1, P]], channel_multiplier=1).then_inc(consts_ready, 1)
            g.iota(iota_i[:, :], pattern=[[1, PK]], base=0, channel_multiplier=0).then_inc(consts_ready, 1)

            for n in range(ARING, 8 * len(ADA)):
                load_ada(n)

            await_job(pool, ("pq", 3))
            await_job(pool, ("ada", 11))
            for slot in slot_free:
                pool.sem_inc(slot, 1)
            for b in range(TB):
                with pool.Fori(0, PH // 2) as r:
                    for par in range(2):
                        take(pool, idx_ready)
                        for use in range(4):
                            for s in range(NGR):
                                k = (use % 2) * NGR + s
                                take(pool, slot_free[s])
                                rows = u_rows if use < 2 else v_rows
                                g.indirect_dma_start(
                                    out=gathered[:, s, :], out_offset=None, in_=rows,
                                    in_offset=bass.IndirectOffsetOnAxis(ap=eidx[:, par, k:k + 1], axis=0),
                                ).then_inc(row_landed[s], 16)

        @block.scalar
        def _(act):
            s = nc.scalar
            steps = Steps(act, act_step)

            def free(ins):
                ins.then_inc(psum_freed["act"], 1)

            def row(v, n):
                return v.rearrange("l (r p) -> (l r) p", p=P)[0:n]

            act.dma_start(paramA[PAR_C:PAR_C + KT, :], c.rearrange("l (r p) -> (l r) p", p=P)).then_inc(c_landed, 16)
            act.dma_start(paramA[PAR_BADA:PAR_BADA + 96, :], row(b_ada, 96)).then_inc(c_landed, 16)
            act.dma_start(paramB[0:32, :], conv_w[0].rearrange("j (n p) -> (j n) p", p=P)).then_inc(params_landed, 16)
            for i, v in enumerate((conv_b, b_rg_a, b_rg_x, lru_lambda)):
                act.dma_start(paramB[32 + 8 * i:40 + 8 * i, :], row(v, 8)).then_inc(params_landed, 16)
            for b in range(TB):
                act.dma_start(pos_i[:, b:b + 1], positions[0, b * P:(b + 1) * P].unsqueeze(1)).then_inc(small_landed, 16)
            act.dma_start(kig[:, :], k_idx_g[0].partition_broadcast(P)).then_inc(small_landed, 16)
            act.dma_start(w_tail, w_in[0, :, COL_KI:D_IN].rearrange("(k p) n -> p k n", p=P)).then_inc(tail_landed, 16)
            act.dma_start(gate_w[:, 0], w_rg_a[0].rearrange("n d e -> d n e")).then_inc(gates_landed, 16)
            act.dma_start(gate_w[:, 1], w_rg_x[0].rearrange("n d e -> d n e")).then_inc(gates_landed, 16)

            await_taken(act, ("par", 0))
            s.activation(sT[:, :], parT[:, PAR_C:PAR_C + KT], ACT.Silu).then_inc(sT_ready, 1)
            for b in range(TB):
                act.wait_ge(var_ready, b + 1)
                s.activation(rstd[:, b:b + 1], rstd[:, b:b + 1], ACT.Sqrt).then_inc(std_ready, 1)
            for i in range(4):
                b, half = i // 2, i % 2
                await_job(act, ("zt", i))
                free(s.copy(uT[:, 8 * half:8 * half + 8, b * P:(b + 1) * P],
                            bank(("zt", i)).rearrange("p (k t) -> p k t", k=8)))
            act.wait_ge(ang_ready, 1)
            s.activation(sin[:, :, :], ang[:, :, :], ACT.Sin).then_inc(sincos_ready, 1)
            s.activation(cos[:, :, :], ang2[:, :, :], ACT.Sin).then_inc(sincos_ready, 1)
            act.wait_ge(lam_exp, 1)
            s.activation(sp[:, 1, :], sp[:, 0, :], ACT.Exp).then_inc(lam_exp, 1)

            await_job(act, ("kiwi", 0))
            free(s.copy(tok[:, :, T_KI:NT],
                        bank(("kiwi", 0)).rearrange("p (b n) -> p b n", b=TB)[:, :, 0:80]))

            def keep(kind, cc, at):
                await_job(act, (kind, cc))
                free(s.copy(tok[:, :, at + cc * CW:at + (cc + 1) * CW],
                            bank((kind, cc)).rearrange("p (b n) -> p b n", b=TB)))

            for b in range(TB):
                act.wait_ge(var_ready, TB + b + 1)
                s.activation(rstd[:, b:b + 1], rstd[:, b:b + 1], ACT.Sqrt).then_inc(std_ready, 1)
            keep("qi", 0, T_QI)
            keep("qi", 1, T_QI)

            def keep_xl(i):
                await_job(act, ("xl", i))
                free(s.copy(xlp[:, 4 * i:4 * i + 4, 3:3 + SEQ], bank(("xl", i)).rearrange("p (n t) -> p n t", n=4)))

            def keep_gl(i):
                await_job(act, ("gl", i))
                free(s.activation(concatT[:, 4 * i:4 * i + 4, :], bank(("gl", i)).rearrange("p (n t) -> p n t", n=4),
                                  ACT.Gelu_apprx_tanh))

            keep_xl(0)
            for i in range(2):
                await_job(act, ("qit", i))
                free(s.copy(qiT[:, 4 * i:4 * i + 4, :], bank(("qit", i)).rearrange("p (h t) -> p h t", h=4)))
            keep_xl(1)
            for i, (b, h0, n, keys) in enumerate(LG_UNITS):
                await_job(act, ("lg", i))
                if i >= 2:
                    act.wait_ge(relu_used, i - 1)
                free(s.activation(sm[:, i % 2, :], bank(("lg", i)), ACT.Relu, scale=ID ** -0.5))
            keep_gl(0)
            keep_gl(1)
            for i in range(4):
                await_job(act, ("gate", i))
                pb = bank(("gate", i)).rearrange("p (n g t) -> p n g t", n=2, g=2)
                for j in range(2):
                    n = 2 * i + j
                    steps.mark(s.activation(rg[:, n], pb[:, j, 0], ACT.Sigmoid, bias=parT[:, PAR_BA + n:PAR_BA + n + 1]))
                    ins = s.activation(ig[:, n], pb[:, j, 1], ACT.Sigmoid, bias=parT[:, PAR_BX + n:PAR_BX + n + 1])
                free(ins)
            steps.settle()
            for n in range(NLT):
                steps.mark(s.activation(th[:, n], rg[:, n], ACT.Tanh, scale=psp8[:, n:n + 1]))
            for n in range(NLT):
                s.activation(rg[:, n], rg[:, n], ACT.Exp, scale=nsp8[:, n:n + 1]).then_inc(decay_ready, 1)
            act.wait_ge(pow_ready, 1)
            s.activation(th[:, :, :], th[:, :, :], ACT.Sqrt).then_inc(sqrt_ready, 1)

            def broadcast_out(vec, slot):
                for i in range(2):
                    await_job(act, ("bc", (vec, i)))
                    free(s.copy(bc[slot][:, 1024 * i:1024 * (i + 1)], bank(("bc", (vec, i)))))

            keep("q", 0, T_Q)
            keep("q", 1, T_Q)
            keep("k", 0, T_K)
            keep("k", 1, T_K)
            keep("v", 0, T_V)
            act.wait_ge(lru_done, 1)
            for i in range(2):
                await_job(act, ("qt", i))
                free(s.copy(qT[:, 4 * i:4 * i + 4, :], bank(("qt", i)).rearrange("p (h t) -> p h t", h=4)))
            for i in range(2):
                await_job(act, ("kt", i))
                free(s.copy(kT[:, 4 * i:4 * i + 4, :], bank(("kt", i)).rearrange("p (h t) -> p h t", h=4)))

            def exps(u):
                b, h0, n, keys = UNITS[u]
                act.wait_ge(scored_ready, u + 1)
                for h in range(n):
                    sl = scores_of(u)[:, h * keys:(h + 1) * keys]
                    s.activation(sl, sl, ACT.Exp, bias=amax[:, 8 * u + h:8 * u + h + 1],
                                 accum_out=asum[:, 8 * u + h:8 * u + h + 1]).then_inc(exp_ready, 1)

            def keep_p(u):
                await_job(act, ("pt", u))
                free(s.copy(PT[:, u % 2, :], bank(("pt", u))))

            def keep_y(u):
                b, h0, n, keys = UNITS[u]
                await_job(act, ("pv", u))
                free(s.copy(concatT[:, NLT + h0:NLT + h0 + n, b * P:(b + 1) * P],
                            bank(("pv", u))[:, 0:n * P].rearrange("p (h t) -> p h t", h=n)))

            for u in range(len(UNITS)):
                exps(u)
            keep("v", 1, T_V)
            keep_p(0)
            keep_p(1)
            keep_y(0)
            keep_p(2)
            keep_y(1)
            keep_y(2)

            def broadcast_out(vec, slot):
                for i in range(2):
                    await_job(act, ("bc", (vec, i)))
                    free(s.copy(bc[slot][:, 1024 * i:1024 * (i + 1)], bank(("bc", (vec, i)))))

            act.dma_start(bc[BC_G], ln1_g[0].partition_broadcast(P)).then_inc(ln1_landed, 16)
            act.dma_start(bc[BC_B], ln1_b[0].partition_broadcast(P)).then_inc(ln1_landed, 16)
            act.dma_start(keyscore[:, 0:2 * PH * P].rearrange("p (h d) -> p h d", h=2 * PH),
                          peer_sub_keys[0].rearrange("h a n d -> n (h a) d")).then_inc(subkeys_landed, 16)
            broadcast_out(GT1, BC_GT1)
            broadcast_out(SC2, BC_SC2)
            broadcast_out(SH2, BC_SH2)
            broadcast_out(GT2, BC_GT2)
            for i in range(2):
                await_job(act, ("skt", i))
                free(s.copy(subkT[:, 8 * i:8 * i + 8, :], bank(("skt", i)).rearrange("p (n t) -> p n t", n=8)))
            for b in range(TB):
                for i in range(2):
                    act.wait_ge(var_ready, 2 * TB + 2 * b + i + 1)
                    s.activation(rstd[:, b:b + 1], rstd[:, b:b + 1], ACT.Sqrt).then_inc(std_ready, 1)
            for i in range(4):
                b, half = i // 2, i % 2
                await_job(act, ("ut", i))
                for j in range(8):
                    k = 8 * half + j
                    ins = s.activation(uT[:, k, b * P:(b + 1) * P], bank(("ut", i))[:, j * P:(j + 1) * P], ACT.Identity,
                                       bias=mod[:, SH2 * KT + k:SH2 * KT + k + 1],
                                       scale=mod[:, SC2 * KT + k:SC2 * KT + k + 1])
                    if j < 7:
                        steps.mark(ins)
                free(ins)
            flat = stage[:, :, :].rearrange("p a n -> p (a n)")
            for i in range(4):
                await_job(act, ("pq", i))
                if i == 0:
                    act.wait_ge(z2_ready, TB)
                free(s.copy(qpT[:, 4 * i:4 * i + 4, :], bank(("pq", i)).rearrange("p (h t) -> p h t", h=4)))
                await_job(act, ("sc", i))
                free(s.copy(keyscore[:, :].rearrange("p (b n) -> p b n", b=TB)[:, :, 4 * P * i:4 * P * (i + 1)],
                            bank(("sc", i)).rearrange("p (b n) -> p b n", b=TB)))
                if i == 0:
                    await_taken(act, ("sc", 0))
                    s.copy(flat, keyscore[:, 0:256]).then_inc(stage_ready, 1)
            act.dma_start(bc[BC_G], ln2_g[0].partition_broadcast(P)).then_inc(ln2_landed, 16)
            act.dma_start(bc[BC_B], ln2_b[0].partition_broadcast(P)).then_inc(ln2_landed, 16)
            await_taken(act, ("sc", 3))
            for b in range(TB):
                with act.Fori(0, PH // 2) as r:
                    for par in range(2):
                        it = r * 2 + (PH * b + par)
                        act.wait_ge(top_ready, it + 1)
                        s.activation(gexp[:, par, :], tops[:, par, :], ACT.Exp, bias=ntop[:, par:par + 1],
                                     accum_out=gsum[:, par:par + 1]).then_inc(gexp_ready, 1)
                        s.copy(flat, tokbuf[:, bass.ds(it * 256 + 256, 256)]).then_inc(stage_ready, 1)
                        act.wait_ge(dots_done, it + 1)
                        s.activation(gel[:, par, :], dots[:, par, :], ACT.Gelu_apprx_tanh).then_inc(gel_ready, 1)
                        act.wait_ge(hk_ready, it + 1)
                        for k in range(PK):
                            act.wait_ge(v_started, it * PK + (k + PK - 8 + 2))
                            s.mul(diag[:, k // 4 % 2, k % 4, :], ident[:, :], hk[:, par, k:k + 1]).then_inc(diag_ready, 1)
            for b in range(TB):
                act.wait_ge(var_ready, 4 * TB + b + 1)
                s.activation(rstd[:, b:b + 1], rstd[:, b:b + 1], ACT.Sqrt).then_inc(std_ready, 1)

        @block.vector
        def _(dve):
            v = nc.vector
            steps = Steps(dve, dve_step)
            norms = [0]

            def free(ins):
                ins.then_inc(psum_freed["dve"], 1)

            def normalise(b, dst, src, stats=None):
                w = src.shape[-1]
                parts = max(1, w // 512)
                if stats is None:
                    stats = st
                    for i in range(parts):
                        steps.mark(v.bn_stats(st[:, i, :], src[:, i * (w // parts):(i + 1) * (w // parts)]))
                    steps.settle()
                steps.seq(v.bn_aggr(mv[:, b, :], stats[:, 0:parts, :]))
                v.tensor_scalar(rstd[:, b:b + 1], mv[:, b, 1:2], EPS, None, ALU.add).then_inc(var_ready, 1)
                norms[0] += 1
                dve.wait_ge(std_ready, norms[0])
                steps.seq(v.reciprocal(rstd[:, b:b + 1], rstd[:, b:b + 1]))
                return v.tensor_scalar(dst, src, mv[:, b, 0:1], rstd[:, b:b + 1], ALU.subtract, ALU.mult)

            for i, (c0, n) in enumerate(((0, 112), (112, 64))):
                await_job(dve, ("par", i))
                free(v.tensor_copy(parT[:, c0:c0 + n], bank(("par", i))[:, 0:n]))
            for b in range(TB):
                dve.wait_ge(x_landed[b], 16)
                normalise(b, z[:, b, :], xres[:, b, :]).then_inc(z_ready, 1)

            await_taken(dve, ("par", 1))
            TWO_PI = 2.0 * np.pi
            C1 = 6.28125
            C2 = 0.00193500518798828125
            C3 = float(TWO_PI - C1 - C2)
            ROUND = 1.5 * 2.0 ** 23
            dve.wait_ge(small_landed, 48)
            dve.wait_ge(consts_ready, 1 + NF + 2)
            steps.seq(v.tensor_copy(posf[:, :], pos_i[:, :]))
            for b in range(TB):
                steps.mark(v.tensor_scalar(ang[:, b, :], freq[:, :], posf[:, b:b + 1], None, ALU.mult))
            steps.settle()
            steps.seq(v.tensor_scalar(ang2[:, :, :], ang[:, :, :], 1.0 / TWO_PI, ROUND, ALU.mult, ALU.add))
            steps.seq(v.tensor_scalar(ang2[:, :, :], ang2[:, :, :], -ROUND, None, ALU.add))
            for part in (C1, C2, C3):
                steps.seq(v.scalar_tensor_tensor(out=ang[:, :, :], in0=ang2[:, :, :], scalar=-part, in1=ang[:, :, :],
                                                 op0=ALU.mult, op1=ALU.add))
            PI32 = float(np.nextafter(np.float32(np.pi), np.float32(0)))
            steps.seq(v.tensor_scalar(ang[:, :, :], ang[:, :, :], PI32, -PI32, ALU.min, ALU.max))
            steps.seq(v.tensor_scalar(ang2[:, :, :], ang[:, :, :], -1.0, None, ALU.mult))
            steps.seq(v.tensor_tensor(ang2[:, :, :], ang[:, :, :], ang2[:, :, :], ALU.max))
            v.tensor_scalar(ang2[:, :, :], ang2[:, :, :], -1.0, float(np.pi / 2), ALU.mult, ALU.add).then_inc(ang_ready, 1)

            steps.mark(v.tensor_copy(iota[:, :], iota_i[:, :]))
            lam = parT[:, PAR_LAM:PAR_LAM + NLT]
            steps.seq(v.tensor_scalar(sp[:, 2, :], lam, -1.0, None, ALU.mult))
            steps.seq(v.tensor_tensor(sp[:, 0, :], lam, sp[:, 2, :], ALU.min))
            v.tensor_scalar(sp[:, 2, :], sp[:, 2, :], 0.0, None, ALU.max).then_inc(lam_exp, 1)
            dve.wait_ge(lam_exp, 2)
            steps.seq(v.tensor_scalar(sp[:, 3, :], sp[:, 1, :], 2.0, None, ALU.add))
            steps.seq(v.reciprocal(sp[:, 3, :], sp[:, 3, :]))
            steps.seq(v.tensor_tensor(sp[:, 3, :], sp[:, 3, :], sp[:, 1, :], ALU.mult))
            steps.seq(v.tensor_tensor(sp[:, 4, :], sp[:, 3, :], sp[:, 3, :], ALU.mult))
            NTERM = 9
            steps.seq(v.tensor_scalar(sp[:, 5, :], sp[:, 4, :], 1.0 / (2 * NTERM + 1), 1.0 / (2 * NTERM - 1), ALU.mult, ALU.add))
            for j in range(NTERM - 1, 0, -1):
                steps.seq(v.tensor_tensor(sp[:, 5, :], sp[:, 5, :], sp[:, 4, :], ALU.mult))
                steps.seq(v.tensor_scalar(sp[:, 5, :], sp[:, 5, :], 1.0 / (2 * j - 1), None, ALU.add))
            steps.seq(v.tensor_tensor(sp[:, 5, :], sp[:, 5, :], sp[:, 3, :], ALU.mult))
            steps.seq(v.scalar_tensor_tensor(out=sp[:, 5, :], in0=sp[:, 5, :], scalar=2.0, in1=sp[:, 2, :],
                                             op0=ALU.mult, op1=ALU.add))
            steps.mark(v.tensor_scalar(nsp8[:, :], sp[:, 5, :], -8.0, None, ALU.mult))
            steps.mark(v.tensor_scalar(psp8[:, :], sp[:, 5, :], 8.0, None, ALU.mult))
            steps.mark(v.memset(xlp[:, :, 0:3], 0.0))
            steps.settle()

            def ada_sums(i):
                dve.wait_ge(sT_ready, 1)
                if i >= 2:
                    await_job(dve, ("ada", i - 2))
                for cc in range(2):
                    acc = partial[:, i % 2, cc, :]
                    for k in range(KT):
                        n = (2 * i + cc) * NPIECE + k // PIECE_K
                        w = aring[:, n % ARING, k % PIECE_K, :]
                        if k % PIECE_K == 0:
                            dve.wait_ge(ada_landed[n % ARING], 16 * (n // ARING + 1))
                        if k == 0:
                            ins = v.tensor_scalar(acc, w, sT[:, k:k + 1], None, ALU.mult)
                        else:
                            ins = v.scalar_tensor_tensor(out=acc, in0=w, scalar=sT[:, k:k + 1], in1=acc,
                                                         op0=ALU.mult, op1=ALU.add)
                        if k % PIECE_K == PIECE_K - 1:
                            ins.then_inc(ada_summed, 1)
                            dve.wait_ge(ada_summed, n + 1)
                        else:
                            steps.seq(ins)

            def ada_out(i):
                group, half = ADA[i]
                j = group * KT + 8 * half
                await_job(dve, ("ada", i))
                free(v.scalar_tensor_tensor(out=mod[:, j:j + 8], in0=bank(("ada", i))[:, 0:8],
                                            scalar=0.0 if group in (SH1, SH2) else 1.0,
                                            in1=parT[:, PAR_BADA + j:PAR_BADA + j + 8], op0=ALU.add, op1=ALU.add))
                await_taken(dve, ("ada", i))

            ada_sums(0)
            for i in range(1, 4):
                ada_sums(i)
                ada_out(i - 1)
            ada_out(3)
            await_taken(dve, ("zt", 3))
            for k in range(KT):
                v.tensor_scalar(uT[:, k, :], uT[:, k, :], mod[:, SC1 * KT + k:SC1 * KT + k + 1],
                                mod[:, SH1 * KT + k:SH1 * KT + k + 1], ALU.mult, ALU.add).then_inc(zt_scaled, 1)

            def rope(col, heads, width, half, f0):
                xs = tok[:, :, col:col + heads * width].rearrange("p b (h w) -> p b h w", h=heads)
                x1, x2 = xs[:, :, :, 0:half], xs[:, :, :, half:2 * half]
                cs = cos[:, :, f0:f0 + half].unsqueeze(2).to_broadcast([P, TB, heads, half])
                sn = sin[:, :, f0:f0 + half].unsqueeze(2).to_broadcast([P, TB, heads, half])
                n = TB * heads * half
                t = [ropet[:, i * 512:i * 512 + n].rearrange("p (b h f) -> p b h f", b=TB, h=heads) for i in range(4)]
                steps.mark(v.tensor_tensor(t[0], x1, cs, ALU.mult))
                steps.mark(v.tensor_tensor(t[1], x2, sn, ALU.mult))
                steps.mark(v.tensor_tensor(t[2], x2, cs, ALU.mult))
                steps.mark(v.tensor_tensor(t[3], x1, sn, ALU.mult))
                steps.settle()
                steps.mark(v.tensor_tensor(x1, t[0], t[1], ALU.subtract))
                return v.tensor_tensor(x2, t[2], t[3], ALU.add)

            dve.wait_ge(sincos_ready, 2)
            await_taken(dve, ("kiwi", 0))
            for b in range(TB):
                ki = tok[:, b, T_KI:T_KI + ID]
                steps.seq(normalise(b, ki, ki))
                steps.seq(v.tensor_tensor(ki, ki, kig[:, :], ALU.mult))
            steps.seq(rope(T_KI, 1, ID, RI, RA))
            for i in range(2):
                v.tensor_copy(kd[:, :, ID * i:ID * (i + 1)], tok[:, :, T_KI:T_KI + ID]).then_inc(kd_ready, 1)
            steps.seq(v.tensor_scalar(tok[:, :, T_WI:T_WI + NI], tok[:, :, T_WI:T_WI + NI], NI ** -0.5, None, ALU.mult))
            await_taken(dve, ("qi", 1))
            rope(T_QI, NI, ID, RI, RA).then_inc(qi_roped, 1)
            await_job(dve, ("kit", 0))
            free(v.tensor_copy(kdT, bank(("kit", 0))[:, 0:SEQ]))

            def conv(i):
                await_taken(dve, ("xl", i))
                for j in range(CONV_W):
                    for n in range(4 * i, 4 * i + 4):
                        wj = parT[:, PAR_CW + j * NLT + n:PAR_CW + j * NLT + n + 1]
                        if j == 0:
                            ins = v.tensor_scalar(xc[:, n], xlp[:, n, 0:SEQ], wj, parT[:, PAR_CB + n:PAR_CB + n + 1],
                                                  ALU.mult, ALU.add)
                        else:
                            ins = v.scalar_tensor_tensor(out=xc[:, n], in0=xlp[:, n, j:j + SEQ], scalar=wj,
                                                         in1=xc[:, n], op0=ALU.mult, op1=ALU.add)
                        if j < CONV_W - 1:
                            steps.mark(ins)
                        else:
                            ins.then_inc(xc_ready, 1)
                    if j < CONV_W - 1:
                        steps.settle()

            conv(0)
            conv(1)

            seen = 0
            for i, (b, h0, n, keys) in enumerate(LG_UNITS):
                await_taken(dve, ("lg", i))
                for j in range(n):
                    h = h0 + j
                    wcol = tok[:, b, T_WI + h:T_WI + h + 1]
                    o = lg_col(j, n, keys)
                    rl = sm[:, i % 2, o:o + keys]
                    if h == 0:
                        ins = v.tensor_scalar(score[:, b, 0:keys], rl, wcol, None, ALU.mult)
                    else:
                        ins = v.scalar_tensor_tensor(out=score[:, b, 0:keys], in0=rl, scalar=wcol,
                                                     in1=score[:, b, 0:keys], op0=ALU.mult, op1=ALU.add)
                    if j == n - 1:
                        ins.then_inc(relu_used, 1)
                        dve.wait_ge(relu_used, i + 1)
                    else:
                        steps.seq(ins)
            for b in range(TB):
                steps.mark(v.memset(score[0:CHUNK, b, (2 * b + 1) * CHUNK:(2 * b + 2) * CHUNK], NEG))
            steps.settle()
            for rnd in range(TOPK // 8):
                for b in range(TB):
                    keys = (b + 1) * P
                    steps.seq(v.max(m8[:, :], score[:, b, 0:keys]))
                    steps.seq(v.match_replace(score[:, b, 0:keys], m8[:, :], score[:, b, 0:keys], TAKEN))
            for b in range(TB):
                keys = (b + 1) * P
                steps.seq(v.tensor_scalar(score[:, b, 0:keys], score[:, b, 0:keys], TAKEN / 2, NEG, ALU.is_gt, ALU.mult))
            ada_sums(4)
            ada_sums(5)

            dve.wait_ge(xc_ready, NLT)
            await_taken(dve, ("gate", 3))
            steps.seq(v.tensor_tensor(xc[:, :, :], xc[:, :, :], ig[:, :, :], ALU.mult))
            dve.wait_ge(decay_ready, NLT)
            steps.seq(v.tensor_tensor(ig[:, :, :], rg[:, :, :], rg[:, :, :], ALU.mult))
            v.scalar_tensor_tensor(out=th[:, :, :], in0=ig[:, :, :], scalar=1.0, in1=th[:, :, :], op0=ALU.add,
                                   op1=ALU.mult).then_inc(pow_ready, 1)
            dve.wait_ge(sqrt_ready, 1)
            steps.seq(v.tensor_tensor(xc[:, :, :], xc[:, :, :], th[:, :, :], ALU.mult))
            for n in range(NLT):
                steps.mark(v.tensor_tensor_scan(ig[:, n], rg[:, n], xc[:, n], 0.0, ALU.mult, ALU.add))
            steps.settle()
            v.tensor_tensor(concatT[:, 0:NLT, :], ig[:, :, :], concatT[:, 0:NLT, :], ALU.mult).then_inc(lru_done, 1)
            ada_out(4)
            ada_out(5)
            ada_sums(6)
            ada_sums(7)
            ada_sums(8)
            ada_out(6)
            ada_out(7)
            await_taken(dve, ("k", 1))
            rope(T_Q, 2 * NH, HD, RA, 0).then_inc(qk_roped, 1)
            dve.wait_ge(qk_roped, 1)
            ada_sums(9)
            ada_out(8)

            def attention_scores(u):
                b, h0, n, keys = UNITS[u]
                await_job(dve, ("at", u))
                sc = scores_of(u).rearrange("p (h k) -> p h k", h=n)
                mx = amax[:, 8 * u:8 * u + n]
                free(v.scalar_tensor_tensor(out=sc, in0=bank(("at", u)).rearrange("p (h k) -> p h k", h=n),
                                            scalar=HD ** -0.5,
                                            in1=score[:, b, 0:keys].unsqueeze(1).to_broadcast([P, n, keys]),
                                            op0=ALU.mult, op1=ALU.add))
                await_taken(dve, ("at", u))
                steps.seq(v.tensor_reduce(mx, sc, AX.X, ALU.max))
                v.tensor_scalar(mx, mx, -1.0, None, ALU.mult).then_inc(scored_ready, 1)

            def probabilities(u):
                b, h0, n, keys = UNITS[u]
                dve.wait_ge(exp_ready, sum(w[2] for w in UNITS[0:u + 1]))
                tot = asum[:, 8 * u:8 * u + n]
                steps.seq(v.reciprocal(tot, tot))
                sc = scores_of(u).rearrange("p (h k) -> p h k", h=n)
                v.tensor_tensor(sc, sc, tot.unsqueeze(2).to_broadcast([P, n, keys]), ALU.mult).then_inc(prob_ready, 1)

            for u in range(len(UNITS)):
                attention_scores(u)
            for u in range(len(UNITS)):
                probabilities(u)
            ada_sums(10)
            ada_out(9)

            def diagonals(vec):
                for i in range(2):
                    n = BC_SEEN.index((vec, i))
                    if n:
                        await_job(dve, ("bc", BC_SEEN[n - 1]))
                    j = vec * KT + 8 * i
                    cols = mod[:, j:j + 8].rearrange("p (u k) -> p u k", u=2).unsqueeze(3)
                    eye = ident[:, :].unsqueeze(1).unsqueeze(1)
                    v.tensor_tensor(diag, eye.to_broadcast([P, 2, 4, P]), cols.to_broadcast([P, 2, 4, P]),
                                    ALU.mult).then_inc(diag_built, 1)

            await_job(dve, ("pt", 1))
            diagonals(GT1)

            def residual(cc):
                await_job(dve, ("wo", cc))
                sl = slice(cc * CW, (cc + 1) * CW)
                pb = bank(("wo", cc)).rearrange("p (b n) -> p b n", b=TB)
                tmp = sm[:, :, 0:CW]
                free(v.tensor_tensor(tmp, pb, bc[BC_GT1][:, sl].unsqueeze(1).to_broadcast([P, TB, CW]), ALU.mult))
                await_taken(dve, ("wo", cc))
                steps.seq(v.scalar_tensor_tensor(out=xres[:, :, sl], in0=xres[:, :, sl], scalar=ALPHA, in1=tmp,
                                                 op0=ALU.mult, op1=ALU.add))
                for b in range(TB):
                    steps.mark(v.bn_stats(st2[:, b, cc, :], xres[:, b, sl]))

            await_taken(dve, ("bc", (GT1, 1)))
            residual(0)
            ada_sums(11)
            ada_out(10)
            diagonals(SC2)
            residual(1)
            ada_out(11)
            diagonals(SH2)
            residual(2)
            diagonals(GT2)
            residual(3)
            steps.settle()
            dve.wait_ge(ln1_landed, 32)
            for b in range(TB):
                steps.seq(normalise(b, xres[:, b, :], xres[:, b, :], st2[:, b]))
                steps.seq(v.tensor_tensor(xres[:, b, :], xres[:, b, :], bc[BC_G], ALU.mult))
                steps.seq(v.tensor_tensor(xres[:, b, :], xres[:, b, :], bc[BC_B], ALU.add))
                normalise(b, u2[:, b, :], xres[:, b, :]).then_inc(z2_ready, 1)
            v.memset(zeros, 0.0).then_inc(peer_zeros, 1)
            await_taken(dve, ("bc", (SH2, 1)))
            for b in range(TB):
                await_job(dve, ("ut", 2 * b + 1))
                dve.wait_ge(z2_ready, b + 1)
                steps.seq(v.tensor_tensor(u2[:, b, :], u2[:, b, :], bc[BC_SC2], ALU.mult))
                v.tensor_tensor(u2[:, b, :], u2[:, b, :], bc[BC_SH2], ALU.add).then_inc(u2_ready, 1)
            dve.wait_ge(u2_ready, TB)

            def route(it, par):
                take(dve, stage_ready)
                for i in range(2):
                    steps.mark(v.max(topv[:, i, 0:8], stage[:, i, :]))
                steps.settle()
                for i in range(2):
                    steps.mark(v.max_index(topi[:, i, 0:8], topv[:, i, 0:8], stage[:, i, :]))
                    steps.mark(v.match_replace(stage[:, i, :], topv[:, i, 0:8], stage[:, i, :], TAKEN))
                steps.settle()
                for i in range(2):
                    steps.mark(v.max(topv[:, i, 8:16], stage[:, i, :]))
                steps.settle()
                for i in range(2):
                    steps.mark(v.max_index(topi[:, i, 8:16], topv[:, i, 8:16], stage[:, i, :]))
                steps.mark(v.tensor_tensor(cand[:, :, :], topv[:, 0, :].unsqueeze(2).to_broadcast([P, PK, PK]),
                                           topv[:, 1, :].unsqueeze(1).to_broadcast([P, PK, PK]), ALU.add))
                steps.settle()
                cf = cand[:, :, :].rearrange("p a c -> p (a c)")
                steps.mark(v.tensor_copy(topf[:, :, :], topi[:, :, :]))
                steps.seq(v.max(tops[:, par, 0:8], cf))
                steps.mark(v.max_index(pick[:, 0:8], tops[:, par, 0:8], cf))
                steps.seq(v.match_replace(cf, tops[:, par, 0:8], cf, TAKEN))
                steps.seq(v.max(tops[:, par, 8:16], cf))
                steps.mark(v.tensor_scalar(ntop[:, par:par + 1], tops[:, par, 0:1], -1.0, None, ALU.mult))
                v.max_index(pick[:, 8:16], tops[:, par, 8:16], cf).then_inc(top_ready, 1)
                steps.settle()
                dve.wait_ge(top_ready, it + 1)
                steps.mark(v.tensor_scalar(pick2[:, 0, :], pick[:, :], 4, None, ALU.logical_shift_right))
                steps.mark(v.tensor_scalar(pick2[:, 1, :], pick[:, :], PK - 1, None, ALU.bitwise_and))
                steps.settle()
                steps.seq(v.tensor_copy(pickf[:, :, :], pick2[:, :, :]))
                for i in range(2):
                    steps.seq(v.tensor_tensor(onehot[:, :, :], pickf[:, i, :].unsqueeze(2).to_broadcast([P, PK, PK]),
                                              iota[:, :].unsqueeze(1).to_broadcast([P, PK, PK]), ALU.is_equal))
                    steps.seq(v.tensor_tensor(onehot[:, :, :], onehot[:, :, :],
                                              topf[:, i, :].unsqueeze(1).to_broadcast([P, PK, PK]), ALU.mult))
                    steps.seq(v.tensor_reduce(esel[:, i, :], onehot[:, :, :], AX.X, ALU.add))
                v.scalar_tensor_tensor(out=eidx[:, par, :], in0=esel[:, 0, :], scalar=float(NK), in1=esel[:, 1, :],
                                       op0=ALU.mult, op1=ALU.add).then_inc(idx_ready, 1)

            for b in range(TB):
                steps.restart()
                with dve.Fori(0, PH // 2) as r:
                    for par in range(2):
                        it = r * 2 + (PH * b + par)
                        route(it, par)
                        for k in range(PK):
                            dve.wait_ge(row_landed[k % NGR], it * 64 + 16 * (k // NGR + 1))
                            v.scalar_tensor_tensor(out=gathered[:, k % NGR, :], in0=gathered[:, k % NGR, :], scalar=1.0,
                                                   in1=u2[:, b, :], op0=ALU.mult, op1=ALU.mult,
                                                   accum_out=dots[:, par, k:k + 1]).then_inc(slot_free[k % NGR], 1)
                        dve.wait_ge(gexp_ready, it + 1)
                        v.reciprocal(gsum[:, par:par + 1], gsum[:, par:par + 1]).then_inc(dots_done, 1)
                        dve.wait_ge(dots_done, it + 1)
                        dve.wait_ge(gel_ready, it + 1)
                        v.scalar_tensor_tensor(out=hk[:, par, :], in0=gexp[:, par, :], scalar=gsum[:, par:par + 1],
                                               in1=gel[:, par, :], op0=ALU.mult, op1=ALU.mult).then_inc(hk_ready, 1)
                    steps.restart()

            await_taken(dve, ("bc", (GT2, 1)))
            dve.wait_ge(ln2_landed, 32)
            for b in range(TB):
                dve.wait_ge(y_ready, b + 1)
                y = ps[:, 2 * b:2 * b + 2, :].rearrange("p a n -> p (a n)")
                steps.seq(v.tensor_tensor(u2[:, b, :], y, bc[BC_GT2], ALU.mult))
                steps.seq(v.scalar_tensor_tensor(out=xres[:, b, :], in0=xres[:, b, :], scalar=ALPHA, in1=u2[:, b, :],
                                                 op0=ALU.mult, op1=ALU.add))
                steps.seq(normalise(b, xres[:, b, :], xres[:, b, :]))
                steps.seq(v.tensor_tensor(xres[:, b, :], xres[:, b, :], bc[BC_G], ALU.mult))
                v.tensor_tensor(xres[:, b, :], xres[:, b, :], bc[BC_B], ALU.add).then_inc(out_ready, 1)

        @block.tensor
        def _(pe):
            t = nc.tensor
            piece = [0]

            def ada_total(i):
                out_ = start_job(("ada", i))
                pe.wait_ge(ada_summed, 2 * NPIECE * (i + 1))
                for j in range(8):
                    last = t.matmul(out_[:, j:j + 1], partial[:, i % 2, j // 4, j % 4 * P:(j % 4 + 1) * P],
                                    ones[:, 0:1], start=True, stop=True)
                last.then_inc(psum_full, 1)

            def start_job(name):
                n = JOB_AT[name]
                if n >= NPAIR:
                    await_taken(pe, (JOBS[n - NPAIR][0], JOBS[n - NPAIR][1]))
                return bank(name)

            def stream(name, step):
                out_ = start_job(name)
                for q in range(NPIECE):
                    n = piece[0]
                    pe.wait_ge(piece_landed[n % RING], 16 * (n // RING + 1))
                    for kk in range(PIECE_K):
                        last = step(out_, q * PIECE_K + kk, ring[:, n % RING, kk, :])
                    last.then_inc(psum_full if q == NPIECE - 1 else pieces_used, 1)
                    piece[0] += 1

            def token_step(act_T):
                def step(out_, k, w):
                    for b in range(TB):
                        last = t.matmul(out_[:, b * CW:(b + 1) * CW], act_T[:, k, b * P:(b + 1) * P], w,
                                        start=(k == 0), stop=(k == KT - 1))
                    return last
                return step

            def channel_step(out_, k, w):
                for j in range(4):
                    last = t.matmul(out_[:, j * SEQ:(j + 1) * SEQ], w[:, j * P:(j + 1) * P], uT[:, k, :],
                                    start=(k == 0 and j % 2 == 0), stop=(k == KT - 1), skip_group_check=True)
                return last

            def transposes(name, tiles, rows=P):
                out_ = start_job(name)
                for j, tile_ in enumerate(tiles):
                    n = tile_.shape[0]
                    last = t.transpose(out_[:, j * P:j * P + n], tile_, ident[0:n, 0:n])
                last.then_inc(psum_full, 1)

            def token_transposes(name, col, i):
                transposes(name, [tok[:, b, col + (4 * i + j) * P:col + (4 * i + j + 1) * P]
                                  for j in range(4) for b in range(TB)])

            pe.wait_ge(consts_ready, 1 + NF + 1)
            pe.wait_ge(c_landed, 32)
            transposes(("par", 0), [paramA[0:112, :]])
            pe.wait_ge(params_landed, 16 * 5)
            transposes(("par", 1), [paramB[0:64, :]])
            for i in range(4):
                b, half = i // 2, i % 2
                pe.wait_ge(z_ready, b + 1)
                transposes(("zt", i), [z[:, b, (8 * half + k) * P:(8 * half + k + 1) * P] for k in range(8)])
            for i in range(4):
                ada_total(i)

            pe.wait_ge(zt_scaled, KT)
            pe.wait_ge(tail_landed, 16)
            out_ = start_job(("kiwi", 0))
            for b in range(TB):
                for k in range(KT):
                    last = t.matmul(out_[:, b * CW:b * CW + 80], uT[:, k, b * P:(b + 1) * P], w_tail[:, k, :],
                                    start=(k == 0), stop=(k == KT - 1))
            last.then_inc(psum_full, 1)
            stream(("qi", 0), token_step(uT))
            stream(("qi", 1), token_step(uT))
            stream(("xl", 0), channel_step)
            pe.wait_ge(kd_ready, 2)
            transposes(("kit", 0), [kd[:, b, :] for b in range(TB)])
            pe.wait_ge(qi_roped, 1)
            token_transposes(("qit", 0), T_QI, 0)
            token_transposes(("qit", 1), T_QI, 1)
            stream(("xl", 1), channel_step)
            await_taken(pe, ("kit", 0))
            await_taken(pe, ("qit", 1))
            for i, (b, h0, n, keys) in enumerate(LG_UNITS):
                out_ = start_job(("lg", i))
                for j in range(n):
                    h = h0 + j
                    p0 = ID * (h % 2)
                    o = lg_col(j, n, keys)
                    last = t.matmul(out_[:, o:o + keys], qiT[p0:p0 + ID, h // 2, b * P:(b + 1) * P],
                                    kdT[p0:p0 + ID, 0:keys], start=True, stop=True)
                last.then_inc(psum_full, 1)
            stream(("gl", 0), channel_step)
            stream(("gl", 1), channel_step)
            pe.wait_ge(gates_landed, 32)
            for i in range(4):
                out_ = start_job(("gate", i))
                pe.wait_ge(xc_ready, 2 * i + 2)
                for j in range(2):
                    for w in range(2):
                        o = (2 * j + w) * SEQ
                        last = t.matmul(out_[:, o:o + SEQ], gate_w[:, w, 2 * i + j, :], xc[:, 2 * i + j, :],
                                        start=True, stop=True)
                last.then_inc(psum_full, 1)
            stream(("q", 0), token_step(uT))
            ada_total(4)
            ada_total(5)
            stream(("q", 1), token_step(uT))
            stream(("k", 0), token_step(uT))
            ada_total(6)
            ada_total(7)
            stream(("k", 1), token_step(uT))
            stream(("v", 0), token_step(uT))
            ada_total(8)
            pe.wait_ge(qk_roped, 1)
            for kind, col in (("qt", T_Q), ("kt", T_K)):
                for i in range(2):
                    token_transposes((kind, i), col, i)
            for u, (b, h0, n, keys) in enumerate(UNITS):
                out_ = start_job(("at", u))
                await_taken(pe, ("kt", 1))
                for j in range(n):
                    last = t.matmul(out_[:, j * keys:(j + 1) * keys], qT[:, h0 + j, b * P:(b + 1) * P],
                                    kT[:, h0 + j, 0:keys], start=True, stop=True)
                last.then_inc(psum_full, 1)
            stream(("v", 1), token_step(uT))
            ada_total(9)

            def turn(u):
                if u == 2:
                    await_job(pe, ("pv", 0))
                pe.wait_ge(prob_ready, u + 1)
                transposes(("pt", u), [scores_of(u)[:, j * P:(j + 1) * P] for j in range(8)])

            def attend(u):
                b, h0, n, keys = UNITS[u]
                out_ = start_job(("pv", u))
                await_taken(pe, ("pt", u))
                await_taken(pe, ("v", 1))
                for j in range(n):
                    for i in range(keys // P):
                        last = t.matmul(out_[:, j * P:(j + 1) * P],
                                        tok[:, i, T_V + (h0 + j) * HD:T_V + (h0 + j + 1) * HD],
                                        PT[:, u % 2, j * keys + i * P:j * keys + (i + 1) * P],
                                        start=(i == 0), stop=(i == keys // P - 1))
                last.then_inc(psum_full, 1)

            turn(0)
            turn(1)
            attend(0)
            turn(2)
            attend(1)
            attend(2)

            def broadcast(vec):
                for i in range(2):
                    out_ = start_job(("bc", (vec, i)))
                    pe.wait_ge(diag_built, BC_SEEN.index((vec, i)) + 1)
                    for u in range(2):
                        last = t.matmul(out_[:, u * 512:(u + 1) * 512], ones[:, :],
                                        diag[:, u].rearrange("p k n -> p (k n)"), start=True, stop=True)
                    last.then_inc(psum_full, 1)

            broadcast(GT1)
            pe.wait_ge(lru_done, 1)
            await_taken(pe, ("pv", 2))
            stream(("wo", 0), token_step(concatT))
            ada_total(10)
            broadcast(SC2)
            stream(("wo", 1), token_step(concatT))
            ada_total(11)
            broadcast(SH2)
            stream(("wo", 2), token_step(concatT))
            stream(("wo", 3), token_step(concatT))
            broadcast(GT2)
            pe.wait_ge(subkeys_landed, 16)
            for i in range(2):
                transposes(("skt", i), [keyscore[:, (8 * i + j) * P:(8 * i + j + 1) * P] for j in range(8)])
            for i in range(4):
                b, half = i // 2, i % 2
                pe.wait_ge(z2_ready, b + 1)
                transposes(("ut", i), [u2[:, b, (8 * half + k) * P:(8 * half + k + 1) * P] for k in range(8)])
            await_taken(pe, ("ut", 3))
            for c4 in range(4):
                stream(("pq", c4), channel_step)
                out_ = start_job(("sc", c4))
                await_taken(pe, ("pq", c4))
                for b in range(TB):
                    for j in range(4):
                        hp = 4 * c4 + j
                        last = t.matmul(out_[:, (4 * b + j) * P:(4 * b + j + 1) * P], qpT[:, hp, b * P:(b + 1) * P],
                                        subkT[:, hp, :], start=True, stop=True)
                last.then_inc(psum_full, 1)

            await_taken(pe, ("sc", 3))
            pe.wait_ge(peer_zeros, 1)
            for b in range(TB):
                y = ps[:, 2 * b:2 * b + 2, :].rearrange("p a n -> p (a n)")
                for j in range(4):
                    last = t.matmul(y[:, j * 512:(j + 1) * 512], ones[:, :], zeros, start=True, stop=False,
                                    skip_group_check=True)
                if b == 0:
                    last.then_inc(v_started, PK)
                with pe.Fori(0, PH // 2) as r:
                    for par in range(2):
                        it = r * 2 + (PH * b + par)
                        for k in range(PK):
                            pe.wait_ge(diag_ready, it * PK + (k + 1))
                            pe.wait_ge(row_landed[k % NGR], it * 64 + (32 + 16 * (k // NGR + 1)))
                            for j in range(4):
                                last = t.matmul(y[:, j * 512:(j + 1) * 512], diag[:, k // 4 % 2, k % 4, :],
                                                gathered[:, k % NGR, j * 512:(j + 1) * 512], start=False,
                                                stop=False, skip_group_check=True)
                                if j == 0:
                                    last.then_inc(v_started, 1)
                            last.then_inc(slot_free[k % NGR], 1)
                t.matmul(y[:, 0:512], ones[:, :], zeros, start=False, stop=True,
                         skip_group_check=True).then_inc(y_ready, 1)


_INS = ["x", "c", "positions", "w_ada", "b_ada", "w_in", "conv_w", "conv_b", "w_rg_a", "b_rg_a", "w_rg_x", "b_rg_x",
        "lru_lambda", "k_idx_g", "w_out", "ln1_g", "ln1_b", "w_pq", "peer_sub_keys", "peer_u", "peer_v", "ln2_g",
        "ln2_b"]


def kernel(**inputs):
    import concourse.bacc as _bacc
    from concourse.bass_utils import run_bass_kernel_spmd as _run

    nc = _bacc.Bacc("TRN2", target_bir_lowering=False, num_devices=1)
    arrays, args = {}, []
    for name in _INS:
        a = np.ascontiguousarray(inputs[name])
        arrays[f"in_{name}_dram"] = a
        args.append(nc.dram_tensor(f"in_{name}_dram", a.shape, mybir.dt.from_np(a.dtype), kind="ExternalInput").ap())
    args.append(nc.dram_tensor("out_dram", (1, SEQ, D), F32, kind="ExternalOutput").ap())
    build_layer(nc, *args)
    r = _run(nc, [arrays], core_ids=[0])
    return r.results[0]["out_dram"]
```

```python
from contextlib import ExitStack

import numpy as np
import concourse.bass as bass
from concourse import mybir

ALU = mybir.AluOpType
ACT = mybir.ActivationFunctionType
AX = mybir.AxisListType
F32 = mybir.dt.float32
I32 = mybir.dt.int32
U32 = mybir.dt.uint32

P = 128
SEQ = 256
TB = SEQ // P
D = 2048
KT = D // P
D_LRU = 1024
NLT = D_LRU // P
CONV_W = 4
NH, HD = 8, 128
NI, ID = 16, 64
CHUNK = 64
TOPK = 64
D_IN = 2 * D_LRU + 3 * NH * HD + NI * ID + ID + NI
COL_Q, COL_QI, COL_KI = 2 * D_LRU, 2 * D_LRU + 3 * NH * HD, 2 * D_LRU + 3 * NH * HD + NI * ID
NT = D_IN - COL_Q
T_Q, T_K, T_V, T_QI, T_KI, T_WI = 0, 1024, 2048, 3072, 4096, 4160
PH, NK, PK = 8, 128, 16
EPS = 1e-5
ALPHA = 2.0 ** 0.25
ROPE_THETA = 500000.0
RA, RI = 16, 8
NF = RA + RI
NEG = -1.0e30
TAKEN = -3.0e38

PIECE_K = 4
NPIECE = KT // PIECE_K
CW = 512
RING = 3
ARING = 4
NGR = 8
FIRST_SLOT = RING
NPAIR = 4
DVE_ROWS = (2, 5, 8, 11)
PE_ROWS = tuple(k for k in range(PK) if k not in DVE_ROWS)
NPE = len(PE_ROWS)
NDIAG = 8
LO, HI = 0, 1

SH1, SC1, GT1, SH2, SC2, GT2 = range(6)

CHUNKS = [(w, c) for w, n in (("qi", 2), ("xl", 2), ("gl", 2), ("q", 2), ("k", 2), ("v", 2), ("wo", 4), ("pq", 4))
          for c in range(n)]
ADA = [(g, half) for g in (SH1, SC1, GT1, SC2, SH2, GT2) for half in range(2)]
ADA_PE = (1, 3)
PAIR_PIECES = 2 * NPIECE
_dve = [(i, n) for i in range(len(ADA)) if i not in ADA_PE for n in range(PAIR_PIECES)]
_pe = [(i, n) for i in ADA_PE for n in range(PAIR_PIECES)]
ADA_PIECES = [piece for both in zip(_dve, _pe) for piece in both] + _dve[len(_pe):]
ADA_POS = {piece: n for n, piece in enumerate(ADA_PIECES)}
_pairs = [i for i in range(len(ADA)) if i not in ADA_PE]
ADA_SLOT = {i: n % 2 for n, i in enumerate(_pairs)}
ADA_BEFORE = {i: _pairs[n - 2] for n, i in enumerate(_pairs) if n >= 2}

JOBS = [("par", 0, "dve"), ("row", 0, "act"), ("row", 1, "act")] + [("zt", i, "act") for i in range(4)]
JOBS += [("ada", 0, "dve"), ("ada", 1, "dve"), ("row", 2, "act"), ("row", 3, "act"), ("par", 1, "dve")]
JOBS += [("ada", 2, "dve"), ("ada", 3, "dve")]
JOBS += [("kiwi", 0, "act"), ("qi", 0, "act"), ("qi", 1, "act"), ("ada", 4, "dve"), ("xl", 0, "act")]
JOBS += [("kit", 0, "act"), ("qit", 0, "act"), ("qit", 1, "act"), ("ada", 5, "dve"), ("xl", 1, "act"), ("ada", 6, "dve")]
JOBS += [("lg", i, "act") for i in range(6)]
JOBS += [("gl", 0, "act"), ("gl", 1, "act")] + [("gate", i, "act") for i in range(4)]
JOBS += [("ada", 7, "dve"), ("q", 0, "act"), ("ada", 8, "dve"), ("q", 1, "act"), ("ada", 9, "dve"), ("k", 0, "act"), ("ada", 10, "dve")]
JOBS += [("k", 1, "act"), ("v", 0, "act"), ("ada", 11, "dve")]
JOBS += [("qt", 0, "act"), ("qt", 1, "act"), ("kt", 0, "act"), ("kt", 1, "act")]
JOBS += [("at", 0, "dve"), ("at", 1, "dve"), ("at", 2, "dve"), ("v", 1, "act")]
JOBS += [("pt", 0, "act"), ("pt", 1, "act"), ("pv", 0, "act"), ("pt", 2, "act"), ("pv", 1, "act"), ("pv", 2, "act")]
JOBS += [("bc", (GT1, 0), "act"), ("bc", (GT1, 1), "act"), ("wo", 0, "dve")]
JOBS += [("bc", (SC2, 0), "act"), ("bc", (SC2, 1), "act"), ("wo", 1, "dve")]
JOBS += [("bc", (SH2, 0), "act"), ("bc", (SH2, 1), "act"), ("wo", 2, "dve"), ("wo", 3, "dve")]
JOBS += [("ut", 0, "act"), ("ut", 1, "act"), ("skt", 0, "act"), ("skt", 1, "act")]
JOBS += [("bc", (GT2, 0), "act"), ("bc", (GT2, 1), "act"), ("ut", 2, "act"), ("ut", 3, "act")]
JOBS += [("pq", "first", "act"), ("sc", "first", "act"), ("pq", 0, "act"), ("sc", 0, "act")]
for _c in range(1, 4):
    JOBS += [("pq", _c, "act"), ("sc", _c, "act")]
JOB_AT = {(kind, i): n for n, (kind, i, _) in enumerate(JOBS)}
JOB_ENG = [e for _, _, e in JOBS]
BC_SEEN = [i for k, i, _ in JOBS if k == "bc"]

PAR_C, PAR_BADA = 0, KT
PAR_CW, PAR_CB, PAR_BA, PAR_BX, PAR_LAM = 112, 144, 152, 160, 168
NPAR = 176
UNITS = [(0, 0, 8, P), (1, 0, 4, SEQ), (1, 4, 4, SEQ)]
LG_UNITS = [(0, 0, 8, P), (0, 8, 8, P)] + [(1, 4 * i, 4, SEQ) for i in range(4)]


class Steps:

    def __init__(self, eng, sem):
        self.eng, self.sem, self.n = eng, sem, 0

    def mark(self, ins):
        ins.then_inc(self.sem, 1)
        self.n += 1

    def settle(self):
        self.eng.wait_ge(self.sem, self.n)

    def restart(self):
        self.settle()
        self.eng.sem_clear(self.sem)
        self.n = 0

    def seq(self, ins):
        self.mark(ins)
        self.settle()


def lg_col(j, n, keys):
    return ((j % 2) * (n // 2) + j // 2) * keys


def take(eng, sem):
    eng.wait_ge(sem, 1)
    eng.sem_clear(sem)


def build_layer(nc, x, c, positions, w_ada, b_ada, w_in, conv_w, conv_b, w_rg_a, b_rg_a, w_rg_x, b_rg_x,
                lru_lambda, k_idx_g, w_out, ln1_g, ln1_b, w_pq, peer_sub_keys, peer_u, peer_v, ln2_g, ln2_b, out):
    ctx = ExitStack()
    with ctx:
        def sb(name, shape, dt=F32):
            return ctx.enter_context(nc.sbuf_tensor(name, shape, dt))

        def sem(name):
            return ctx.enter_context(nc.semaphore(name))

        arena = sb("arena", [P, 64 * 256])
        ring = arena[:, 0:RING * PIECE_K * CW].rearrange("p (s k n) -> p s k n", s=RING, k=PIECE_K)
        A0 = RING * PIECE_K * CW
        A1 = A0 + ARING * PIECE_K * CW
        aring = arena[:, A0:A1].rearrange("p (s k n) -> p s k n", s=ARING, k=PIECE_K)
        partial = arena[:, A1:A1 + 4 * CW].rearrange("p (a c n) -> p a c n", a=2, c=2)
        gathered = arena[:, :].rearrange("p (s d) -> p s d", s=NGR)
        xres = sb("xres", [P, TB, D])
        uT = sb("uT", [P, KT, SEQ])
        tokbuf = sb("tokbuf", [P, TB * NT])
        tok = tokbuf[:, 0:TB * NT].rearrange("p (b n) -> p b n", b=TB)
        z = tokbuf[:, 0:TB * D].rearrange("p (b d) -> p b d", b=TB)
        keyscore = tokbuf[:, 0:TB * D]
        u2 = tokbuf[:, TB * D:2 * TB * D].rearrange("p (b d) -> p b d", b=TB)
        lru = sb("lru", [P, 5 * D + 32])
        work = [lru[:, 32 + i * D:32 + (i + 1) * D] for i in range(5)]
        xlp = lru[:, 0:NLT * (SEQ + 3)].rearrange("p (n t) -> p n t", n=NLT)
        xc, rg, ig, th = (w.rearrange("p (n t) -> p n t", n=NLT) for w in work[1:5])
        w_tail = work[3][:, 0:KT * 80].rearrange("p (k n) -> p k n", k=KT)
        PT = work[2].rearrange("p (u n) -> p u n", u=2)
        qT, kT = (w.rearrange("p (h t) -> p h t", h=NH) for w in work[3:5])
        qpT = lru[:, 32:32 + 2 * D].rearrange("p (h t) -> p h t", h=2 * PH)
        gate_w = work[4].rearrange("p (w n e) -> p w n e", w=2, n=NLT)
        BC_GT1, BC_G, BC_B, BC_SC2, BC_SH2 = range(5)
        vsum = work[3:5]
        BC_GT2 = 5
        concatT = sb("concatT", [P, KT, SEQ])
        qiT = concatT[:, NLT:KT, :]
        bc = work + [concatT[:, NLT:KT, :].rearrange("p n t -> p (n t)")]
        subkT = concatT[:, 0:NLT, :].rearrange("p n (a t) -> p (n a) t", a=2)
        sm = sb("sm", [P, 2, 1024])
        small = sb("small", [P, 1024])
        score = small[:, 0:TB * SEQ].rearrange("p (b s) -> p b s", b=TB)
        kdT = small[:, 512:768]
        kd = small[:, 768:1024].rearrange("p (b n) -> p b n", b=TB)
        cand = small[:, 0:256].rearrange("p (a c) -> p a c", a=PK)
        onehot = small[:, 256:512].rearrange("p (a c) -> p a c", a=PK)
        stage = small[:, 512:768].rearrange("p (a n) -> p a n", a=2)
        ident = sb("ident", [P, P])
        ones = sb("ones", [P, P])
        diag = sm[:, :, 512:1024].rearrange("p u (k n) -> p u k n", k=4)
        zeros = sm[:, 0, 0:512]
        ada_row = [v[0:1, :].rearrange("p (c n) -> p c n", c=2) for v in (sm[:, 0, :], small)]
        late = [w.rearrange("p (k n) -> p k n", k=PIECE_K) for w in work[2:5]]
        paramA, paramB = sm[:, 0, 0:P], sm[:, 1, 0:P]
        parT = sb("parT", [P, NPAR])
        sT = sb("sT", [P, KT])
        mod = sb("mod", [P, 6 * KT])
        pos_i = sb("pos_i", [P, TB], I32)
        posf = sb("posf", [P, TB])
        freq = sb("freq", [P, NF])
        ang = sb("ang", [P, TB, NF])
        ang2 = sb("ang2", [P, TB, NF])
        sin = sb("sin", [P, TB, NF])
        cos = sb("cos", [P, TB, NF])
        kig = sb("kig", [P, ID])
        st = sb("st", [P, 4, 6])
        st2 = sb("st2", [P, TB, 4, 6])
        mv = sb("mv", [P, TB, 2])
        rstd = sb("rstd", [P, TB])
        m8 = sb("m8", [P, 8])
        amax = sb("amax", [P, 24])
        asum = sb("asum", [P, 24])
        sp = sb("sp", [P, 6, NLT])
        nsp8 = sb("nsp8", [P, NLT])
        psp8 = sb("psp8", [P, NLT])
        iota_i = sb("iota_i", [P, PK], I32)
        iota = sb("iota", [P, PK])
        topv = sb("topv", [P, 2, PK])
        topi = sb("topi", [P, 2, PK], U32)
        topf = sb("topf", [P, 2, PK])
        tops = sb("tops", [P, 2, PK])
        pick = sb("pick", [P, PK], U32)
        pick2 = sb("pick2", [P, 2, PK], U32)
        pickf = sb("pickf", [P, 2, PK])
        esel = sb("esel", [P, 2, PK])
        eidx = sb("eidx", [P, 2, PK], U32)
        ntop = sb("ntop", [P, 2])
        gexp = sb("gexp", [P, 2, PK])
        gsum = sb("gsum", [P, 2])
        dots = sb("dots", [P, 2, PK])
        gel = sb("gel", [P, 2, PK])
        hk = sb("hk", [P, 2, PK])
        ropet = sm[:, :, :].rearrange("p u n -> p (u n)")
        ps = ctx.enter_context(nc.psum_tensor("ps", [P, NPAIR, 1024], F32))

        def scores_of(u):
            return sm[:, u, :] if u < 2 else work[1][:, 0:1024]

        piece_landed = [sem(f"piece_landed{i}") for i in range(RING)]
        pieces_used = sem("pieces_used")
        ada_landed = [sem(f"ada_landed{i}") for i in range(ARING)]
        ada_summed = sem("ada_summed")
        ada_multiplied = sem("ada_multiplied")
        late_landed = [sem(f"late_landed{i}") for i in range(RING)]
        c_landed = sem("c_landed")
        psum_full = sem("psum_full")
        psum_freed = {"act": sem("psum_freed_by_act"), "dve": sem("psum_freed_by_dve")}
        x_landed = [sem(f"x_landed{i}") for i in range(TB)]
        params_landed = sem("params_landed")
        small_landed = sem("small_landed")
        tail_landed = sem("tail_landed")
        gates_landed = sem("gates_landed")
        subkeys_landed = sem("subkeys_landed")
        ln1_landed = sem("ln1_landed")
        ln2_landed = sem("ln2_landed")
        out_landed = sem("out_landed")
        consts_ready = sem("consts_ready")
        pool_step = sem("pool_step")
        dve_step = sem("dve_step")
        act_step = sem("act_step")
        var_ready = sem("var_ready")
        std_ready = sem("std_ready")
        z_ready = sem("z_ready")
        zt_scaled = sem("zt_scaled")
        sT_ready = sem("sT_ready")
        lam_exp = sem("lam_exp")
        ang_ready = sem("ang_ready")
        sincos_ready = sem("sincos_ready")
        qi_roped = sem("qi_roped")
        kd_ready = sem("kd_ready")
        relu_used = sem("relu_used")
        qk_roped = sem("qk_roped")
        scored_ready = sem("scored_ready")
        exp_ready = sem("exp_ready")
        prob_ready = sem("prob_ready")
        xc_ready = sem("xc_ready")
        decay_ready = sem("decay_ready")
        pow_ready = sem("pow_ready")
        sqrt_ready = sem("sqrt_ready")
        lru_done = sem("lru_done")
        diag_built = sem("diag_built")
        z2_ready = sem("z2_ready")
        u2_ready = sem("u2_ready")
        peer_zeros = sem("peer_zeros")
        stage_ready = sem("stage_ready")
        idx_ready = sem("idx_ready")
        top_ready = sem("top_ready")
        gexp_ready = sem("gexp_ready")
        dots_done = sem("dots_done")
        gel_ready = sem("gel_ready")
        hk_ready = sem("hk_ready")
        diag_ready = sem("diag_ready")
        row_landed = [sem(f"row_landed{i}") for i in range(NGR)]
        slot_free = [sem(f"slot_free{i}") for i in range(NGR)]
        v_started = sem("v_started")
        vsum_added = sem("vsum_added")
        vsum_zeroed = sem("vsum_zeroed")
        y_ready = sem("y_ready")
        out_ready = sem("out_ready")

        SRC = {"qi": (w_in, COL_QI), "q": (w_in, COL_Q), "k": (w_in, COL_Q + 1024), "v": (w_in, COL_Q + 2048),
               "xl": (w_in, 0), "gl": (w_in, D_LRU), "wo": (w_out, 0), "pq": (w_pq, 0)}
        u_rows = peer_u[0]
        v_rows = peer_v[0]

        LATE = (len(CHUNKS) - 4) * NPIECE + RING

        def piece_place(n):
            if n < LATE:
                return ring[:, n % RING], piece_landed[n % RING], n // RING + 1
            n -= LATE
            return late[n % RING], late_landed[n % RING], n // RING + 1

        def await_piece_used(eng, n):
            if n % NPIECE == NPIECE - 1:
                await_job(eng, CHUNKS[n // NPIECE])
            else:
                eng.wait_ge(pieces_used, n - n // NPIECE + 1)

        def await_ada_used(eng, n):
            on_pe = [i in ADA_PE for i, _ in ADA_PIECES[0:n + 1]]
            used = on_pe.count(on_pe[n])
            if on_pe[n] and used % NPIECE == 0:
                await_job(eng, ("row", used // NPIECE - 1))
            elif on_pe[n]:
                eng.wait_ge(ada_multiplied, used - used // NPIECE)
            else:
                eng.wait_ge(ada_summed, used)

        def slot_of(k):
            return (k + FIRST_SLOT) % NGR

        def bank(name):
            return ps[:, JOB_AT[name] % NPAIR, :]

        def await_job(eng, name):
            eng.wait_ge(psum_full, JOB_AT[name] + 1)

        def await_taken(eng, name):
            n = JOB_AT[name]
            eng.wait_ge(psum_freed[JOB_ENG[n]], JOB_ENG[0:n + 1].count(JOB_ENG[n]))

        block = ctx.enter_context(nc.Block())

        @block.sync
        def _(sp_):
            for b in range(TB):
                sp_.dma_start(xres[:, b, :], x[0, b * P:(b + 1) * P, :]).then_inc(x_landed[b], 16)
            await_job(sp_, ("row", 3))
            n = 0
            for kind, col in CHUNKS:
                w, c0 = SRC[kind]
                for q in range(NPIECE):
                    if n == LATE:
                        sp_.wait_ge(z2_ready, TB)
                    elif LATE < n < LATE + RING:
                        sp_.wait_ge(u2_ready, TB)
                    elif n >= RING:
                        await_piece_used(sp_, n - RING)
                    place, landed, _ = piece_place(n)
                    src = w[0, q * PIECE_K * P:(q + 1) * PIECE_K * P, c0 + col * CW:c0 + (col + 1) * CW]
                    sp_.dma_start(place, src.rearrange("(k p) n -> p k n", p=P)).then_inc(landed, 16)
                    n += 1
            for b in range(TB):
                sp_.wait_ge(out_ready, b + 1)
                sp_.dma_start(out[0, b * P:(b + 1) * P, :], xres[:, b, :]).then_inc(out_landed, 16)
            sp_.wait_ge(out_landed, 16 * TB)

        @block.gpsimd
        def _(pool):
            g = nc.gpsimd

            def load_ada(n):
                if n >= ARING:
                    await_ada_used(pool, n - ARING)
                i, m = ADA_PIECES[n]
                (grp, half), cc, q = ADA[i], m // NPIECE, m % NPIECE
                c0 = grp * D + (2 * half + cc) * CW
                src = w_ada[0, q * PIECE_K * P:(q + 1) * PIECE_K * P, c0:c0 + CW]
                g.dma_start(aring[:, n % ARING], src.rearrange("(k p) n -> p k n", p=P)).then_inc(
                    ada_landed[n % ARING], 16)

            for n in range(ARING):
                load_ada(n)
            steps = Steps(pool, pool_step)
            steps.mark(g.memset(ident[:, :], 0.0))
            g.memset(ones[:, :], 1.0).then_inc(consts_ready, 1)
            for j in range(RA):
                f = float(np.float32(ROPE_THETA) ** (-np.float32(j) / np.float32(RA)))
                g.memset(freq[:, j:j + 1], f).then_inc(consts_ready, 1)
            for j in range(RI):
                f = float(np.float32(ROPE_THETA) ** (-np.float32(j) / np.float32(RI)))
                g.memset(freq[:, RA + j:RA + j + 1], f).then_inc(consts_ready, 1)
            steps.settle()
            g.affine_select(out=ident[:, :], in_=ident[:, :], compare_op=ALU.not_equal, fill=1.0, base=0,
                            pattern=[[-1, P]], channel_multiplier=1).then_inc(consts_ready, 1)
            g.iota(iota_i[:, :], pattern=[[1, PK]], base=0, channel_multiplier=0).then_inc(consts_ready, 1)

            for n in range(ARING, len(ADA_PIECES)):
                load_ada(n)

            def diagonals(vec):
                for i in range(2):
                    n = BC_SEEN.index((vec, i))
                    if n:
                        await_job(pool, ("bc", BC_SEEN[n - 1]))
                    j = vec * KT + 8 * i
                    cols = mod[:, j:j + 8].rearrange("p (u k) -> p u k", u=2).unsqueeze(3)
                    eye = ident[:, :].unsqueeze(1).unsqueeze(1)
                    g.tensor_tensor(diag, eye.to_broadcast([P, 2, 4, P]), cols.to_broadcast([P, 2, 4, P]),
                                    ALU.mult).then_inc(diag_built, 1)

            await_taken(pool, ("ada", len(ADA) - 1))
            await_job(pool, ("pt", 1))
            for vec in (GT1, SC2, SH2, GT2):
                diagonals(vec)

            for slot in slot_free:
                pool.sem_inc(slot, 1)
            def gather_head(par, pace=False):
                take(pool, idx_ready)
                for use in range(4):
                    for i in range(NGR):
                        k, s = (use % 2) * NGR + i, slot_of(i)
                        if pace and use == 0 and s < RING:
                            await_piece_used(pool, LATE - 1)
                        if pace and use < 2:
                            n = LATE - 3 + k * (len(CHUNKS) * NPIECE - LATE + 3) // (PK + 4)
                            if n >= LATE:
                                await_piece_used(pool, n)
                        take(pool, slot_free[s])
                        rows = u_rows if use < 2 else v_rows
                        g.indirect_dma_start(
                            out=gathered[:, s, :], out_offset=None, in_=rows,
                            in_offset=bass.IndirectOffsetOnAxis(ap=eidx[:, par, k:k + 1], axis=0),
                        ).then_inc(row_landed[s], 16)

            gather_head(0, pace=True)
            gather_head(1)
            for b in range(TB):
                with pool.Fori(1 - b, PH // 2) as r:
                    for par in range(2):
                        gather_head(par)

        @block.scalar
        def _(act):
            s = nc.scalar
            steps = Steps(act, act_step)

            def free(ins):
                ins.then_inc(psum_freed["act"], 1)

            def row(v, n):
                return v.rearrange("l (r p) -> (l r) p", p=P)[0:n]

            act.dma_start(paramA[PAR_C:PAR_C + KT, :], c.rearrange("l (r p) -> (l r) p", p=P)).then_inc(c_landed, 16)
            act.dma_start(paramA[PAR_BADA:PAR_BADA + 96, :], row(b_ada, 96)).then_inc(c_landed, 16)
            act.dma_start(paramB[0:32, :], conv_w[0].rearrange("j (n p) -> (j n) p", p=P)).then_inc(params_landed, 16)
            for i, v in enumerate((conv_b, b_rg_a, b_rg_x, lru_lambda)):
                act.dma_start(paramB[32 + 8 * i:40 + 8 * i, :], row(v, 8)).then_inc(params_landed, 16)
            for b in range(TB):
                act.dma_start(pos_i[:, b:b + 1], positions[0, b * P:(b + 1) * P].unsqueeze(1)).then_inc(small_landed, 16)
            act.dma_start(kig[:, :], k_idx_g[0].partition_broadcast(P)).then_inc(small_landed, 16)

            await_taken(act, ("par", 0))
            s.activation(sT[:, :], parT[:, PAR_C:PAR_C + KT], ACT.Silu).then_inc(sT_ready, 1)
            for b in range(TB):
                act.wait_ge(var_ready, b + 1)
                s.activation(rstd[:, b:b + 1], rstd[:, b:b + 1], ACT.Sqrt).then_inc(std_ready, 1)
            def keep_row(i):
                await_job(act, ("row", i))
                free(s.copy(ada_row[i // 2][:, i % 2, :], bank(("row", i))[0:1, 0:CW]))

            keep_row(0)
            keep_row(1)
            for i in range(4):
                b, half = i // 2, i % 2
                await_job(act, ("zt", i))
                free(s.copy(uT[:, 8 * half:8 * half + 8, b * P:(b + 1) * P],
                            bank(("zt", i)).rearrange("p (k t) -> p k t", k=8)))
            keep_row(2)
            keep_row(3)
            act.dma_start(w_tail, w_in[0, :, COL_KI:D_IN].rearrange("(k p) n -> p k n", p=P)).then_inc(tail_landed, 16)
            act.dma_start(gate_w[:, 0], w_rg_a[0].rearrange("n d e -> d n e")).then_inc(gates_landed, 16)
            act.dma_start(gate_w[:, 1], w_rg_x[0].rearrange("n d e -> d n e")).then_inc(gates_landed, 16)
            act.wait_ge(ang_ready, 1)
            s.activation(sin[:, :, :], ang[:, :, :], ACT.Sin).then_inc(sincos_ready, 1)
            s.activation(cos[:, :, :], ang2[:, :, :], ACT.Sin).then_inc(sincos_ready, 1)
            act.wait_ge(lam_exp, 1)
            s.activation(sp[:, 1, :], sp[:, 0, :], ACT.Exp).then_inc(lam_exp, 1)

            await_job(act, ("kiwi", 0))
            free(s.copy(tok[:, :, T_KI:NT],
                        bank(("kiwi", 0)).rearrange("p (b n) -> p b n", b=TB)[:, :, 0:80]))

            def keep(kind, cc, at):
                await_job(act, (kind, cc))
                free(s.copy(tok[:, :, at + cc * CW:at + (cc + 1) * CW],
                            bank((kind, cc)).rearrange("p (b n) -> p b n", b=TB)))

            for b in range(TB):
                act.wait_ge(var_ready, TB + b + 1)
                s.activation(rstd[:, b:b + 1], rstd[:, b:b + 1], ACT.Sqrt).then_inc(std_ready, 1)
            keep("qi", 0, T_QI)
            keep("qi", 1, T_QI)

            def keep_xl(i):
                await_job(act, ("xl", i))
                free(s.copy(xlp[:, 4 * i:4 * i + 4, 3:3 + SEQ], bank(("xl", i)).rearrange("p (n t) -> p n t", n=4)))

            def keep_gl(i):
                await_job(act, ("gl", i))
                free(s.activation(concatT[:, 4 * i:4 * i + 4, :], bank(("gl", i)).rearrange("p (n t) -> p n t", n=4),
                                  ACT.Gelu_apprx_tanh))

            keep_xl(0)
            await_job(act, ("kit", 0))
            free(s.copy(kdT, bank(("kit", 0))[:, 0:SEQ]))
            for i in range(2):
                await_job(act, ("qit", i))
                free(s.copy(qiT[:, 4 * i:4 * i + 4, :], bank(("qit", i)).rearrange("p (h t) -> p h t", h=4)))
            keep_xl(1)
            for i, (b, h0, n, keys) in enumerate(LG_UNITS):
                await_job(act, ("lg", i))
                if i >= 2:
                    act.wait_ge(relu_used, i - 1)
                free(s.activation(sm[:, i % 2, :], bank(("lg", i)), ACT.Relu, scale=ID ** -0.5))
            keep_gl(0)
            keep_gl(1)
            for i in range(4):
                await_job(act, ("gate", i))
                pb = bank(("gate", i)).rearrange("p (n g t) -> p n g t", n=2, g=2)
                for j in range(2):
                    n = 2 * i + j
                    steps.mark(s.activation(rg[:, n], pb[:, j, 0], ACT.Sigmoid, bias=parT[:, PAR_BA + n:PAR_BA + n + 1]))
                    ins = s.activation(ig[:, n], pb[:, j, 1], ACT.Sigmoid, bias=parT[:, PAR_BX + n:PAR_BX + n + 1])
                free(ins)
            steps.settle()
            for n in range(NLT):
                steps.mark(s.activation(th[:, n], rg[:, n], ACT.Tanh, scale=psp8[:, n:n + 1]))
            for n in range(NLT):
                s.activation(rg[:, n], rg[:, n], ACT.Exp, scale=nsp8[:, n:n + 1]).then_inc(decay_ready, 1)
            act.wait_ge(pow_ready, 1)
            s.activation(th[:, :, :], th[:, :, :], ACT.Sqrt).then_inc(sqrt_ready, 1)

            def broadcast_out(vec, slot):
                for i in range(2):
                    await_job(act, ("bc", (vec, i)))
                    free(s.copy(bc[slot][:, 1024 * i:1024 * (i + 1)], bank(("bc", (vec, i)))))

            keep("q", 0, T_Q)
            keep("q", 1, T_Q)
            keep("k", 0, T_K)
            keep("k", 1, T_K)
            keep("v", 0, T_V)
            act.wait_ge(lru_done, 1)
            for i in range(2):
                await_job(act, ("qt", i))
                free(s.copy(qT[:, 4 * i:4 * i + 4, :], bank(("qt", i)).rearrange("p (h t) -> p h t", h=4)))
            for i in range(2):
                await_job(act, ("kt", i))
                free(s.copy(kT[:, 4 * i:4 * i + 4, :], bank(("kt", i)).rearrange("p (h t) -> p h t", h=4)))

            def exps(u):
                b, h0, n, keys = UNITS[u]
                act.wait_ge(scored_ready, u + 1)
                for h in range(n):
                    sl = scores_of(u)[:, h * keys:(h + 1) * keys]
                    s.activation(sl, sl, ACT.Exp, bias=amax[:, 8 * u + h:8 * u + h + 1],
                                 accum_out=asum[:, 8 * u + h:8 * u + h + 1]).then_inc(exp_ready, 1)

            def keep_p(u):
                await_job(act, ("pt", u))
                free(s.copy(PT[:, u % 2, :], bank(("pt", u))))

            def keep_y(u):
                b, h0, n, keys = UNITS[u]
                await_job(act, ("pv", u))
                free(s.copy(concatT[:, NLT + h0:NLT + h0 + n, b * P:(b + 1) * P],
                            bank(("pv", u))[:, 0:n * P].rearrange("p (h t) -> p h t", h=n)))

            for u in range(len(UNITS)):
                exps(u)
            keep("v", 1, T_V)
            keep_p(0)
            keep_p(1)
            keep_y(0)
            keep_p(2)
            keep_y(1)
            keep_y(2)

            def broadcast_out(vec, slot):
                for i in range(2):
                    await_job(act, ("bc", (vec, i)))
                    free(s.copy(bc[slot][:, 1024 * i:1024 * (i + 1)], bank(("bc", (vec, i)))))

            act.dma_start(bc[BC_G], ln1_g[0].partition_broadcast(P)).then_inc(ln1_landed, 16)
            act.dma_start(bc[BC_B], ln1_b[0].partition_broadcast(P)).then_inc(ln1_landed, 16)
            act.dma_start(keyscore[:, 0:2 * PH * P].rearrange("p (h d) -> p h d", h=2 * PH),
                          peer_sub_keys[0].rearrange("h a n d -> n (h a) d")).then_inc(subkeys_landed, 16)
            broadcast_out(GT1, BC_GT1)
            broadcast_out(SC2, BC_SC2)
            broadcast_out(SH2, BC_SH2)
            def deviation(b, i):
                act.wait_ge(var_ready, 2 * TB + 2 * b + i + 1)
                s.activation(rstd[:, b:b + 1], rstd[:, b:b + 1], ACT.Sqrt).then_inc(std_ready, 1)

            def modulated(i):
                b, half = i // 2, i % 2
                await_job(act, ("ut", i))
                for j in range(8):
                    k = 8 * half + j
                    ins = s.activation(uT[:, k, b * P:(b + 1) * P], bank(("ut", i))[:, j * P:(j + 1) * P], ACT.Identity,
                                       bias=mod[:, SH2 * KT + k:SH2 * KT + k + 1],
                                       scale=mod[:, SC2 * KT + k:SC2 * KT + k + 1])
                    if j < 7:
                        steps.mark(ins)
                free(ins)

            deviation(0, 0)
            deviation(0, 1)
            deviation(1, 0)
            modulated(0)
            modulated(1)
            deviation(1, 1)
            for i in range(2):
                await_job(act, ("skt", i))
                free(s.copy(subkT[:, 8 * i:8 * i + 8, :], bank(("skt", i)).rearrange("p (n t) -> p n t", n=8)))
            broadcast_out(GT2, BC_GT2)
            modulated(2)
            modulated(3)
            flat = stage[:, :, :].rearrange("p a n -> p (a n)")
            def keep_queries(name, first, n):
                await_job(act, ("pq", name))
                free(s.copy(qpT[:, first:first + n, :],
                            bank(("pq", name))[:, 0:n * SEQ].rearrange("p (h t) -> p h t", h=n)))
                await_job(act, ("sc", name))
                free(s.copy(keyscore[:, :].rearrange("p (b n) -> p b n", b=TB)[:, :, P * first:P * (first + n)],
                            bank(("sc", name)).rearrange("p (b n) -> p b n", b=TB)[:, :, 0:n * P]))

            act.wait_ge(z2_ready, TB)
            keep_queries("first", 0, 2)
            await_taken(act, ("sc", "first"))
            s.copy(flat, keyscore[:, 0:256]).then_inc(stage_ready, 1)
            keep_queries(0, 2, 2)
            for i in range(1, 4):
                keep_queries(i, 4 * i, 4)
            act.dma_start(bc[BC_G], ln2_g[0].partition_broadcast(P)).then_inc(ln2_landed, 16)
            act.dma_start(bc[BC_B], ln2_b[0].partition_broadcast(P)).then_inc(ln2_landed, 16)
            await_taken(act, ("sc", 3))
            act.wait_ge(peer_zeros, 1)
            s.copy(vsum[0].rearrange("p (a n) -> p a n", a=4), zeros.unsqueeze(1).to_broadcast([P, 4, 512])).then_inc(
                vsum_zeroed, 1)
            for b in range(TB):
                with act.Fori(0, PH // 2) as r:
                    for par in range(2):
                        it = r * 2 + (PH * b + par)
                        act.wait_ge(top_ready, it + 1)
                        s.activation(gexp[:, par, :], tops[:, par, :], ACT.Exp, bias=ntop[:, par:par + 1],
                                     accum_out=gsum[:, par:par + 1]).then_inc(gexp_ready, 1)
                        s.copy(flat, tokbuf[:, bass.ds(it * 256 + 256, 256)]).then_inc(stage_ready, 1)
                        act.wait_ge(dots_done, it + 1)
                        s.activation(gel[:, par, :], dots[:, par, :], ACT.Gelu_apprx_tanh).then_inc(gel_ready, 1)
                        act.wait_ge(hk_ready, it + 1)
                        for j, k in enumerate(PE_ROWS):
                            act.wait_ge(v_started, it * NPE + (j + 2))
                            n = (par * NPE + j) % NDIAG
                            s.mul(diag[:, n // 4, n % 4, :], ident[:, :], hk[:, par, k:k + 1]).then_inc(diag_ready, 1)
                act.wait_ge(var_ready, 4 * TB + b + 1)
                s.activation(rstd[:, b:b + 1], rstd[:, b:b + 1], ACT.Sqrt).then_inc(std_ready, 1)

        @block.vector
        def _(dve):
            v = nc.vector
            steps = Steps(dve, dve_step)
            norms = [0]

            def free(ins):
                ins.then_inc(psum_freed["dve"], 1)

            def normalise(b, dst, src, stats=None, gain=None, offset=None):
                w = src.shape[-1]
                parts = max(1, w // 512)
                if stats is None:
                    stats = st
                    for i in range(parts):
                        steps.mark(v.bn_stats(st[:, i, :], src[:, i * (w // parts):(i + 1) * (w // parts)]))
                    steps.settle()
                steps.seq(v.bn_aggr(mv[:, b, :], stats[:, 0:parts, :]))
                v.tensor_scalar(rstd[:, b:b + 1], mv[:, b, 1:2], EPS, None, ALU.add).then_inc(var_ready, 1)
                norms[0] += 1
                dve.wait_ge(std_ready, norms[0])
                steps.seq(v.reciprocal(rstd[:, b:b + 1], rstd[:, b:b + 1]))
                if gain is not None:
                    steps.seq(v.scalar_tensor_tensor(out=dst, in0=src, scalar=mv[:, b, 0:1], in1=gain,
                                                     op0=ALU.subtract, op1=ALU.mult))
                    return v.scalar_tensor_tensor(out=dst, in0=dst, scalar=rstd[:, b:b + 1], in1=offset,
                                                  op0=ALU.mult, op1=ALU.add)
                return v.tensor_scalar(dst, src, mv[:, b, 0:1], rstd[:, b:b + 1], ALU.subtract, ALU.mult)

            def channel_params(i, c0, n):
                await_job(dve, ("par", i))
                free(v.tensor_copy(parT[:, c0:c0 + n], bank(("par", i))[:, 0:n]))

            def ada_sums(i, chunks=(0, 1)):
                dve.wait_ge(sT_ready, 1)
                if i in ADA_BEFORE and 0 in chunks:
                    await_job(dve, ("ada", ADA_BEFORE[i]))
                for cc in chunks:
                    acc = partial[:, ADA_SLOT[i], cc, :]
                    for k in range(KT):
                        n = ADA_POS[i, cc * NPIECE + k // PIECE_K]
                        w = aring[:, n % ARING, k % PIECE_K, :]
                        if k % PIECE_K == 0:
                            dve.wait_ge(ada_landed[n % ARING], 16 * (n // ARING + 1))
                        if k == 0:
                            ins = v.tensor_scalar(acc, w, sT[:, k:k + 1], None, ALU.mult)
                        else:
                            ins = v.scalar_tensor_tensor(out=acc, in0=w, scalar=sT[:, k:k + 1], in1=acc,
                                                         op0=ALU.mult, op1=ALU.add)
                        if k % PIECE_K == PIECE_K - 1:
                            ins.then_inc(ada_summed, 1)
                            await_ada_used(dve, n)
                        else:
                            steps.seq(ins)

            def ada_out(i):
                group, half = ADA[i]
                j = group * KT + 8 * half
                await_job(dve, ("ada", i))
                free(v.scalar_tensor_tensor(out=mod[:, j:j + 8], in0=bank(("ada", i))[:, 0:8],
                                            scalar=0.0 if group in (SH1, SH2) else 1.0,
                                            in1=parT[:, PAR_BADA + j:PAR_BADA + j + 8], op0=ALU.add, op1=ALU.add))
                await_taken(dve, ("ada", i))

            channel_params(0, 0, 112)
            for b in range(TB):
                ada_sums(0, (b,))
                dve.wait_ge(x_landed[b], 16)
                normalise(b, z[:, b, :], xres[:, b, :]).then_inc(z_ready, 1)
            ada_sums(2)
            await_taken(dve, ("par", 0))
            ada_out(0)
            ada_out(1)
            channel_params(1, 112, 64)
            ada_out(2)
            ada_out(3)
            await_taken(dve, ("zt", 3))
            for k in range(KT):
                v.tensor_scalar(uT[:, k, :], uT[:, k, :], mod[:, SC1 * KT + k:SC1 * KT + k + 1],
                                mod[:, SH1 * KT + k:SH1 * KT + k + 1], ALU.mult, ALU.add).then_inc(zt_scaled, 1)

            await_taken(dve, ("par", 1))
            TWO_PI = 2.0 * np.pi
            C1 = 6.28125
            C2 = 0.00193500518798828125
            C3 = float(TWO_PI - C1 - C2)
            ROUND = 1.5 * 2.0 ** 23
            dve.wait_ge(small_landed, 48)
            dve.wait_ge(consts_ready, 1 + NF + 2)
            steps.seq(v.tensor_copy(posf[:, :], pos_i[:, :]))
            for b in range(TB):
                steps.mark(v.tensor_scalar(ang[:, b, :], freq[:, :], posf[:, b:b + 1], None, ALU.mult))
            steps.settle()
            steps.seq(v.tensor_scalar(ang2[:, :, :], ang[:, :, :], 1.0 / TWO_PI, ROUND, ALU.mult, ALU.add))
            steps.seq(v.tensor_scalar(ang2[:, :, :], ang2[:, :, :], -ROUND, None, ALU.add))
            for part in (C1, C2, C3):
                steps.seq(v.scalar_tensor_tensor(out=ang[:, :, :], in0=ang2[:, :, :], scalar=-part, in1=ang[:, :, :],
                                                 op0=ALU.mult, op1=ALU.add))
            PI32 = float(np.nextafter(np.float32(np.pi), np.float32(0)))
            steps.seq(v.tensor_scalar(ang[:, :, :], ang[:, :, :], PI32, -PI32, ALU.min, ALU.max))
            steps.seq(v.tensor_scalar(ang2[:, :, :], ang[:, :, :], -1.0, None, ALU.mult))
            steps.seq(v.tensor_tensor(ang2[:, :, :], ang[:, :, :], ang2[:, :, :], ALU.max))
            v.tensor_scalar(ang2[:, :, :], ang2[:, :, :], -1.0, float(np.pi / 2), ALU.mult, ALU.add).then_inc(ang_ready, 1)

            steps.mark(v.tensor_copy(iota[:, :], iota_i[:, :]))
            lam = parT[:, PAR_LAM:PAR_LAM + NLT]
            steps.seq(v.tensor_scalar(sp[:, 2, :], lam, -1.0, None, ALU.mult))
            steps.seq(v.tensor_tensor(sp[:, 0, :], lam, sp[:, 2, :], ALU.min))
            v.tensor_scalar(sp[:, 2, :], sp[:, 2, :], 0.0, None, ALU.max).then_inc(lam_exp, 1)
            dve.wait_ge(lam_exp, 2)
            steps.seq(v.tensor_scalar(sp[:, 3, :], sp[:, 1, :], 2.0, None, ALU.add))
            steps.seq(v.reciprocal(sp[:, 3, :], sp[:, 3, :]))
            steps.seq(v.tensor_tensor(sp[:, 3, :], sp[:, 3, :], sp[:, 1, :], ALU.mult))
            steps.seq(v.tensor_tensor(sp[:, 4, :], sp[:, 3, :], sp[:, 3, :], ALU.mult))
            NTERM = 9
            steps.seq(v.tensor_scalar(sp[:, 5, :], sp[:, 4, :], 1.0 / (2 * NTERM + 1), 1.0 / (2 * NTERM - 1), ALU.mult, ALU.add))
            for j in range(NTERM - 1, 0, -1):
                steps.seq(v.tensor_tensor(sp[:, 5, :], sp[:, 5, :], sp[:, 4, :], ALU.mult))
                steps.seq(v.tensor_scalar(sp[:, 5, :], sp[:, 5, :], 1.0 / (2 * j - 1), None, ALU.add))
            steps.seq(v.tensor_tensor(sp[:, 5, :], sp[:, 5, :], sp[:, 3, :], ALU.mult))
            steps.seq(v.scalar_tensor_tensor(out=sp[:, 5, :], in0=sp[:, 5, :], scalar=2.0, in1=sp[:, 2, :],
                                             op0=ALU.mult, op1=ALU.add))
            steps.mark(v.tensor_scalar(nsp8[:, :], sp[:, 5, :], -8.0, None, ALU.mult))
            steps.mark(v.tensor_scalar(psp8[:, :], sp[:, 5, :], 8.0, None, ALU.mult))
            steps.mark(v.memset(xlp[:, :, 0:3], 0.0))
            steps.settle()

            def rope(col, heads, width, half, f0):
                xs = tok[:, :, col:col + heads * width].rearrange("p b (h w) -> p b h w", h=heads)
                x1, x2 = xs[:, :, :, 0:half], xs[:, :, :, half:2 * half]
                cs = cos[:, :, f0:f0 + half].unsqueeze(2).to_broadcast([P, TB, heads, half])
                sn = sin[:, :, f0:f0 + half].unsqueeze(2).to_broadcast([P, TB, heads, half])
                n = TB * heads * half
                t = [ropet[:, i * 512:i * 512 + n].rearrange("p (b h f) -> p b h f", b=TB, h=heads) for i in range(4)]
                steps.mark(v.tensor_tensor(t[0], x1, cs, ALU.mult))
                steps.mark(v.tensor_tensor(t[1], x2, sn, ALU.mult))
                steps.mark(v.tensor_tensor(t[2], x2, cs, ALU.mult))
                steps.mark(v.tensor_tensor(t[3], x1, sn, ALU.mult))
                steps.settle()
                steps.mark(v.tensor_tensor(x1, t[0], t[1], ALU.subtract))
                return v.tensor_tensor(x2, t[2], t[3], ALU.add)

            dve.wait_ge(sincos_ready, 2)
            await_taken(dve, ("kiwi", 0))
            for b in range(TB):
                ki = tok[:, b, T_KI:T_KI + ID]
                steps.seq(normalise(b, ki, ki))
                steps.seq(v.tensor_tensor(ki, ki, kig[:, :], ALU.mult))
            steps.seq(rope(T_KI, 1, ID, RI, RA))
            for i in range(2):
                v.tensor_copy(kd[:, :, ID * i:ID * (i + 1)], tok[:, :, T_KI:T_KI + ID]).then_inc(kd_ready, 1)
            steps.seq(v.tensor_scalar(tok[:, :, T_WI:T_WI + NI], tok[:, :, T_WI:T_WI + NI], NI ** -0.5, None, ALU.mult))
            ada_sums(4)
            ada_sums(5)
            await_taken(dve, ("qi", 1))
            rope(T_QI, NI, ID, RI, RA).then_inc(qi_roped, 1)
            ada_out(4)
            ada_sums(6)

            def conv(i):
                await_taken(dve, ("xl", i))
                for j in range(CONV_W):
                    for n in range(4 * i, 4 * i + 4):
                        wj = parT[:, PAR_CW + j * NLT + n:PAR_CW + j * NLT + n + 1]
                        if j == 0:
                            ins = v.tensor_scalar(xc[:, n], xlp[:, n, 0:SEQ], wj, parT[:, PAR_CB + n:PAR_CB + n + 1],
                                                  ALU.mult, ALU.add)
                        else:
                            ins = v.scalar_tensor_tensor(out=xc[:, n], in0=xlp[:, n, j:j + SEQ], scalar=wj,
                                                         in1=xc[:, n], op0=ALU.mult, op1=ALU.add)
                        if j < CONV_W - 1:
                            steps.mark(ins)
                        else:
                            ins.then_inc(xc_ready, 1)
                    if j < CONV_W - 1:
                        steps.settle()

            conv(0)
            ada_out(5)
            ada_out(6)
            conv(1)

            seen = 0
            for i, (b, h0, n, keys) in enumerate(LG_UNITS):
                await_taken(dve, ("lg", i))
                for j in range(n):
                    h = h0 + j
                    wcol = tok[:, b, T_WI + h:T_WI + h + 1]
                    o = lg_col(j, n, keys)
                    rl = sm[:, i % 2, o:o + keys]
                    if h == 0:
                        ins = v.tensor_scalar(score[:, b, 0:keys], rl, wcol, None, ALU.mult)
                    else:
                        ins = v.scalar_tensor_tensor(out=score[:, b, 0:keys], in0=rl, scalar=wcol,
                                                     in1=score[:, b, 0:keys], op0=ALU.mult, op1=ALU.add)
                    if j == n - 1:
                        ins.then_inc(relu_used, 1)
                        dve.wait_ge(relu_used, i + 1)
                    else:
                        steps.seq(ins)
            for b in range(TB):
                steps.mark(v.memset(score[0:CHUNK, b, (2 * b + 1) * CHUNK:(2 * b + 2) * CHUNK], NEG))
            steps.settle()
            for rnd in range(TOPK // 8):
                for b in range(TB):
                    keys = (b + 1) * P
                    steps.seq(v.max(m8[:, :], score[:, b, 0:keys]))
                    steps.seq(v.match_replace(score[:, b, 0:keys], m8[:, :], score[:, b, 0:keys], TAKEN))
            for b in range(TB):
                keys = (b + 1) * P
                steps.seq(v.tensor_scalar(score[:, b, 0:keys], score[:, b, 0:keys], TAKEN / 2, NEG, ALU.is_gt, ALU.mult))
            ada_sums(7)
            ada_sums(8)

            dve.wait_ge(xc_ready, NLT)
            await_taken(dve, ("gate", 3))
            steps.seq(v.tensor_tensor(xc[:, :, :], xc[:, :, :], ig[:, :, :], ALU.mult))
            dve.wait_ge(decay_ready, NLT)
            steps.seq(v.tensor_tensor(ig[:, :, :], rg[:, :, :], rg[:, :, :], ALU.mult))
            v.scalar_tensor_tensor(out=th[:, :, :], in0=ig[:, :, :], scalar=1.0, in1=th[:, :, :], op0=ALU.add,
                                   op1=ALU.mult).then_inc(pow_ready, 1)
            dve.wait_ge(sqrt_ready, 1)
            steps.seq(v.tensor_tensor(xc[:, :, :], xc[:, :, :], th[:, :, :], ALU.mult))
            for n in range(NLT):
                steps.mark(v.tensor_tensor_scan(ig[:, n], rg[:, n], xc[:, n], 0.0, ALU.mult, ALU.add))
            steps.settle()
            v.tensor_tensor(concatT[:, 0:NLT, :], ig[:, :, :], concatT[:, 0:NLT, :], ALU.mult).then_inc(lru_done, 1)
            ada_out(7)
            ada_out(8)
            ada_sums(9)
            ada_sums(10)
            ada_out(9)
            ada_sums(11)
            ada_out(10)
            await_taken(dve, ("k", 1))
            rope(T_Q, 2 * NH, HD, RA, 0).then_inc(qk_roped, 1)
            ada_out(11)

            def attention_scores(u):
                b, h0, n, keys = UNITS[u]
                await_job(dve, ("at", u))
                sc = scores_of(u).rearrange("p (h k) -> p h k", h=n)
                mx = amax[:, 8 * u:8 * u + n]
                free(v.scalar_tensor_tensor(out=sc, in0=bank(("at", u)).rearrange("p (h k) -> p h k", h=n),
                                            scalar=HD ** -0.5,
                                            in1=score[:, b, 0:keys].unsqueeze(1).to_broadcast([P, n, keys]),
                                            op0=ALU.mult, op1=ALU.add))
                await_taken(dve, ("at", u))
                steps.seq(v.tensor_reduce(mx, sc, AX.X, ALU.max))
                v.tensor_scalar(mx, mx, -1.0, None, ALU.mult).then_inc(scored_ready, 1)

            def probabilities(u):
                b, h0, n, keys = UNITS[u]
                dve.wait_ge(exp_ready, sum(w[2] for w in UNITS[0:u + 1]))
                tot = asum[:, 8 * u:8 * u + n]
                steps.seq(v.reciprocal(tot, tot))
                sc = scores_of(u).rearrange("p (h k) -> p h k", h=n)
                v.tensor_tensor(sc, sc, tot.unsqueeze(2).to_broadcast([P, n, keys]), ALU.mult).then_inc(prob_ready, 1)

            for u in range(len(UNITS)):
                attention_scores(u)
            for u in range(len(UNITS)):
                probabilities(u)

            def residual(cc):
                await_job(dve, ("wo", cc))
                sl = slice(cc * CW, (cc + 1) * CW)
                pb = bank(("wo", cc)).rearrange("p (b n) -> p b n", b=TB)
                tmp = sm[:, :, 0:CW]
                free(v.tensor_tensor(tmp, pb, bc[BC_GT1][:, sl].unsqueeze(1).to_broadcast([P, TB, CW]), ALU.mult))
                await_taken(dve, ("wo", cc))
                steps.seq(v.scalar_tensor_tensor(out=xres[:, :, sl], in0=xres[:, :, sl], scalar=ALPHA, in1=tmp,
                                                 op0=ALU.mult, op1=ALU.add))
                for b in range(TB):
                    steps.mark(v.bn_stats(st2[:, b, cc, :], xres[:, b, sl]))

            await_taken(dve, ("bc", (GT1, 1)))
            residual(0)
            residual(1)
            residual(2)
            residual(3)
            steps.settle()
            dve.wait_ge(ln1_landed, 32)
            for b in range(TB):
                steps.seq(normalise(b, xres[:, b, :], xres[:, b, :], st2[:, b], bc[BC_G], bc[BC_B]))
                normalise(b, u2[:, b, :], xres[:, b, :]).then_inc(z2_ready, 1)
            v.memset(zeros, 0.0).then_inc(peer_zeros, 1)
            await_taken(dve, ("bc", (SH2, 1)))
            for b in range(TB):
                await_job(dve, ("ut", 2 * b + 1))
                dve.wait_ge(z2_ready, b + 1)
                steps.seq(v.tensor_tensor(u2[:, b, :], u2[:, b, :], bc[BC_SC2], ALU.mult))
                v.tensor_tensor(u2[:, b, :], u2[:, b, :], bc[BC_SH2], ALU.add).then_inc(u2_ready, 1)
            dve.wait_ge(u2_ready, TB)

            def route(it, par):
                take(dve, stage_ready)
                for i in range(2):
                    steps.mark(v.max(topv[:, i, 0:8], stage[:, i, :]))
                steps.settle()
                for i in range(2):
                    steps.mark(v.max_index(topi[:, i, 0:8], topv[:, i, 0:8], stage[:, i, :]))
                    steps.mark(v.match_replace(stage[:, i, :], topv[:, i, 0:8], stage[:, i, :], TAKEN))
                steps.settle()
                for i in range(2):
                    steps.mark(v.max(topv[:, i, 8:16], stage[:, i, :]))
                steps.settle()
                for i in range(2):
                    steps.mark(v.max_index(topi[:, i, 8:16], topv[:, i, 8:16], stage[:, i, :]))
                steps.mark(v.tensor_tensor(cand[:, :, :], topv[:, 0, :].unsqueeze(2).to_broadcast([P, PK, PK]),
                                           topv[:, 1, :].unsqueeze(1).to_broadcast([P, PK, PK]), ALU.add))
                steps.settle()
                cf = cand[:, :, :].rearrange("p a c -> p (a c)")
                steps.mark(v.tensor_copy(topf[:, :, :], topi[:, :, :]))
                steps.seq(v.max(tops[:, par, 0:8], cf))
                steps.mark(v.max_index(pick[:, 0:8], tops[:, par, 0:8], cf))
                steps.seq(v.match_replace(cf, tops[:, par, 0:8], cf, TAKEN))
                steps.seq(v.max(tops[:, par, 8:16], cf))
                steps.mark(v.tensor_scalar(ntop[:, par:par + 1], tops[:, par, 0:1], -1.0, None, ALU.mult))
                v.max_index(pick[:, 8:16], tops[:, par, 8:16], cf).then_inc(top_ready, 1)
                steps.settle()
                dve.wait_ge(top_ready, it + 1)
                steps.mark(v.tensor_scalar(pick2[:, 0, :], pick[:, :], 4, None, ALU.logical_shift_right))
                steps.mark(v.tensor_scalar(pick2[:, 1, :], pick[:, :], PK - 1, None, ALU.bitwise_and))
                steps.settle()
                steps.seq(v.tensor_copy(pickf[:, :, :], pick2[:, :, :]))
                for i in range(2):
                    steps.seq(v.tensor_tensor(onehot[:, :, :], pickf[:, i, :].unsqueeze(2).to_broadcast([P, PK, PK]),
                                              iota[:, :].unsqueeze(1).to_broadcast([P, PK, PK]), ALU.is_equal))
                    steps.seq(v.tensor_tensor(onehot[:, :, :], onehot[:, :, :],
                                              topf[:, i, :].unsqueeze(1).to_broadcast([P, PK, PK]), ALU.mult))
                    steps.seq(v.tensor_reduce(esel[:, i, :], onehot[:, :, :], AX.X, ALU.add))
                v.scalar_tensor_tensor(out=eidx[:, par, :], in0=esel[:, 0, :], scalar=float(NK), in1=esel[:, 1, :],
                                       op0=ALU.mult, op1=ALU.add).then_inc(idx_ready, 1)

            def finish(b):
                if b == 0:
                    await_taken(dve, ("bc", (GT2, 1)))
                    dve.wait_ge(ln2_landed, 32)
                steps.seq(v.tensor_tensor(vsum[b], vsum[b], bc[BC_GT2], ALU.mult))
                steps.seq(v.scalar_tensor_tensor(out=xres[:, b, :], in0=xres[:, b, :], scalar=ALPHA, in1=vsum[b],
                                                 op0=ALU.mult, op1=ALU.add))
                dve.wait_ge(y_ready, b + 1)
                y = ps[:, 2 * b:2 * b + 2, :].rearrange("p a n -> p (a n)")
                steps.seq(v.tensor_tensor(u2[:, b, :], y, bc[BC_GT2], ALU.mult))
                steps.seq(v.tensor_tensor(xres[:, b, :], xres[:, b, :], u2[:, b, :], ALU.add))
                normalise(b, xres[:, b, :], xres[:, b, :], gain=bc[BC_G], offset=bc[BC_B]).then_inc(out_ready, 1)

            route(0, 0)
            for b in range(TB):
                if b > 0:
                    steps.mark(v.memset(vsum[b], 0.0))
                steps.restart()
                with dve.Fori(0, PH // 2) as r:
                    for par in range(2):
                        it = r * 2 + (PH * b + par)
                        for k in range(PK):
                            slot = slot_of(k)
                            dve.wait_ge(row_landed[slot], it * 64 + 16 * (k // NGR + 1))
                            v.scalar_tensor_tensor(out=gathered[:, slot, :], in0=gathered[:, slot, :], scalar=1.0,
                                                   in1=u2[:, b, :], op0=ALU.mult, op1=ALU.mult,
                                                   accum_out=dots[:, par, k:k + 1]).then_inc(slot_free[slot], 1)
                        dve.wait_ge(gexp_ready, it + 1)
                        v.reciprocal(gsum[:, par:par + 1], gsum[:, par:par + 1]).then_inc(dots_done, 1)
                        dve.wait_ge(dots_done, it + 1)
                        dve.wait_ge(gel_ready, it + 1)
                        v.scalar_tensor_tensor(out=hk[:, par, :], in0=gexp[:, par, :], scalar=gsum[:, par:par + 1],
                                               in1=gel[:, par, :], op0=ALU.mult, op1=ALU.mult).then_inc(hk_ready, 1)
                        route(it + 1, 1 - par)
                        dve.wait_ge(hk_ready, it + 1)
                        if b == 0:
                            dve.wait_ge(vsum_zeroed, 1)
                        for n, k in enumerate(DVE_ROWS):
                            slot = slot_of(k)
                            dve.wait_ge(row_landed[slot], it * 64 + (32 + 16 * (k // NGR + 1)))
                            v.scalar_tensor_tensor(out=vsum[b], in0=gathered[:, slot, :], scalar=hk[:, par, k:k + 1],
                                                   in1=vsum[b], op0=ALU.mult, op1=ALU.add).then_inc(vsum_added, 1)
                            dve.wait_ge(vsum_added, it * len(DVE_ROWS) + (n + 1))
                            dve.sem_inc(slot_free[slot], 1)
                    steps.restart()
                finish(b)

        @block.tensor
        def _(pe):
            t = nc.tensor
            piece = [0]

            def ada_total(i):
                out_ = start_job(("ada", i))
                await_ada_used(pe, ADA_POS[i, PAIR_PIECES - 1])
                for j in range(8):
                    last = t.matmul(out_[:, j:j + 1], partial[:, ADA_SLOT[i], j // 4, j % 4 * P:(j % 4 + 1) * P],
                                    ones[:, 0:1], start=True, stop=True)
                last.then_inc(psum_full, 1)

            def start_job(name):
                n = JOB_AT[name]
                if n >= NPAIR:
                    await_taken(pe, (JOBS[n - NPAIR][0], JOBS[n - NPAIR][1]))
                return bank(name)

            def stream(name, step):
                out_ = start_job(name)
                for q in range(NPIECE):
                    n = piece[0]
                    place, landed, count = piece_place(n)
                    pe.wait_ge(landed, 16 * count)
                    for kk in range(PIECE_K):
                        last = step(out_, q * PIECE_K + kk, place[:, kk, :])
                    last.then_inc(psum_full if q == NPIECE - 1 else pieces_used, 1)
                    piece[0] += 1

            def token_step(act_T):
                def step(out_, k, w):
                    for b in range(TB):
                        last = t.matmul(out_[:, b * CW:(b + 1) * CW], act_T[:, k, b * P:(b + 1) * P], w,
                                        start=(k == 0), stop=(k == KT - 1))
                    return last
                return step

            def channel_step(out_, k, w):
                for j in range(4):
                    last = t.matmul(out_[:, j * SEQ:(j + 1) * SEQ], w[:, j * P:(j + 1) * P], uT[:, k, :],
                                    start=(k == 0 and j % 2 == 0), stop=(k == KT - 1), skip_group_check=True)
                return last

            def transposes(name, tiles, rows=P):
                out_ = start_job(name)
                for j, tile_ in enumerate(tiles):
                    n = tile_.shape[0]
                    last = t.transpose(out_[:, j * P:j * P + n], tile_, ident[0:n, 0:n])
                last.then_inc(psum_full, 1)

            def token_transposes(name, col, i):
                transposes(name, [tok[:, b, col + (4 * i + j) * P:col + (4 * i + j + 1) * P]
                                  for j in range(4) for b in range(TB)])

            pe.wait_ge(consts_ready, 1 + NF + 1)
            pe.wait_ge(c_landed, 32)
            transposes(("par", 0), [paramA[0:112, :]])
            def ada_row_of(i):
                out_ = start_job(("row", i))
                for q in range(NPIECE):
                    n = ADA_POS[ADA_PE[i // 2], i % 2 * NPIECE + q]
                    pe.wait_ge(ada_landed[n % ARING], 16 * (n // ARING + 1))
                    for kk in range(PIECE_K):
                        k = q * PIECE_K + kk
                        last = t.matmul(out_[0:1, 0:CW], sT[:, k:k + 1], aring[:, n % ARING, kk, :],
                                        start=(k == 0), stop=(k == KT - 1))
                    last.then_inc(ada_multiplied if q < NPIECE - 1 else psum_full, 1)

            def turn_rows(u):
                out_ = start_job(("ada", ADA_PE[u]))
                await_taken(pe, ("row", 2 * u + 1))
                for j in range(8):
                    last = t.matmul(out_[:, j:j + 1], ada_row[u][:, j // 4, j % 4 * P:(j % 4 + 1) * P],
                                    ones[0:1, 0:1], start=True, stop=True)
                last.then_inc(psum_full, 1)

            pe.wait_ge(sT_ready, 1)
            ada_row_of(0)
            ada_row_of(1)
            for i in range(4):
                b, half = i // 2, i % 2
                pe.wait_ge(z_ready, b + 1)
                transposes(("zt", i), [z[:, b, (8 * half + k) * P:(8 * half + k + 1) * P] for k in range(8)])
            ada_total(0)
            turn_rows(0)
            ada_row_of(2)
            ada_row_of(3)
            pe.wait_ge(params_landed, 16 * 5)
            transposes(("par", 1), [paramB[0:64, :]])
            ada_total(2)
            turn_rows(1)

            pe.wait_ge(tail_landed, 16)
            out_ = start_job(("kiwi", 0))
            for k in range(KT):
                pe.wait_ge(zt_scaled, k + 1)
                for b in range(TB):
                    last = t.matmul(out_[:, b * CW:b * CW + 80], uT[:, k, b * P:(b + 1) * P], w_tail[:, k, :],
                                    start=(k == 0), stop=(k == KT - 1))
            last.then_inc(psum_full, 1)
            stream(("qi", 0), token_step(uT))
            stream(("qi", 1), token_step(uT))
            ada_total(4)
            stream(("xl", 0), channel_step)
            pe.wait_ge(kd_ready, 2)
            transposes(("kit", 0), [kd[:, b, :] for b in range(TB)])
            pe.wait_ge(qi_roped, 1)
            token_transposes(("qit", 0), T_QI, 0)
            token_transposes(("qit", 1), T_QI, 1)
            ada_total(5)
            stream(("xl", 1), channel_step)
            ada_total(6)
            await_taken(pe, ("kit", 0))
            await_taken(pe, ("qit", 1))
            for i, (b, h0, n, keys) in enumerate(LG_UNITS):
                out_ = start_job(("lg", i))
                for j in range(n):
                    h = h0 + j
                    p0 = ID * (h % 2)
                    o = lg_col(j, n, keys)
                    last = t.matmul(out_[:, o:o + keys], qiT[p0:p0 + ID, h // 2, b * P:(b + 1) * P],
                                    kdT[p0:p0 + ID, 0:keys], start=True, stop=True)
                last.then_inc(psum_full, 1)
            stream(("gl", 0), channel_step)
            stream(("gl", 1), channel_step)
            pe.wait_ge(gates_landed, 32)
            for i in range(4):
                out_ = start_job(("gate", i))
                pe.wait_ge(xc_ready, 2 * i + 2)
                for j in range(2):
                    for w in range(2):
                        o = (2 * j + w) * SEQ
                        last = t.matmul(out_[:, o:o + SEQ], gate_w[:, w, 2 * i + j, :], xc[:, 2 * i + j, :],
                                        start=True, stop=True)
                last.then_inc(psum_full, 1)
            ada_total(7)
            stream(("q", 0), token_step(uT))
            ada_total(8)
            stream(("q", 1), token_step(uT))
            ada_total(9)
            stream(("k", 0), token_step(uT))
            ada_total(10)
            stream(("k", 1), token_step(uT))
            stream(("v", 0), token_step(uT))
            ada_total(11)
            pe.wait_ge(qk_roped, 1)
            for kind, col in (("qt", T_Q), ("kt", T_K)):
                for i in range(2):
                    token_transposes((kind, i), col, i)
            for u, (b, h0, n, keys) in enumerate(UNITS):
                out_ = start_job(("at", u))
                await_taken(pe, ("kt", 1))
                for j in range(n):
                    last = t.matmul(out_[:, j * keys:(j + 1) * keys], qT[:, h0 + j, b * P:(b + 1) * P],
                                    kT[:, h0 + j, 0:keys], start=True, stop=True)
                last.then_inc(psum_full, 1)
            stream(("v", 1), token_step(uT))

            def turn(u):
                if u == 2:
                    await_job(pe, ("pv", 0))
                pe.wait_ge(prob_ready, u + 1)
                transposes(("pt", u), [scores_of(u)[:, j * P:(j + 1) * P] for j in range(8)])

            def attend(u):
                b, h0, n, keys = UNITS[u]
                out_ = start_job(("pv", u))
                await_taken(pe, ("pt", u))
                await_taken(pe, ("v", 1))
                for j in range(n):
                    for i in range(keys // P):
                        last = t.matmul(out_[:, j * P:(j + 1) * P],
                                        tok[:, i, T_V + (h0 + j) * HD:T_V + (h0 + j + 1) * HD],
                                        PT[:, u % 2, j * keys + i * P:j * keys + (i + 1) * P],
                                        start=(i == 0), stop=(i == keys // P - 1))
                last.then_inc(psum_full, 1)

            turn(0)
            turn(1)
            attend(0)
            turn(2)
            attend(1)
            attend(2)

            def broadcast(vec):
                for i in range(2):
                    out_ = start_job(("bc", (vec, i)))
                    pe.wait_ge(diag_built, BC_SEEN.index((vec, i)) + 1)
                    for u in range(2):
                        last = t.matmul(out_[:, u * 512:(u + 1) * 512], ones[:, :],
                                        diag[:, u].rearrange("p k n -> p (k n)"), start=True, stop=True)
                    last.then_inc(psum_full, 1)

            broadcast(GT1)
            pe.wait_ge(lru_done, 1)
            await_taken(pe, ("pv", 2))
            stream(("wo", 0), token_step(concatT))
            broadcast(SC2)
            stream(("wo", 1), token_step(concatT))
            broadcast(SH2)
            stream(("wo", 2), token_step(concatT))
            stream(("wo", 3), token_step(concatT))
            def turn_z2(b):
                pe.wait_ge(z2_ready, b + 1)
                for half in range(2):
                    transposes(("ut", 2 * b + half),
                               [u2[:, b, (8 * half + k) * P:(8 * half + k + 1) * P] for k in range(8)])

            turn_z2(0)
            pe.wait_ge(subkeys_landed, 16)
            for i in range(2):
                transposes(("skt", i), [keyscore[:, (8 * i + j) * P:(8 * i + j + 1) * P] for j in range(8)])
            broadcast(GT2)
            turn_z2(1)
            await_taken(pe, ("ut", 3))

            def half_chunk(name, tiles, last_use):
                out_ = start_job(name)
                n0 = CHUNKS.index(("pq", 0)) * NPIECE
                for q in range(NPIECE):
                    place, landed, count = piece_place(n0 + q)
                    pe.wait_ge(landed, 16 * count)
                    for kk in range(PIECE_K):
                        k = q * PIECE_K + kk
                        for m, j in enumerate(tiles):
                            last = t.matmul(out_[:, m * SEQ:(m + 1) * SEQ], place[:, kk, j * P:(j + 1) * P], uT[:, k, :],
                                            start=(k == 0 and m == 0), stop=(k == KT - 1), skip_group_check=True)
                    if q == NPIECE - 1:
                        last.then_inc(psum_full, 1)
                    elif last_use:
                        last.then_inc(pieces_used, 1)
                    if last_use:
                        piece[0] += 1

            def sub_key_scores(name, first, n):
                out_ = start_job(("sc", name))
                await_taken(pe, ("pq", name))
                for b in range(TB):
                    for j in range(n):
                        hp = first + j
                        last = t.matmul(out_[:, (4 * b + j) * P:(4 * b + j + 1) * P], qpT[:, hp, b * P:(b + 1) * P],
                                        subkT[:, hp, :], start=True, stop=True)
                last.then_inc(psum_full, 1)

            half_chunk(("pq", "first"), (0, 1), False)
            sub_key_scores("first", 0, 2)
            half_chunk(("pq", 0), (2, 3), True)
            sub_key_scores(0, 2, 2)
            for i in range(1, 4):
                stream(("pq", i), channel_step)
                sub_key_scores(i, 4 * i, 4)

            await_taken(pe, ("sc", 3))
            pe.wait_ge(peer_zeros, 1)
            for b in range(TB):
                y = ps[:, 2 * b:2 * b + 2, :].rearrange("p a n -> p (a n)")
                for j in range(4):
                    last = t.matmul(y[:, j * 512:(j + 1) * 512], ones[:, :], zeros, start=True, stop=False,
                                    skip_group_check=True)
                if b == 0:
                    last.then_inc(v_started, NDIAG)
                with pe.Fori(0, PH // 2) as r:
                    for par in range(2):
                        it = r * 2 + (PH * b + par)
                        for m, k in enumerate(PE_ROWS):
                            n = (par * NPE + m) % NDIAG
                            pe.wait_ge(diag_ready, it * NPE + (m + 1))
                            slot = slot_of(k)
                            pe.wait_ge(row_landed[slot], it * 64 + (32 + 16 * (k // NGR + 1)))
                            for j in range(4):
                                last = t.matmul(y[:, j * 512:(j + 1) * 512], diag[:, n // 4, n % 4, :],
                                                gathered[:, slot, j * 512:(j + 1) * 512], start=False,
                                                stop=False, skip_group_check=True)
                                if j == 0:
                                    last.then_inc(v_started, 1)
                            last.then_inc(slot_free[slot], 1)
                t.matmul(y[:, 0:512], ones[:, :], zeros, start=False, stop=True,
                         skip_group_check=True).then_inc(y_ready, 1)


_INS = ["x", "c", "positions", "w_ada", "b_ada", "w_in", "conv_w", "conv_b", "w_rg_a", "b_rg_a", "w_rg_x", "b_rg_x",
        "lru_lambda", "k_idx_g", "w_out", "ln1_g", "ln1_b", "w_pq", "peer_sub_keys", "peer_u", "peer_v", "ln2_g",
        "ln2_b"]


def kernel(**inputs):
    import concourse.bacc as _bacc
    from concourse.bass_utils import run_bass_kernel_spmd as _run

    nc = _bacc.Bacc("TRN2", target_bir_lowering=False, num_devices=1)
    arrays, args = {}, []
    for name in _INS:
        a = np.ascontiguousarray(inputs[name])
        arrays[f"in_{name}_dram"] = a
        args.append(nc.dram_tensor(f"in_{name}_dram", a.shape, mybir.dt.from_np(a.dtype), kind="ExternalInput").ap())
    args.append(nc.dram_tensor("out_dram", (1, SEQ, D), F32, kind="ExternalOutput").ap())
    build_layer(nc, *args)
    r = _run(nc, [arrays], core_ids=[0])
    return r.results[0]["out_dram"]
```
